# Optimizing a Trainium2 kernel written in Bass

```python
import jax, jax.numpy as jnp
from jax import lax
import numpy as np
import math

D_MODEL = 1024
BATCH = 1
SEQ = 256
DEPTH = 2

CHUNK = 64
MEM_LEN = 256
Q_BLOCK = 128
N_MIXERS = 2
DA_HEADS = 6
DA_HEAD_DIM = 64
DA_WIDTH = DA_HEADS * 2 * DA_HEAD_DIM
HG_HEADS = 6
HG_KEY_DIM = 128
HG_VAL_DIM = 128
HG_KEY_WIDTH = HG_HEADS * HG_KEY_DIM
HG_VAL_WIDTH = HG_HEADS * HG_VAL_DIM
MEM_HEADS = 4
MEM_HEAD_DIM = 64
MEM_WIDTH = MEM_HEADS * MEM_HEAD_DIM
MIX_WIDTH = DA_WIDTH + MEM_WIDTH
D_FF_DENSE = 2816
N_EXPERTS = 8
TOP_K = 2
D_FF_EXPERT = 3584
EPS = 1e-6
MASK_VALUE = -1e30
N_A = (DEPTH + 1) // 2
N_B = DEPTH // 2


F32 = jnp.float32

def rms_norm(x, g):
    xf = x.astype(F32)
    y = xf * lax.rsqrt(jnp.mean(xf * xf, axis=-1, keepdims=True) + EPS)
    return (y * g.astype(F32)).astype(x.dtype)

def alibi_slopes(n):
    return jnp.asarray(2.0 ** (-8.0 * np.arange(1, n + 1) / n), F32)

def memory_attention(q_mem, mem, mem_norm_g, w_mem_kv):
    B, S, _ = q_mem.shape
    kv = rms_norm(mem, mem_norm_g) @ w_mem_kv
    k, v = jnp.split(kv, 2, axis=-1)
    q = q_mem.reshape(B, S, MEM_HEADS, MEM_HEAD_DIM)
    k = k.reshape(B, -1, MEM_HEADS, MEM_HEAD_DIM)
    v = v.reshape(B, -1, MEM_HEADS, MEM_HEAD_DIM)
    s = jnp.einsum('bshd,bmhd->bhsm', q, k).astype(F32) * (MEM_HEAD_DIM ** -0.5)
    p = jax.nn.softmax(s, axis=-1).astype(v.dtype)
    o = jnp.einsum('bhsm,bmhd->bshd', p, v)
    return o.reshape(B, S, MEM_WIDTH)

def diff_attention(q, k, v, lam, lam_init, subln_g):
    B, S = q.shape[:2]
    nb = S // Q_BLOCK
    scale = DA_HEAD_DIM ** -0.5
    slopes = alibi_slopes(DA_HEADS)
    kpos = jnp.arange(S)
    kchunk = kpos // CHUNK
    qb = q.reshape(B, nb, Q_BLOCK, DA_HEADS, 2, DA_HEAD_DIM).transpose(1, 0, 2, 3, 4, 5)
    starts = jnp.arange(nb) * Q_BLOCK

    def block(args):
        q_blk, start = args
        qpos = start + jnp.arange(Q_BLOCK)
        dist = jnp.abs(qpos[:, None] - kpos[None, :]).astype(F32)
        allowed = kchunk[None, :] <= (qpos // CHUNK)[:, None]
        bias = jnp.where(allowed[None], -slopes[:, None, None] * dist[None], MASK_VALUE)
        s = jnp.einsum('bqhmd,bkhmd->bhmqk', q_blk, k).astype(F32) * scale + bias[None, :, None]
        p = jax.nn.softmax(s, axis=-1)
        a = (p[:, :, 0] - lam * p[:, :, 1]).astype(v.dtype)
        return jnp.einsum('bhqk,bkhe->bqhe', a, v)

    o = lax.map(block, (qb, starts))
    o = o.transpose(1, 0, 2, 3, 4).reshape(B, S, DA_HEADS, 2 * DA_HEAD_DIM)
    o = rms_norm(o, subln_g) * (1.0 - lam_init)
    return o.reshape(B, S, DA_WIDTH)

def diff_attention_mixer(h, mem, w_in, lq1, lk1, lq2, lk2, subln_g, mem_norm_g, w_mem_kv, w_out, lam_init):
    B, S, _ = h.shape
    proj = h @ w_in
    q, k, v, qm = jnp.split(proj, [DA_WIDTH, 2 * DA_WIDTH, 3 * DA_WIDTH], axis=-1)
    q = q.reshape(B, S, DA_HEADS, 2, DA_HEAD_DIM)
    k = k.reshape(B, S, DA_HEADS, 2, DA_HEAD_DIM)
    v = v.reshape(B, S, DA_HEADS, 2 * DA_HEAD_DIM)
    lam = (jnp.exp(jnp.sum(lq1.astype(F32) * lk1.astype(F32)))
           - jnp.exp(jnp.sum(lq2.astype(F32) * lk2.astype(F32))) + lam_init)
    o = diff_attention(q, k, v, lam, lam_init, subln_g).astype(h.dtype)
    om = memory_attention(qm, mem, mem_norm_g, w_mem_kv).astype(h.dtype)
    return jnp.concatenate([o, om], axis=-1) @ w_out

def hgrn2_chunkwise(q, k, v, log_f):
    B, S, H, dk = q.shape
    dv = v.shape[-1]
    nc = S // CHUNK

    def to_chunks(t):
        return t.astype(F32).reshape(B, nc, CHUNK, H, t.shape[-1]).transpose(1, 0, 3, 2, 4)

    xs = (to_chunks(q), to_chunks(k), to_chunks(v), to_chunks(log_f))
    causal = jnp.tril(jnp.ones((CHUNK, CHUNK), bool))[None, None, :, :, None]

    def step(state, inp):
        q_, k_, v_, g_ = inp
        b = jnp.cumsum(g_, axis=2)
        b_last = b[:, :, -1:, :]
        diff = jnp.where(causal, b[:, :, :, None, :] - b[:, :, None, :, :], 0.0)
        decay = jnp.where(causal, jnp.exp(diff), 0.0)
        attn = jnp.einsum('bhtsk,bhsk->bhts', q_[:, :, :, None, :] * decay, k_)
        o = (jnp.einsum('bhts,bhsv->bhtv', attn, v_)
             + jnp.einsum('bhtk,bhkv->bhtv', q_ * jnp.exp(b), state))
        state = (jnp.exp(b_last)[:, :, 0, :, None] * state
                 + jnp.einsum('bhsk,bhsv->bhkv', k_ * jnp.exp(b_last - b), v_))
        return state, o

    state0 = jnp.zeros((B, H, dk, dv), F32)
    _, o = lax.scan(step, state0, xs)
    return o.transpose(1, 0, 3, 2, 4).reshape(B, S, H, dv)

def hgrn2_mixer(h, mem, w_in, lb, out_norm_g, mem_norm_g, w_mem_kv, w_out):
    B, S, _ = h.shape
    proj = h @ w_in
    q, fz, i, g, qm = jnp.split(
        proj, [HG_KEY_WIDTH, 2 * HG_KEY_WIDTH, 2 * HG_KEY_WIDTH + HG_VAL_WIDTH,
               2 * HG_KEY_WIDTH + 2 * HG_VAL_WIDTH], axis=-1)
    fz32 = fz.astype(F32)
    f = lb + (1.0 - lb) * jax.nn.sigmoid(fz32)
    log_f = jnp.log(f)
    k = (1.0 - lb) * jax.nn.sigmoid(-fz32)
    heads = lambda t: t.reshape(B, S, HG_HEADS, -1)
    o = hgrn2_chunkwise(heads(q), heads(k), heads(i), heads(log_f))
    o = rms_norm(o, out_norm_g) * jax.nn.silu(heads(g).astype(F32))
    o = o.reshape(B, S, HG_VAL_WIDTH).astype(h.dtype)
    om = memory_attention(qm, mem, mem_norm_g, w_mem_kv).astype(h.dtype)
    return jnp.concatenate([o, om], axis=-1) @ w_out

def dense_swiglu(h, w_gate_up, w_down):
    gt, up = jnp.split(h @ w_gate_up, 2, axis=-1)
    return (jax.nn.silu(gt) * up) @ w_down

def moe_swiglu(h, w_router, w_gate_up, w_down):
    B, S, D = h.shape
    t = h.reshape(-1, D)
    logits = (t @ w_router).astype(F32)
    top_val, top_idx = lax.top_k(logits, TOP_K)
    top_w = jax.nn.softmax(top_val, axis=-1)
    combine = jnp.sum(jax.nn.one_hot(top_idx, N_EXPERTS, dtype=F32) * top_w[..., None], axis=1)
    out = jnp.zeros_like(t)
    for e in range(N_EXPERTS):
        gt, up = jnp.split(t @ w_gate_up[e], 2, axis=-1)
        y = (jax.nn.silu(gt) * up) @ w_down[e]
        out = out + combine[:, e:e + 1].astype(t.dtype) * y
    return out.reshape(B, S, D)

def first_inputs(seed: int = 0) -> dict:
    key = jax.random.key(seed)
    ks = iter(jax.random.split(key, 40))
    D = D_MODEL
    res = (2.0 * DEPTH) ** -0.5

    def nrm(shape, scale):
        return jax.random.normal(next(ks), shape, F32) * scale

    def gain(shape):
        return 1.0 + 0.02 * jax.random.normal(next(ks), shape, F32)

    return {
        "x": nrm((BATCH, SEQ, D), 1.0),
        "mem": nrm((BATCH, MEM_LEN, D), 1.0),
        "a_norm_mix": gain((N_A, D)),
        "a_w_in": nrm((N_A, D, 3 * DA_WIDTH + MEM_WIDTH), D ** -0.5),
        "a_lam_q1": nrm((N_A, DA_HEAD_DIM), 0.1),
        "a_lam_k1": nrm((N_A, DA_HEAD_DIM), 0.1),
        "a_lam_q2": nrm((N_A, DA_HEAD_DIM), 0.1),
        "a_lam_k2": nrm((N_A, DA_HEAD_DIM), 0.1),
        "a_subln": gain((N_A, 2 * DA_HEAD_DIM)),
        "a_mem_norm": gain((N_A, D)),
        "a_w_mem_kv": nrm((N_A, D, 2 * MEM_WIDTH), D ** -0.5),
        "a_w_out": nrm((N_A, MIX_WIDTH, D), MIX_WIDTH ** -0.5 * res),
        "b_norm_mix": gain((N_B, D)),
        "b_w_in": nrm((N_B, D, 2 * HG_KEY_WIDTH + 2 * HG_VAL_WIDTH + MEM_WIDTH), D ** -0.5),
        "b_lb_logits": nrm((N_B, HG_KEY_WIDTH), 0.5),
        "b_out_norm": gain((N_B, HG_VAL_DIM)),
        "b_mem_norm": gain((N_B, D)),
        "b_w_mem_kv": nrm((N_B, D, 2 * MEM_WIDTH), D ** -0.5),
        "b_w_out": nrm((N_B, HG_VAL_WIDTH + MEM_WIDTH, D), (HG_VAL_WIDTH + MEM_WIDTH) ** -0.5 * res),
        "dense_norm": gain((N_A, D)),
        "dense_w_gate_up": nrm((N_A, D, 2 * D_FF_DENSE), D ** -0.5),
        "dense_w_down": nrm((N_A, D_FF_DENSE, D), D_FF_DENSE ** -0.5 * res),
        "moe_norm": gain((N_B, D)),
        "moe_router": nrm((N_B, D, N_EXPERTS), D ** -0.5),
        "moe_w_gate_up": nrm((N_B, N_EXPERTS, D, 2 * D_FF_EXPERT), D ** -0.5),
        "moe_w_down": nrm((N_B, N_EXPERTS, D_FF_EXPERT, D), D_FF_EXPERT ** -0.5 * res),
        "final_norm": gain((D,)),
    }

def first_block(x, mem,
              a_norm_mix, a_w_in, a_lam_q1, a_lam_k1, a_lam_q2, a_lam_k2, a_subln, a_mem_norm, a_w_mem_kv, a_w_out,
              b_norm_mix, b_w_in, b_lb_logits, b_out_norm, b_mem_norm, b_w_mem_kv, b_w_out,
              dense_norm, dense_w_gate_up, dense_w_down,
              moe_norm, moe_router, moe_w_gate_up, moe_w_down,
              final_norm):
    lb_p = jax.nn.softmax(b_lb_logits.astype(F32), axis=0)
    lb_all = jnp.cumsum(lb_p, axis=0) - lb_p[0:1]
    for i in range(DEPTH):
        if i % N_MIXERS == 0:
            j = i // N_MIXERS
            lam_init = 0.8 - 0.6 * float(np.exp(-0.3 * i))
            h = rms_norm(x, a_norm_mix[j])
            x = x + diff_attention_mixer(h, mem, a_w_in[j], a_lam_q1[j], a_lam_k1[j], a_lam_q2[j], a_lam_k2[j],
                                         a_subln[j], a_mem_norm[j], a_w_mem_kv[j], a_w_out[j], lam_init)
        else:
            j = i // N_MIXERS
            h = rms_norm(x, b_norm_mix[j])
            x = x + hgrn2_mixer(h, mem, b_w_in[j], lb_all[j], b_out_norm[j], b_mem_norm[j],
                                b_w_mem_kv[j], b_w_out[j])
        if i % 2 == 0:
            j = i // 2
            x = x + dense_swiglu(rms_norm(x, dense_norm[j]), dense_w_gate_up[j], dense_w_down[j])
        else:
            j = i // 2
            x = x + moe_swiglu(rms_norm(x, moe_norm[j]), moe_router[j], moe_w_gate_up[j], moe_w_down[j])
    return rms_norm(x, final_norm)


DEPTH_2 = 1

D_MIX = D_MODEL
GLA_HEADS = 4
GLA_DV = (D_MIX // 2) // GLA_HEADS
GLA_DK = GLA_DV // 2
GLA_GATE_RANK = 16
GLA_TAU = 16.0
GLA_CHUNK = 64
MOBA_HEADS = 8
MOBA_HD = (D_MIX - GLA_HEADS * GLA_DV) // MOBA_HEADS
MOBA_BLOCK = 256
MOBA_TOPK = 3
MOBA_QCHUNK = 8
REL_BUCKETS = 32
REL_MAX_DIST = 128
D_FF = 4 * D_MODEL
N_ADA = 6

GLA_QK_W = GLA_HEADS * GLA_DK
GLA_V_W = GLA_HEADS * GLA_DV
MOBA_W = MOBA_HEADS * MOBA_HD
IN_WIDTHS = (GLA_QK_W, GLA_QK_W, GLA_V_W, GLA_V_W, GLA_GATE_RANK, MOBA_W, MOBA_W, MOBA_W)
D_IN = sum(IN_WIDTHS)
IN_SPLITS = [int(v) for v in np.cumsum(IN_WIDTHS)[:-1]]


def rmsnorm(x, g):
    xf = x.astype(jnp.float32)
    y = xf * lax.rsqrt(jnp.mean(xf * xf, axis=-1, keepdims=True) + EPS)
    return y.astype(x.dtype) * g

def modulate(h, shift, scale):
    return h * (1.0 + scale[:, None, :]) + shift[:, None, :]

def gla_mixer(q, k, v, log_a):
    B, S, H, dk = q.shape
    dv = v.shape[-1]
    C = GLA_CHUNK
    N = S // C
    f32 = jnp.float32

    def chunks(t):
        return t.astype(f32).reshape(B, N, C, H, t.shape[-1]).transpose(0, 3, 1, 2, 4)

    q = chunks(q) * (dk ** -0.5)
    k = chunks(k)
    v = chunks(v)
    g = chunks(log_a)
    b = jnp.cumsum(g, axis=3)
    b_last = b[:, :, :, -1:, :]
    b_ref = b[:, :, :, C // 2 - 1:C // 2, :]
    att = jnp.einsum('bhnid,bhnjd->bhnij', q * jnp.exp(b - b_ref), k * jnp.exp(b_ref - b))
    causal = jnp.tril(jnp.ones((C, C), dtype=bool))
    att = jnp.where(causal, att, 0.0)
    o_intra = jnp.einsum('bhnij,bhnjv->bhniv', att, v)
    kv = jnp.einsum('bhncd,bhncv->bhndv', k * jnp.exp(b_last - b), v)
    decay = jnp.exp(b_last[:, :, :, 0, :])

    def step(s_prev, inp):
        kv_n, dec_n = inp
        return dec_n[..., None] * s_prev + kv_n, s_prev

    s0 = jnp.zeros((B, H, dk, dv), f32)
    _, s_before = lax.scan(step, s0, (kv.transpose(2, 0, 1, 3, 4), decay.transpose(2, 0, 1, 3)))
    s_before = s_before.transpose(1, 2, 0, 3, 4)
    o_inter = jnp.einsum('bhncd,bhndv->bhncv', q * jnp.exp(b), s_before)
    o = o_intra + o_inter
    return o.transpose(0, 2, 3, 1, 4).reshape(B, S, H, dv)

def t5_bucket(rel):
    n = jnp.maximum(rel, 0)
    max_exact = REL_BUCKETS // 2
    ratio = jnp.maximum(n, 1).astype(jnp.float32) / max_exact
    large = max_exact + (jnp.log(ratio) / math.log(REL_MAX_DIST / max_exact)
                         * (REL_BUCKETS - max_exact)).astype(jnp.int32)
    large = jnp.minimum(large, REL_BUCKETS - 1)
    return jnp.where(n < max_exact, n, large)

def moba_mixer(q, k, v, rel_bias):
    B, S, H, hd = q.shape
    BLK = MOBA_BLOCK
    QC = MOBA_QCHUNK
    NB = -(-S // BLK)
    Sp = NB * BLK
    topk = min(MOBA_TOPK, NB)
    f32 = jnp.float32
    qh = q.transpose(0, 2, 1, 3) * (hd ** -0.5)
    pad = ((0, 0), (0, 0), (0, Sp - S), (0, 0))
    kb = jnp.pad(k.transpose(0, 2, 1, 3), pad).reshape(B, H, NB, BLK, hd)
    vb = jnp.pad(v.transpose(0, 2, 1, 3), pad).reshape(B, H, NB, BLK, hd)
    k_mean = jnp.mean(kb.astype(f32), axis=3)
    bias_flat = rel_bias.T.reshape(-1)
    head_off = (jnp.arange(H, dtype=jnp.int32) * REL_BUCKETS)[None, :, None, None]
    blk_pos = jnp.arange(BLK, dtype=jnp.int32)
    blk_ids = jnp.arange(NB, dtype=jnp.int32)
    nq = S // QC
    q_chunks = qh.reshape(B, H, nq, QC, hd).transpose(2, 0, 1, 3, 4)
    gather_blocks = jax.vmap(jax.vmap(lambda kk, ii: kk[ii]))

    def one_chunk(args):
        ci, q_c = args
        t = ci * QC + jnp.arange(QC, dtype=jnp.int32)
        own = (ci * QC) // BLK
        gate = jnp.einsum('bhqd,bhnd->bhqn', q_c.astype(f32), k_mean)
        gate = jnp.where(blk_ids < own, gate, -jnp.inf)
        gval, gidx = lax.top_k(gate, topk)
        valid = jnp.isfinite(gval)
        k_sel = gather_blocks(kb, gidx)
        v_sel = gather_blocks(vb, gidx)
        s_sel = jnp.einsum('bhqd,bhqkld->bhqkl', q_c, k_sel).astype(f32)
        pos_sel = gidx[..., None] * BLK + blk_pos
        rel_sel = t[None, None, :, None, None] - pos_sel
        s_sel = s_sel + bias_flat[head_off[..., None] + t5_bucket(rel_sel)]
        s_sel = jnp.where(valid[..., None], s_sel, -jnp.inf)
        k_own = lax.dynamic_slice_in_dim(kb, own, 1, axis=2)[:, :, 0]
        v_own = lax.dynamic_slice_in_dim(vb, own, 1, axis=2)[:, :, 0]
        s_own = jnp.einsum('bhqd,bhld->bhql', q_c, k_own).astype(f32)
        rel_own = t[:, None] - (own * BLK + blk_pos)[None, :]
        s_own = s_own + bias_flat[head_off + t5_bucket(rel_own)[None, None]]
        s_own = jnp.where(rel_own[None, None] >= 0, s_own, -jnp.inf)
        logits = jnp.concatenate([s_sel.reshape(B, H, QC, topk * BLK), s_own], axis=-1)
        p = jax.nn.softmax(logits, axis=-1)
        p_sel = p[..., :topk * BLK].reshape(B, H, QC, topk, BLK).astype(v.dtype)
        p_own = p[..., topk * BLK:].astype(v.dtype)
        return (jnp.einsum('bhqkl,bhqkld->bhqd', p_sel, v_sel)
                + jnp.einsum('bhql,bhld->bhqd', p_own, v_own))

    out = lax.map(one_chunk, (jnp.arange(nq, dtype=jnp.int32), q_chunks))
    return out.transpose(1, 0, 3, 2, 4).reshape(B, S, H, hd)

def second_inputs(seed: int = 0) -> dict:
    key = jax.random.key(seed)
    ks = jax.random.split(key, 16)
    f32 = jnp.float32
    nrm = lambda k, shape, s: (jax.random.normal(k, shape, f32) * s)
    gain = lambda k, shape: 1.0 + 0.05 * jax.random.normal(k, shape, f32)
    return {
        "x": nrm(ks[0], (BATCH, SEQ, D_MODEL), 1.0),
        "c": nrm(ks[1], (BATCH, D_MODEL), 1.0),
        "w_ada": nrm(ks[2], (DEPTH_2, D_MODEL, N_ADA * D_MODEL), D_MODEL ** -0.5),
        "b_ada": nrm(ks[3], (DEPTH_2, N_ADA * D_MODEL), 0.02),
        "g_mix": gain(ks[4], (DEPTH_2, D_MODEL)),
        "w_in": nrm(ks[5], (DEPTH_2, D_MODEL, D_IN), D_MODEL ** -0.5),
        "w_gla_gate": nrm(ks[6], (DEPTH_2, GLA_GATE_RANK, GLA_QK_W), GLA_GATE_RANK ** -0.5),
        "b_gla_gate": nrm(ks[7], (DEPTH_2, GLA_QK_W), 0.1),
        "g_gla_out": gain(ks[8], (DEPTH_2, GLA_V_W)),
        "rel_bias": nrm(ks[9], (REL_BUCKETS, MOBA_HEADS), 0.5),
        "w_out": nrm(ks[10], (DEPTH_2, D_MIX, D_MODEL), D_MIX ** -0.5),
        "g_mlp": gain(ks[11], (DEPTH_2, D_MODEL)),
        "w_ff1": nrm(ks[12], (DEPTH_2, D_MODEL, D_FF), D_MODEL ** -0.5),
        "w_ff2": nrm(ks[13], (DEPTH_2, D_FF, D_MODEL), D_FF ** -0.5),
        "g_final": gain(ks[14], (D_MODEL,)),
    }

def second_block(x, c, w_ada, b_ada, g_mix, w_in, w_gla_gate, b_gla_gate, g_gla_out, rel_bias,
              w_out, g_mlp, w_ff1, w_ff2, g_final):
    B, S, _ = x.shape
    c_act = jax.nn.silu(c)
    for l in range(DEPTH_2):
        ada = c_act @ w_ada[l] + b_ada[l]
        shift_a, scale_a, gate_a, shift_m, scale_m, gate_m = jnp.split(ada, N_ADA, axis=-1)
        h = modulate(rmsnorm(x, g_mix[l]), shift_a, scale_a)
        proj = h @ w_in[l]
        gq, gk, gv, gr, gg, mq, mk, mv = jnp.split(proj, IN_SPLITS, axis=-1)
        log_a = jax.nn.log_sigmoid((gg @ w_gla_gate[l] + b_gla_gate[l]).astype(jnp.float32)) / GLA_TAU
        o_gla = gla_mixer(gq.reshape(B, S, GLA_HEADS, GLA_DK), gk.reshape(B, S, GLA_HEADS, GLA_DK),
                          gv.reshape(B, S, GLA_HEADS, GLA_DV), log_a.reshape(B, S, GLA_HEADS, GLA_DK))
        o_gla = rmsnorm(o_gla.astype(x.dtype), g_gla_out[l].reshape(GLA_HEADS, GLA_DV))
        o_gla = o_gla.reshape(B, S, GLA_V_W) * jax.nn.silu(gr)
        o_moba = moba_mixer(mq.reshape(B, S, MOBA_HEADS, MOBA_HD), mk.reshape(B, S, MOBA_HEADS, MOBA_HD),
                            mv.reshape(B, S, MOBA_HEADS, MOBA_HD), rel_bias).reshape(B, S, MOBA_W)
        y = jnp.concatenate([o_gla, o_moba], axis=-1) @ w_out[l]
        x = x + gate_a[:, None, :] * y
        h = modulate(rmsnorm(x, g_mlp[l]), shift_m, scale_m)
        x = x + gate_m[:, None, :] * (jnp.square(jax.nn.relu(h @ w_ff1[l])) @ w_ff2[l])
    return rmsnorm(x, g_final)


def setup_inputs(seed=0):
    out = dict(first_inputs(seed))
    for name, value in second_inputs(seed + 1).items():
        if name != "x":
            out[name + "_2"] = value
    return out


def reference(
    x, mem, a_norm_mix, a_w_in, a_lam_q1, a_lam_k1, a_lam_q2, a_lam_k2, a_subln, a_mem_norm,
    a_w_mem_kv, a_w_out, b_norm_mix, b_w_in, b_lb_logits, b_out_norm, b_mem_norm, b_w_mem_kv,
    b_w_out, dense_norm, dense_w_gate_up, dense_w_down, moe_norm, moe_router, moe_w_gate_up,
    moe_w_down, final_norm, c_2, w_ada_2, b_ada_2, g_mix_2, w_in_2, w_gla_gate_2, b_gla_gate_2,
    g_gla_out_2, rel_bias_2, w_out_2, g_mlp_2, w_ff1_2, w_ff2_2, g_final_2,
):
    x = first_block(
        x, mem, a_norm_mix, a_w_in, a_lam_q1, a_lam_k1, a_lam_q2, a_lam_k2, a_subln, a_mem_norm,
        a_w_mem_kv, a_w_out, b_norm_mix, b_w_in, b_lb_logits, b_out_norm, b_mem_norm,
        b_w_mem_kv, b_w_out, dense_norm, dense_w_gate_up, dense_w_down, moe_norm, moe_router,
        moe_w_gate_up, moe_w_down, final_norm,
    )
    return second_block(
        x, c_2, w_ada_2, b_ada_2, g_mix_2, w_in_2, w_gla_gate_2, b_gla_gate_2, g_gla_out_2,
        rel_bias_2, w_out_2, g_mlp_2, w_ff1_2, w_ff2_2, g_final_2,
    )


_drawn_inputs = setup_inputs


def setup_inputs(seed=0):
    import zlib

    import numpy as np

    out = dict(_drawn_inputs(seed))
    spreads = {}
    factors = {'a_lam_k1': 3.059,
     'a_lam_q2': 3.217,
     'a_subln': 6.119,
     'a_mem_norm': 8.0,
     'b_norm_mix': 4.196,
     'b_out_norm': 8.0,
     'b_mem_norm': 8.0,
     'dense_norm': 4.298,
     'b_gla_gate_2': 3.188,
     'g_gla_out_2': 3.45,
     'moe_norm': 8.0}
    for name, (base, spread) in spreads.items():
        noise = np.random.default_rng([zlib.crc32(name.encode()), seed]).standard_normal(out[name].shape)
        drawn = base * np.exp(spread * noise) if base else spread * noise
        out[name] = __import__('jax').numpy.asarray(drawn.astype(out[name].dtype))
    for name, factor in factors.items():
        out[name] = (out[name] * factor).astype(out[name].dtype)
    return out
```

```python
from contextlib import ExitStack

import numpy as np

import concourse.bass as bass
from concourse import mybir

F32 = mybir.dt.float32
F32R = mybir.dt.float32r
BF16 = mybir.dt.bfloat16
I32 = mybir.dt.int32
U32 = mybir.dt.uint32
ALU = mybir.AluOpType
ACT = mybir.ActivationFunctionType
AX = mybir.AxisListType

P = 128
SEQ = 256
TILES = SEQ // P
D = 1024
KC = D // P
EPS = 1e-6
MASKED = -1e30

DA_HEADS = 6
DA_W = DA_HEADS * P
CHUNK = 64
LAM_INIT = 0.8 - 0.6 * float(np.exp(0.0))
MEM_PAIRS = 2
HG_HEADS = 6
HG_W = HG_HEADS * P
FF_DENSE = 2816
EXPERTS = 8
FF_EXPERT = 3584
CAPACITY = 128
GLA_HEADS = 4
GLA_DK = 64
GLA_W = GLA_HEADS * P
GLA_RANK = 16
GLA_TAU = 16.0
MOBA_PAIRS = 4
BUCKETS = 32
MAX_DIST = 128
FF2 = 4096
N_ADA = 6
PAIR_SCALE = 64 ** -0.5

UNIT = 2048
RING = 6
SPLIT = 2
HID = 256
DENSE_STEPS = FF_DENSE // HID
EXPERT_STEPS = FF_EXPERT // HID
FF2_STEPS = FF2 // HID
EXPERT_ROUNDS = EXPERT_STEPS // 2 - 1

C_IDENT, C_LATER, C_IOTA, C_TREE = 0, P, 2 * P, 3 * P
C_DIST = C_TREE + 8 * P
C_MASK = C_DIST + TILES * SEQ
C_BEFORE = C_MASK + TILES * SEQ
C_ALL = C_BEFORE + EXPERTS * EXPERTS

GAINS = ["a_mem_norm", "b_mem_norm", "a_norm_mix", "a_subln", "dense_norm", "b_norm_mix", "b_out_norm",
         "moe_norm", "final_norm", "g_mix_2", "g_gla_out_2", "g_mlp_2", "g_final_2"]

STAGES = ["prep", "memory", "a_in", "diff", "a_mem", "a_out", "dense", "b_in", "hgrn", "b_mem", "b_out",
          "route", "experts", "ada", "in_2", "gla", "moba", "out_2", "ff_2", "final"]


def constants():
    c = np.zeros((P, C_ALL), np.float32)
    a = np.arange(P)
    c[:, C_IDENT:C_IDENT + P] = np.eye(P)
    c[:, C_LATER:C_LATER + P] = a[:, None] < a[None, :]
    c[:, C_IOTA:C_IOTA + P] = a[None, :]
    c[:, C_TREE:C_TREE + P] = np.eye(P)
    for level in range(7):
        s, t = a[:, None] >> level, a[None, :] >> level
        c[:, C_TREE + (level + 1) * P:C_TREE + (level + 2) * P] = (t == s + 1) & (s % 2 == 0)
    for tile in range(TILES):
        q, k = tile * P + a[:, None], np.arange(SEQ)[None, :]
        c[:, C_DIST + tile * SEQ:C_DIST + (tile + 1) * SEQ] = abs(q - k)
        c[:, C_MASK + tile * SEQ:C_MASK + (tile + 1) * SEQ] = np.where(k // CHUNK <= q // CHUNK, 0.0, MASKED)
    e = np.arange(EXPERTS)
    c[:, C_BEFORE:] = (e[None, :] < e[:, None]).astype(np.float32).reshape(1, -1)
    n = np.arange(2 * SEQ) - (SEQ - 1)
    exact = BUCKETS // 2
    ratio = np.maximum(n, 1).astype(np.float32) / exact
    large = exact + (np.log(ratio) / np.float32(np.log(MAX_DIST / exact)) * (BUCKETS - exact)).astype(np.int32)
    bucket = np.where(n < exact, n, np.minimum(large, BUCKETS - 1))
    b = np.zeros((BUCKETS + 1, 2 * SEQ), np.float32)
    b[:BUCKETS] = (np.arange(BUCKETS)[:, None] == bucket[None, :]) & (n >= 0)[None, :] & (n < SEQ)[None, :]
    b[BUCKETS] = np.where((n < 0) | (n >= SEQ), MASKED, 0.0)
    return c, b


class Signals:

    def __init__(self, who, semaphore, numbers):
        self.who, self.semaphore, self.numbers = who, semaphore, numbers
        self.name, self.sem, self.n = None, None, 0

    def stage(self, name):
        self.name = f"{self.who}_{name}"
        self.sem, self.n = self.semaphore(self.name), 0

    def __call__(self, *label):
        self.n += 1
        if label:
            assert label not in self.numbers, label
            self.numbers[label] = (self.name, self.n)
        return self.sem

    def also(self, *label):
        self.numbers[label] = (self.name, self.n)

    def last(self):
        return self.sem, self.n


def program(nc, A, consts, buckets, out, semaphores, numbers, known, stages, capacity):
    ctx = ExitStack()

    def sb(name, shape, dt=F32, stack=ctx):
        return stack.enter_context(nc.sbuf_tensor(name, shape, dt))

    def semaphore(name):
        if name not in semaphores:
            semaphores[name] = ctx.enter_context(nc.semaphore(name))
        return semaphores[name]

    def at(*label):
        if known is None:
            return semaphore("prep_dry"), 1
        name, n = known[label]
        return semaphore(name), n

    with ctx:
        raw = sb("raw", [P, RING, UNIT])
        w_hi = sb("w_hi", [P, SPLIT, UNIT], F32R)
        w_lo = sb("w_lo", [P, SPLIT, UNIT], F32R)
        x = sb("x", [P, TILES, D])
        gain = sb("gain", [P, 2, D])
        hT_hi = sb("hT_hi", [P, KC, SEQ], F32R)
        hT_lo = sb("hT_lo", [P, KC, SEQ], F32R)
        con = sb("con", [P, C_ALL])
        mix = sb("mix", [P, TILES, D])
        kv = sb("kv", [P, 2, TILES, 512])
        zero = sb("zero", [P, P], BF16)
        sumsq = sb("sumsq", [P, TILES])
        rstd = sb("rstd", [P, TILES])
        top = sb("top", [P, 2, 4])
        sums = sb("sums", [P, 2, 4])
        headsq = sb("headsq", [P, TILES * HG_HEADS])
        neg_lam = sb("neg_lam", [P, 4])
        lb = sb("lb", [P, 4, HG_HEADS])
        b_gate = sb("b_gate", [P, 2])
        flag = sb("flag", [P, 2], I32)
        ident = con[:, C_IDENT:C_IDENT + P]
        over = ExitStack()
        proj = sb("proj", [P, TILES, 3584], F32, over)
        work = sb("work", [P, 9728], F32, over)
        over.close()
        hid_hi = sb("hid_hi", [P, 3, 2, SEQ], F32R, over)
        hid_lo = sb("hid_lo", [P, 3, 2, SEQ], F32R, over)
        hid = sb("hid", [P, 3, TILES, HID], F32, over)
        gated = sb("gated", [P, 2, TILES, HID], F32, over)
        moe_h_hi = sb("moe_h_hi", [P, TILES, D], F32R, over)
        moe_h_lo = sb("moe_h_lo", [P, TILES, D], F32R, over)
        slot_hi = sb("slot_hi", [P, KC, P], F32R, over)
        slot_lo = sb("slot_lo", [P, KC, P], F32R, over)
        y_hi = sb("y_hi", [P, D], F32R, over)
        y_lo = sb("y_lo", [P, D], F32R, over)
        pick = sb("pick", [P, TILES, P], F32R, over)
        pickT = sb("pickT", [P, TILES, P], F32R, over)
        staged = sb("staged", [P, TILES * P], F32, over)
        w_router = sb("w_router", [P, KC, EXPERTS], F32, over)
        logits = sb("logits", [P, TILES, EXPERTS], F32, over)
        best = sb("best", [P, TILES, 8], F32, over)
        pairs_gt = sb("pairs_gt", [P, TILES, 64], F32, over)
        pairs_eq = sb("pairs_eq", [P, TILES, 64], F32, over)
        rank = sb("rank", [P, TILES, EXPERTS], F32, over)
        chosen = sb("chosen", [P, TILES, EXPERTS], F32, over)
        share = sb("share", [P, TILES, EXPERTS], F32, over)
        share2 = sb("share2", [P, TILES, EXPERTS], F32, over)
        place = sb("place", [P, 2, TILES, EXPERTS], F32, over)
        ratio = sb("ratio", [P, 4, TILES], F32, over)
        counts = sb("counts", [P, EXPERTS + 1], F32, over)
        ones = sb("ones", [P, P], F32, over)
        over.close()
        ada = sb("ada", [P, N_ADA, D], F32, over)
        proj2 = sb("proj2", [P, TILES, 3088], F32, over)
        work2 = sb("work2", [P, 4096], F32, over)
        c_col = sb("c_col", [P, KC], F32, over)
        w_gate = sb("w_gate", [GLA_RANK, 256], F32, over)
        over.close()
        ada_keep = sb("ada_keep", [P, N_ADA, D], F32, over)
        hid2_hi = sb("hid2_hi", [P, 3, 2, SEQ], F32R, over)
        hid2_lo = sb("hid2_lo", [P, 3, 2, SEQ], F32R, over)
        hid2 = sb("hid2", [P, 3, TILES, HID], F32, over)
        over.close()

        bank = [ctx.enter_context(nc.psum_tensor(f"bank{i}", [P, 512], F32)) for i in range(8)]
        rel_rows = nc.dram_tensor("rel_rows", (2 * MOBA_PAIRS, 2 * SEQ), F32, kind="Internal").ap()

        G = {}
        g = 0
        for name, units in (("kv_a", 2), ("kv_b", 2), ("a_in", 10), ("a_out", 4), ("dense", 3 * DENSE_STEPS),
                            ("b_in", 14), ("b_out", 4), ("experts", 3 * EXPERT_STEPS * EXPERTS),
                            ("ada", 24), ("in_2", 13), ("out_2", 4), ("ff_2", 2 * FF2_STEPS)):
            G[name] = g
            g += units
        B = {}
        b = 0
        for name, blocks in (("kv_a", 1), ("kv_b", 1), ("a_in", 5), ("a_out", 2), ("b_in", 7), ("b_out", 2),
                             ("ada", 12), ("in_2", 7), ("out_2", 2)):
            B[name] = b
            b += blocks

        class Ring:

            def __init__(self, name, first=0, credit=0):
                self.first, self.credit = first, credit
                self.landed = [semaphore(f"{name}landed{i}") for i in range(RING)]
                self.hi = semaphore(f"{name}hi_ready")
                self.lo = semaphore(f"{name}lo_ready")
                self.hi_used = semaphore(f"{name}unit_hi_used")
                self.used = semaphore(f"{name}unit_used")

        ring = Ring("")
        more_ring = Ring("more_", G["experts"], RING)
        block_out = semaphore("block_out")
        gain_in = [semaphore("gain_in0"), semaphore("gain_in1")]
        loaded = {n: semaphore(f"in_{n}") for n in
                  ("con", "x", "mem", "lam", "rel", "lb", "router", "c", "b_ada", "bgate", "bias0", "bias1")}
        rel_stored = semaphore("rel_stored")
        out_stored = semaphore("out_stored")

        def have(name):
            return name in stages

        block = ctx.enter_context(nc.Block())

        def wide(ap):
            return ap.rearrange("l (k p) n -> p (l k) n", p=P)

        W = {"kv_a": wide(A["a_w_mem_kv"]), "kv_b": wide(A["b_w_mem_kv"]), "a_in": wide(A["a_w_in"]),
             "a_out": wide(A["a_w_out"]), "b_in": wide(A["b_w_in"]), "b_out": wide(A["b_w_out"]),
             "ada": wide(A["w_ada_2"]), "in_2": wide(A["w_in_2"]), "out_2": wide(A["w_out_2"])}
        W_dense_up = A["dense_w_gate_up"].rearrange("l (k p) (two n) -> p (l k) two n", p=P, two=2)
        W_dense_down = wide(A["dense_w_down"])
        W_up = A["moe_w_gate_up"].rearrange("l e (k p) (two n) -> p (l e) k two n", p=P, two=2)
        W_down = A["moe_w_down"].rearrange("l e (k p) n -> p (l e) k n", p=P)
        W_ff1 = wide(A["w_ff1_2"])
        W_ff2 = wide(A["w_ff2_2"])

        def columns(n):
            return [(c, min(512, n - c)) for c in range(0, n, 512)]

        COLS = {"kv_a": columns(512), "kv_b": columns(512), "a_in": columns(3 * DA_W + 256),
                "a_out": columns(D), "b_in": columns(4 * HG_W + 256), "b_out": columns(D),
                "in_2": [(0, 512), (512, 512), (1024, 512), (1552, 512), (2064, 512), (2576, 512)],
                "out_2": columns(D)}

        def repeat(eng, n, body):
            with eng.Fori(0, n) as i:
                body(i)

        def rel_places():
            return work[0:BUCKETS + 1, 0:8], work[0:BUCKETS + 1, 8:520], work[0:8, 520:1032]

        def lam_place():
            return work[:, 1032:1288].rearrange("p (a n) -> p a n", a=4)

        def bias_place(i):
            return kv[:, i % 2].rearrange("p m (t s) -> p m t s", t=TILES)

        def part(buf, start, *dims):
            n = int(np.prod(dims))
            names = "abc"[:len(dims)]
            pattern = "p (" + " ".join(names) + ") -> p " + " ".join(names)
            return buf[:, start:start + n].rearrange(pattern, **dict(zip(names, dims)))

        class Pairs:

            def __init__(self, tag, n, qT, kT, q_cols, k_cols, probs, probsT, v, dv, first):
                self.tag, self.n, self.qT, self.kT = tag, n, qT, kT
                self.q_cols, self.k_cols = q_cols, k_cols
                self.probs, self.probsT, self.v, self.dv, self.first = probs, probsT, v, dv, first

        diff_bias = part(work, 7168, TILES, SEQ)
        diff_sum = part(work, 7680, 4, P)
        head_scratch = part(work, 8192, TILES, HG_W)
        diff = Pairs("diff", DA_HEADS, part(work, 0, DA_HEADS, SEQ), part(work, 1536, DA_HEADS, SEQ),
                     [proj[:, t, i * P:(i + 1) * P] for i in range(DA_HEADS) for t in range(TILES)],
                     [proj[:, t, DA_W + i * P:DA_W + (i + 1) * P] for i in range(DA_HEADS) for t in range(TILES)],
                     [part(work, 3072 + 1024 * k, 2, TILES, SEQ) for k in range(2)],
                     [part(work, 5120 + 1024 * k, 2, TILES, SEQ) for k in range(2)],
                     lambda i, m, t: proj[:, t, 2 * DA_W + i * P:2 * DA_W + (i + 1) * P], P, 0)

        def memory_pairs(tag, layer, q0):
            kvl = kv[:, layer]
            return Pairs(tag, MEM_PAIRS, part(work, 0, MEM_PAIRS, SEQ), part(work, 512, MEM_PAIRS, SEQ),
                         [proj[:, t, q0 + i * P:q0 + (i + 1) * P] for i in range(MEM_PAIRS) for t in range(TILES)],
                         [kvl[:, t, i * P:(i + 1) * P] for i in range(MEM_PAIRS) for t in range(TILES)],
                         [part(work, 3072 + 1024 * k, 2, TILES, SEQ) for k in range(2)],
                         [part(work, 5120 + 1024 * k, 2, TILES, SEQ) for k in range(2)],
                         lambda i, m, t: kvl[:, t, 256 + (2 * i + m) * 64:256 + (2 * i + m + 1) * 64], 64, 768)

        a_mem = memory_pairs("a_mem", 0, 3 * DA_W)
        b_mem = memory_pairs("b_mem", 1, 4 * HG_W)
        M0 = 3 * 512 + GLA_RANK
        moba = Pairs("moba", MOBA_PAIRS, part(work2, 0, MOBA_PAIRS, SEQ), part(work2, 1024, MOBA_PAIRS, SEQ),
                     [proj2[:, t, M0 + i * P:M0 + (i + 1) * P] for i in range(MOBA_PAIRS) for t in range(TILES)],
                     [proj2[:, t, M0 + 512 + i * P:M0 + 512 + (i + 1) * P] for i in range(MOBA_PAIRS) for t in range(TILES)],
                     [proj2[:, k, 0:1024].rearrange("p (m t s) -> p m t s", m=2, t=TILES) for k in range(2)],
                     [proj2[:, k, M0:M0 + 1024].rearrange("p (m t s) -> p m t s", m=2, t=TILES) for k in range(2)],
                     lambda i, m, t: proj2[:, t, M0 + 1024 + (2 * i + m) * 64:M0 + 1024 + (2 * i + m + 1) * 64], 64, 512)

        class Decayed:

            def __init__(self, tag, groups, per, place, keys, v, widths):
                self.tag, self.groups, self.per = tag, groups, per
                self.heads = groups * per
                n = groups * SEQ
                self.q, self.k, self.after, self.before = (part(place, i * n, groups, SEQ) for i in range(4))
                self.att = [part(place, 4 * n + i * 512, 4, P) for i in range(self.heads * TILES // 4)]
                self.cross = part(place, 4 * n + self.heads * TILES * P, self.heads, P)
                self.dq = mix[:, :, :].rearrange("p t d -> p (t d)")[:, 0:n].rearrange("p (g s) -> p g s", g=groups)
                self.dk = keys.rearrange("p (g s) -> p g s", g=groups)
                self.v = v
                self.widths = widths
                if per == 1:
                    self.outs = [(h, t) for h in range(self.heads) for t in range(TILES)]
                else:
                    self.outs = [(per * g + hh, t) for hh in range(per) for g in range(groups) for t in range(TILES)]

            def rows(self, h):
                n = P // self.per
                return slice((h % self.per) * n, (h % self.per + 1) * n)

        hgrn = Decayed("hgrn", HG_HEADS, 1, work, proj[:, 0, 0:1536],
                       lambda h, t: proj[:, t, 2 * HG_W + h * P:2 * HG_W + (h + 1) * P], None)
        gla = Decayed("gla", GLA_HEADS // 2, 2, work2, proj2[:, 0, 0:512],
                      lambda h, t: proj2[:, t, 512 + h * P:512 + (h + 1) * P], None)
        LEVELS = 7

        def cross_banks(d):
            if d.per == 1:
                return [list(range(h, min(h + 4, d.heads))) for h in range(0, d.heads, 4)]
            return [list(range(hh, d.heads, d.per)) for hh in range(d.per)]

        def out_pieces(d):
            return [(t, h, min(4, d.heads - h)) for t in range(TILES) for h in range(0, d.heads, 4)]

        SCATTER = (1, 3, 6, 7)

        def gla_rankT():
            return work2[0:GLA_RANK, 3584:3840]

        class Loop:

            def __init__(self, name):
                self.gated = semaphore(f"{name}_gated")
                self.hidden = semaphore(f"{name}_hidden")
                self.turned = semaphore(f"{name}_hidden_turned")
                self.hid_hi = semaphore(f"{name}_hidden_hi")
                self.hid_lo = semaphore(f"{name}_hidden_lo")

        class ExpertLoop(Loop):
            def __init__(self, name):
                super().__init__(name)
                self.picked = semaphore(f"{name}_picked")
                self.pick_turned = semaphore(f"{name}_pick_turned")
                self.staged = semaphore(f"{name}_pick_staged")
                self.pickT = semaphore(f"{name}_pickT")
                self.gathered = semaphore(f"{name}_gathered")
                self.slots_hi = semaphore(f"{name}_slots_hi")
                self.slots_lo = semaphore(f"{name}_slots_lo")
                self.y_hi = semaphore(f"{name}_y_hi")
                self.y_lo = semaphore(f"{name}_y_lo")
                self.scattered = semaphore(f"{name}_scattered")
                self.added = semaphore(f"{name}_added")

        dense_loop = Loop("dense")
        expert_loop = ExpertLoop("expert")
        more_loop = ExpertLoop("more")
        ff_loop = Loop("ff")

        def tree_keys(pool, S, tag):
            d = hgrn if tag == "hgrn" else gla
            for level in range(LEVELS + 2):
                pool.wait_ge(*at(tag, "before", level if level > 1 else 0))
                if level > 0:
                    pool.wait_ge(*at(tag, "level", level - 1))
                if level <= LEVELS:
                    o, a, b = d.dk, d.k, d.before
                else:
                    o, a, b = (z[:, :, 0:P] for z in (d.dk, d.k, d.before))
                pool.tensor_tensor(o, a, b, ALU.mult).then_inc(S(tag, "keys", level), 1)

        assert EXPERT_STEPS % 2 == 0 and EXPERT_STEPS * 3 % RING == 0
        FIRST_ROUND = G["experts"] + 2
        NEXT_ROUND = FIRST_ROUND + RING
        TAIL = FIRST_ROUND + RING * EXPERT_ROUNDS
        NEXT_FIRST = TAIL + RING
        PER_EXPERT = 3 * EXPERT_STEPS // RING

        def expert_order(eng, first, rounds, tail, next_first):
            first()
            with eng.Fori(0, EXPERTS - 1) as e:
                with eng.Fori(0, EXPERT_ROUNDS - 1) as i:
                    rounds(e, i)
                tail(e, False)
                next_first(e)
            with eng.Fori(0, EXPERT_ROUNDS - 1) as i:
                rounds(EXPERTS - 1, i)
            tail(EXPERTS - 1, True)

        @block.sync
        def _(sp):
            def load(R, g, rounds, src, split):
                before = g - R.first - RING + 1 + R.credit
                if before > 0:
                    sp.wait_ge(R.hi, before + RING * rounds)
                    sp.wait_ge(R.lo, before + RING * rounds)
                dst = split(raw[:, g % RING, :])
                for n in range(2):
                    if split is two:
                        d, c = dst[:, :, n, :], src[:, :, n, :]
                    else:
                        k = dst.shape[1] // 2
                        d, c = dst[:, n * k:(n + 1) * k, :], src[:, n * k:(n + 1) * k, :]
                    sp.dma_start(d, c).then_inc(R.landed[g % RING], 16)

            def half(n):
                return lambda u: u[:, 0:4 * n].rearrange("p (k n) -> p k n", k=4)

            def load_block(name, j):
                c, n = COLS[name][j]
                for h in range(2):
                    load(ring, G[name] + 2 * j + h, 0, W[name][:, 4 * h:4 * h + 4, c:c + n], half(n))

            def two(u):
                return u.rearrange("p (k two n) -> p k two n", k=4, two=2)

            def down(u):
                return u.rearrange("p (k n) -> p k n", k=2)

            for name in ("kv_a", "kv_b"):
                if have("memory"):
                    load_block(name, 0)
            for name in ("a_in", "a_out"):
                if have(name):
                    for j in range(len(COLS[name])):
                        load_block(name, j)
            if have("dense"):
                def dense_step(g, rounds, step, n):
                    for s in range(n):
                        for h in range(2):
                            load(ring, g + 2 * s + h, rounds,
                                 W_dense_up[:, 4 * h:4 * h + 4, :, bass.ds((step + s) * HID, HID)], two)
                    for s in range(n):
                        load(ring, g + 2 * n + s, rounds, W_dense_down[:, bass.ds((step + s) * 2, 2), :], down)

                repeat(sp, DENSE_STEPS // 2, lambda i: dense_step(G["dense"], i, 2 * i, 2))
                last = DENSE_STEPS - 1
                dense_step(G["dense"] + 3 * last, 0, last, 1)
            for name in ("b_in", "b_out"):
                if have(name):
                    for j in range(len(COLS[name])):
                        load_block(name, j)
            if have("experts"):
                def experts(R):
                    def up(g, rounds, e, step, h):
                        load(R, g, rounds, W_up[:, bass.ds(e, 1), 4 * h:4 * h + 4, :, bass.ds(step * HID, HID)]
                             .rearrange("p e k two n -> p (e k) two n"), two)

                    def down_rows(g, rounds, e, step):
                        load(R, g, rounds, W_down[:, bass.ds(e, 1), bass.ds(step * 2, 2), :]
                             .rearrange("p e k n -> p (e k) n"), down)

                    def one_round(g, rounds, e, i):
                        up(g, rounds, e, 2 * i + 1, 0)
                        up(g + 1, rounds, e, 2 * i + 1, 1)
                        down_rows(g + 2, rounds, e, 2 * i)
                        up(g + 3, rounds, e, 2 * i + 2, 0)
                        up(g + 4, rounds, e, 2 * i + 2, 1)
                        down_rows(g + 5, rounds, e, 2 * i + 1)

                    def first():
                        up(G["experts"], 0, 0, 0, 0)
                        up(G["experts"] + 1, 0, 0, 0, 1)
                        one_round(FIRST_ROUND, 0, 0, 0)

                    def tail(e, last):
                        n, r = EXPERT_STEPS, PER_EXPERT * e
                        up(TAIL, r, e, n - 1, 0)
                        up(TAIL + 1, r, e, n - 1, 1)
                        down_rows(TAIL + 2, r, e, n - 2)
                        if last:
                            down_rows(TAIL + 3, r, e, n - 1)
                        else:
                            up(TAIL + 3, r, e + 1, 0, 0)
                            down_rows(TAIL + 4, r, e, n - 1)
                            up(TAIL + 5, r, e + 1, 0, 1)

                    expert_order(sp, first,
                                 lambda e, i: one_round(NEXT_ROUND, PER_EXPERT * e + i, e, i + 1), tail,
                                 lambda e: one_round(NEXT_FIRST, PER_EXPERT * e, e + 1, 0))

                experts(ring)
                sp.wait_ge(*at("overflow"))
                more = sp.value_load(flag[0:1, 0:1], min_val=0, max_val=1)
                with sp.If(more > 0):
                    sp.wait_ge(ring.hi, G["ada"])
                    sp.wait_ge(ring.lo, G["ada"])
                    experts(more_ring)
                    sp.wait_ge(more_ring.hi, RING + G["ada"] - G["experts"])
                    sp.wait_ge(more_ring.lo, RING + G["ada"] - G["experts"])
            if have("ada"):
                def ada_blocks(i):
                    for j in range(3):
                        for h in range(2):
                            load(ring, G["ada"] + 2 * j + h, i,
                                 W["ada"][:, 4 * h:4 * h + 4, bass.ds(i * 1536 + j * 512, 512)], half(512))
                repeat(sp, 4, ada_blocks)
            if have("in_2"):
                for j in range(6):
                    load_block("in_2", j)
                load(ring, G["in_2"] + 12, 0, W["in_2"][:, :, 1536:1552],
                     lambda u: u[:, 0:KC * GLA_RANK].rearrange("p (k n) -> p k n", k=KC))
            if have("out_2"):
                for j in range(2):
                    load_block("out_2", j)
            if have("ff_2"):
                def ff_up(g, rounds, step):
                    load(ring, g, rounds, W_ff1[:, :, bass.ds(step * HID, HID)],
                         lambda u: u.rearrange("p (k n) -> p k n", k=KC))

                def ff_down(g, rounds, step):
                    load(ring, g, rounds, W_ff2[:, bass.ds(step * 2, 2), :], down)

                def ff_steps(i):
                    g0 = G["ff_2"]
                    ff_up(g0, i, 3 * i)
                    ff_up(g0 + 1, i, 3 * i + 1)
                    ff_down(g0 + 2, i, 3 * i)
                    ff_up(g0 + 3, i, 3 * i + 2)
                    ff_down(g0 + 4, i, 3 * i + 1)
                    ff_down(g0 + 5, i, 3 * i + 2)
                repeat(sp, FF2_STEPS // 3, ff_steps)
                ff_up(G["ff_2"] + 30, 0, 15)
                ff_down(G["ff_2"] + 31, 0, 15)

        @block.gpsimd
        def _(pool):
            S = Signals("pool", semaphore, numbers)
            S.stage("main")
            pool.dma_start(con[:, :], consts).then_inc(loaded["con"], 16)
            pool.dma_start(mix[:, :, :], A["mem"][0].rearrange("(t p) d -> p t d", p=P)).then_inc(loaded["mem"], 16)
            pool.memset(zero[:, :], 0.0).then_inc(S("zero"), 1)
            uses = [0]

            def load_gain():
                n = uses[0]
                name = GAINS[n]
                src = A[name]
                if len(src.shape) == 2:
                    src = src[0]
                if n >= 2:
                    pool.wait_ge(*at("gain used", n - 2))
                pool.dma_start(gain[:, n % 2, 0:src.shape[0]], src.partition_broadcast(P)).then_inc(gain_in[n % 2], 16)
                uses[0] += 1

            load_gain()
            load_gain()
            relx, onehot, relout = rel_places()
            pool.memset(relx, 1.0).then_inc(S("relx"), 1)
            pool.wait_ge(*S.last())
            pool.dma_start(relx[0:BUCKETS, :], A["rel_bias_2"]).then_inc(loaded["rel"], 16)
            pool.dma_start(onehot, buckets).then_inc(loaded["rel"], 16)
            pool.dma_start(x[:, :, :], A["x"][0].rearrange("(t p) d -> p t d", p=P)).then_inc(loaded["x"], 16)
            lam4 = lam_place()
            for n, name in enumerate(("a_lam_q1", "a_lam_q2", "a_lam_k1", "a_lam_k2")):
                pool.dma_start(lam4[:, n, :], A[name][0].partition_broadcast(P)).then_inc(loaded["lam"], 16)
            pool.dma_start(lb[:, 0, :], A["b_lb_logits"].rearrange("l (h p) -> p (l h)", p=P),
                           allow_slow_non_contiguous=True).then_inc(loaded["lb"], 16)
            pool.dma_start(b_gate[:, :], A["b_gla_gate_2"].rearrange("l (g p) -> p (l g)", p=P),
                           allow_slow_non_contiguous=True).then_inc(loaded["bgate"], 16)
            pool.wait_ge(*at("rel rows"))
            pool.dma_start(rel_rows, relout).then_inc(rel_stored, 16)
            if have("a_in"):
                load_gain()
            if have("diff"):
                load_gain()
            if have("dense"):
                load_gain()
            if have("b_in"):
                load_gain()
            if have("hgrn"):
                load_gain()
                tree_keys(pool, S, "hgrn")
            if have("route"):
                pool.wait_ge(*at("b_out", "added", 1))
                pool.dma_start(w_router[:, :, :], A["moe_router"].rearrange("l (k p) e -> p (l k) e", p=P)).then_inc(loaded["router"], 16)
                load_gain()
            if have("ada"):
                load_gain()
                pool.wait_ge(*at("experts done"))
                pool.dma_start(ada[:, :, :].rearrange("p a d -> p (a d)"), A["b_ada_2"][0].partition_broadcast(P)).then_inc(loaded["b_ada"], 16)
                pool.dma_start(c_col[:, :], A["c_2"].rearrange("b (k p) -> p (b k)", p=P),
                               allow_slow_non_contiguous=True).then_inc(loaded["c"], 16)
                pool.dma_start(w_gate[:, :], A["w_gla_gate_2"][0]).then_inc(loaded["c"], 16)
            if have("in_2"):
                load_gain()
            if have("gla"):
                load_gain()
                tree_keys(pool, S, "gla")
            if have("moba"):
                pool.wait_ge(rel_stored, 16)
                for i in range(MOBA_PAIRS):
                    if i >= 2:
                        pool.wait_ge(*at("moba", "biased", i - 2))
                    else:
                        pool.wait_ge(*at("gla", "products"))
                    for m in range(2):
                        src = bass.AP(rel_rows.tensor, (2 * i + m) * 2 * SEQ, [[1, P], [P, TILES], [1, SEQ]])
                        pool.dma_start(bias_place(i)[:, m], src).then_inc(loaded[f"bias{i % 2}"], 16)
            if have("ff_2"):
                load_gain()
            if have("final"):
                load_gain()
            pool.wait_ge(*at("result"))
            pool.dma_start(out[0].rearrange("(t p) d -> p t d", p=P), x[:, :, :]).then_inc(out_stored, 16)
            pool.wait_ge(rel_stored, 16)
            pool.wait_ge(out_stored, 16)

        def flat(ap):
            return ap.rearrange("p a b -> p (a b)")

        NORM_BLOCKS = [(kc, t) for kc in range(KC) for t in range(TILES)]

        @block.scalar
        def _(act):
            S = Signals("scalar", semaphore, numbers)
            S.stage("prep")

            def split_hi(R, g, rounds, n=UNIT):
                u = g - R.first
                act.wait_ge(R.landed[g % RING], 32 * (u // RING + 1) + 32 * rounds)
                before = u - SPLIT + 1 + R.credit
                if before > 0:
                    act.wait_ge(R.hi_used, before + RING * rounds)
                    act.wait_ge(R.lo, before + RING * rounds)
                act.activation(w_hi[:, g % SPLIT, 0:n], raw[:, g % RING, 0:n], ACT.Copy).then_inc(R.hi, 1)

            def norm(tag, src, junk, *waits):
                for w in waits:
                    act.wait_ge(*w)
                for t in range(TILES):
                    sq = act.activation(junk[:, t, 0:D], src[:, t, :], ACT.Square, accum_out=sumsq[:, t:t + 1])
                sq.then_inc(S(tag, "squares"), 1)
                act.wait_ge(*at(tag, "variance"))
                act.activation(rstd[:, :], sumsq[:, :], ACT.Sqrt).then_inc(S(tag, "deviation"), 1)

            def turn_split(tag, unit):
                act.wait_ge(ring.used, unit) if unit else None
                for n in range(4):
                    act.wait_ge(*at(tag, "turned", n))
                    act.activation(flat(hT_hi[:, 2 * n:2 * n + 2, :]), bank[6 + n % 2][:, :], ACT.Copy)\
                       .then_inc(S(tag, "hi", n), 1)

            def turn_copy(tag, dst, cols, scale=1.0):
                for n in range(0, cols, 512):
                    act.wait_ge(*at(tag, "turned", n // 512))
                    act.activation(dst[:, n:n + 512], bank[6 + n // 512 % 2][:, 0:min(512, cols - n)], ACT.Copy, scale=scale)\
                       .then_inc(S(tag, "taken", n // 512), 1)

            def product(name, dst):
                def leave(j):
                    c, n = COLS[name][j]
                    act.wait_ge(ring.used, G[name] + 2 * j + 2)
                    for t in range(TILES):
                        out_ = act.activation(dst[:, t, c:c + n], bank[2 * ((B[name] + j) % 3) + t][:, 0:n], ACT.Copy)
                    out_.then_inc(block_out, 1)

                for j, (c, n) in enumerate(COLS[name]):
                    for h in range(2):
                        split_hi(ring, G[name] + 2 * j + h, 0, 4 * n)
                    if j > 0 and dst is not None:
                        leave(j - 1)
                if dst is not None:
                    leave(len(COLS[name]) - 1)

            def pairs(a):
                turn_copy(a.tag + "_q", flat(a.qT), a.n * SEQ)
                turn_copy(a.tag + "_k", flat(a.kT), a.n * SEQ)
                for i in range(a.n):
                    k = i % 2
                    act.wait_ge(*at(a.tag, "max", i))
                    for m in range(2):
                        for t in range(TILES):
                            j = 2 * m + t
                            e = act.activation(a.probs[k][:, m, t, :], a.probs[k][:, m, t, :], ACT.Exp,
                                               bias=top[:, k, j:j + 1], accum_out=sums[:, k, j:j + 1])
                    e.then_inc(S(a.tag, "exp", i), 1)
                    act.wait_ge(*at(a.tag, "turned", i))
                    if i >= 2:
                        act.wait_ge(*at(a.tag, "values", i - 2))
                    for m in range(2):
                        c = act.activation(flat(a.probsT[k][:, m]), bank[4 + m][:, :], ACT.Copy)
                    c.then_inc(S(a.tag, "probsT", i), 1)

            def head_norm(tag):
                act.wait_ge(*at(tag, "head variance"))
                act.activation(headsq[:, :], headsq[:, :], ACT.Sqrt).then_inc(S(tag, "head deviation"), 1)

            def decayed_out(d):
                act.wait_ge(*at(d.tag, "level", LEVELS + 1))
                done = 0
                for b, heads in enumerate(cross_banks(d)):
                    n = len(heads)
                    c = act.activation(flat(d.cross[:, done:done + n, :]), bank[b][:, 0:n * P], ACT.Copy)
                    done += n
                c.then_inc(S(d.tag, "cross"), 1)
                act.wait_ge(*at(d.tag, "products"))
                for n, (t, h0, m) in enumerate(out_pieces(d)):
                    c = act.activation(mix[:, t, h0 * P:(h0 + m) * P], bank[n][:, 0:m * P], ACT.Copy)
                c.then_inc(S(d.tag, "out"), 1)

            def mlp_round(R, L, g, rounds, step, nt, n):
                def silu(p):
                    act.wait_ge(R.used, g - R.first + R.credit + 2 * p + 2 + RING * rounds)
                    for t in range(nt):
                        act.activation(gated[:, p, t, :], bank[2 * p + t][:, 0:HID], ACT.Silu).then_inc(L.gated, 1)

                def hidden_hi(p):
                    for t in range(nt):
                        act.wait_ge(L.turned, nt * (step + p) + t + 1)
                        act.activation(hid_hi[:, p, :, t * P:(t + 1) * P],
                                       bank[2 * p + t][:, 0:HID].rearrange("p (k s) -> p k s", k=2), ACT.Copy)\
                           .then_inc(L.hid_hi, 1)

                split_hi(R, g, rounds)
                split_hi(R, g + 1, rounds)
                split_hi(R, g + 2, rounds)
                silu(0)
                if n == 2:
                    split_hi(R, g + 3, rounds)
                hidden_hi(0)
                if n == 2:
                    split_hi(R, g + 4, rounds)
                    silu(1)
                    split_hi(R, g + 5, rounds)
                    hidden_hi(1)

            act.wait_ge(*at("lam sums"))
            act.activation(neg_lam[:, 0:2], neg_lam[:, 0:2], ACT.Exp).then_inc(S("lam exp"), 1)
            act.wait_ge(*at("lb shifted"))
            act.activation(lb[:, 1, :], lb[:, 1, :], ACT.Exp).then_inc(S("lb exp"), 1)
            act.wait_ge(*at("rel product"))
            act.activation(rel_places()[2], bank[0][0:8, :], ACT.Copy).then_inc(S("rel rows"), 1)

            if have("memory"):
                S.stage("memory")
                norm("norm_kv_a", mix, proj, (loaded["mem"], 16))
                turn_split("norm_kv_a", 0)
                product("kv_a", kv[:, 0])
                norm("norm_kv_b", mix, proj, at("norm_kv_a", "turned", 3))
                turn_split("norm_kv_b", G["kv_b"])
                product("kv_b", kv[:, 1])
            if have("a_in"):
                S.stage("a_in")
                norm("norm_a", x, mix, (loaded["x"], 16), at("norm_kv_b", "h"))
                turn_split("norm_a", G["a_in"])
                product("a_in", proj)
            if have("diff"):
                S.stage("diff")
                pairs(diff)
                head_norm("diff")
            if have("a_mem"):
                S.stage("a_mem")
                pairs(a_mem)
            if have("a_out"):
                S.stage("a_out")
                turn_split("mix_a", G["a_out"])
                product("a_out", None)
            if have("dense"):
                S.stage("dense")
                norm("norm_dense", x, mix, at("a_out", "added", 1))
                turn_split("norm_dense", G["dense"])
                repeat(act, DENSE_STEPS // 2,
                       lambda i: mlp_round(ring, dense_loop, G["dense"], i, 2 * i, TILES, 2))
                last = DENSE_STEPS - 1
                mlp_round(ring, dense_loop, G["dense"] + 3 * last, 0, last, TILES, 1)
            if have("b_in"):
                S.stage("b_in")
                norm("norm_b", x, mix, at("dense", "added"))
                turn_split("norm_b", G["b_in"])
                product("b_in", proj)
            if have("hgrn"):
                S.stage("hgrn")
                turn_copy("hgrn_q", flat(hgrn.q), HG_W * TILES)
                for n in range(HG_W * TILES // 512):
                    act.wait_ge(*at("hgrn_f", "turned", n))
                    act.activation(flat(hgrn.after)[:, n * 512:(n + 1) * 512], bank[6 + n % 2][:, :], ACT.Sigmoid)
                    act.activation(flat(hgrn.k)[:, n * 512:(n + 1) * 512], bank[6 + n % 2][:, :], ACT.Sigmoid, scale=-1.0)\
                       .then_inc(S("hgrn_f", "taken", n), 1)
                g_cols = proj[:, :, 3 * HG_W:4 * HG_W]
                act.activation(g_cols, g_cols, ACT.Silu).then_inc(S("hgrn", "silu"), 1)
                decayed_out(hgrn)
                head_norm("hgrn")
            if have("b_mem"):
                S.stage("b_mem")
                pairs(b_mem)
            if have("b_out"):
                S.stage("b_out")
                turn_split("mix_b", G["b_out"])
                product("b_out", None)
            if have("route"):
                S.stage("route")
                norm("norm_moe", x, mix, at("b_out", "added", 1))
                turn_split("norm_moe", G["experts"])
                act.activation(flat(moe_h_hi[:, :, :]), flat(mix[:, :, :]), ACT.Copy).then_inc(S("route", "h_hi"), 1)
                act.wait_ge(*at("route", "gap"))
                act.activation(ratio[:, 1, :], ratio[:, 0, :], ACT.Exp).then_inc(S("route", "exp"), 1)
            if have("experts"):
                S.stage("experts")

                def experts(R, L):
                    def silu(p, step, units, rounds):
                        act.wait_ge(R.used, units - R.first + R.credit + RING * rounds)
                        act.activation(gated[:, p, 0, :], bank[2 * p][:, 0:HID], ACT.Silu).then_inc(L.gated, 1)

                    def hidden_hi(p, step):
                        act.wait_ge(L.turned, step + 1)
                        act.activation(hid_hi[:, p, :, 0:P], bank[2 * p][:, 0:HID].rearrange("p (k s) -> p k s", k=2),
                                       ACT.Copy).then_inc(L.hid_hi, 1)

                    def one_round(g, rounds, step, after_two):
                        split_hi(R, g, rounds)
                        if after_two:
                            silu(0, step, g - 1, rounds)
                        split_hi(R, g + 1, rounds)
                        if not after_two:
                            silu(0, step, g, rounds)
                        split_hi(R, g + 2, rounds)
                        hidden_hi(0, step)
                        split_hi(R, g + 3, rounds)
                        silu(1, step + 1, g + 2, rounds)
                        split_hi(R, g + 4, rounds)
                        split_hi(R, g + 5, rounds)
                        hidden_hi(1, step + 1)

                    def slots(n):
                        act.wait_ge(L.gathered, 2 * n - 1)
                        for k in range(2):
                            c = act.activation(flat(slot_hi[:, 4 * k:4 * k + 4, :]), bank[6 + k][:, :], ACT.Copy)
                        c.then_inc(L.slots_hi, 1)

                    def stage_pick(n):
                        act.wait_ge(L.pick_turned, n)
                        act.activation(staged[:, :], bank[1][:, 0:TILES * P], ACT.Copy).then_inc(L.staged, 1)

                    def first():
                        slots(1)
                        stage_pick(1)
                        split_hi(R, G["experts"], 0)
                        split_hi(R, G["experts"] + 1, 0)
                        one_round(FIRST_ROUND, 0, 0, False)

                    def tail(e, last):
                        r, step = PER_EXPERT * e, EXPERT_STEPS * e + EXPERT_STEPS - 2
                        split_hi(R, TAIL, r)
                        silu(0, step, TAIL - 1, r)
                        split_hi(R, TAIL + 1, r)
                        split_hi(R, TAIL + 2, r)
                        hidden_hi(0, step)
                        if not last:
                            slots(e + 2)
                        silu(1, step + 1, TAIL + 2, r)
                        split_hi(R, TAIL + 3, r)
                        if last:
                            hidden_hi(1, step + 1)
                        else:
                            split_hi(R, TAIL + 4, r)
                            hidden_hi(1, step + 1)
                            act.wait_ge(L.pickT, e + 1)
                            stage_pick(e + 2)
                            split_hi(R, TAIL + 5, r)
                        act.wait_ge(R.used, TAIL + (4 if last else 5) - R.first + R.credit + RING * r)
                        for k in range(2):
                            c = act.activation(y_hi[:, k * 512:(k + 1) * 512], bank[4 + k][:, :], ACT.Copy)
                        c.then_inc(L.y_hi, 1)

                    expert_order(act, first,
                                 lambda e, i: one_round(NEXT_ROUND, PER_EXPERT * e + i, EXPERT_STEPS * e + 2 * i + 2, True),
                                 tail,
                                 lambda e: one_round(NEXT_FIRST, PER_EXPERT * e, EXPERT_STEPS * e + EXPERT_STEPS, False))

                experts(ring, expert_loop)
                act.wait_ge(*at("overflow"))
                more = act.value_load(flag[0:1, 0:1], min_val=0, max_val=1)
                with act.If(more > 0):
                    act.wait_ge(ring.used, G["ada"])
                    act.sem_inc(more_ring.hi, RING)
                    experts(more_ring, more_loop)
                    act.wait_ge(more_ring.used, RING + G["ada"] - G["experts"])
            if have("ada"):
                S.stage("ada")
                norm("norm_final", x, mix, at("experts done"))
                act.wait_ge(loaded["c"], 32)
                act.activation(c_col[:, :], c_col[:, :], ACT.Silu).then_inc(S(), 1)
                act.wait_ge(*S.last())
                act.activation(hT_hi[:, :, 0:P], c_col[:, :].unsqueeze(2).broadcast_to([P, KC, P]), ACT.Copy)\
                   .then_inc(S("ada", "c_hi"), 1)
                repeat(act, 4, lambda i: [split_hi(ring, G["ada"] + u, i) for u in range(RING)])
            if have("in_2"):
                S.stage("in_2")
                norm("norm_2", x, mix, at("norm_final", "h"))
                turn_split("norm_2", G["in_2"])
                product("in_2", proj2)
                split_hi(ring, G["in_2"] + 12, 0, KC * GLA_RANK)
                act.wait_ge(ring.used, G["in_2"] + 13)
                for t in range(TILES):
                    c = act.activation(proj2[:, t, 1536:1552], bank[2 * ((B["in_2"] + 6) % 3) + t][:, 0:GLA_RANK], ACT.Copy)
                c.then_inc(block_out, 1)
            if have("gla"):
                S.stage("gla")
                turn_copy("gla_q", flat(gla.q), 512, PAIR_SCALE)
                turn_copy("gla_k", flat(gla.k), 512)
                act.wait_ge(*at("gla", "rank turned"))
                act.activation(gla_rankT(), bank[6][0:GLA_RANK, 0:SEQ], ACT.Copy).then_inc(S("gla", "rankT"), 1)
                act.wait_ge(*at("gla", "gate"))
                act.wait_ge(loaded["bgate"], 16)
                f = gla.after
                for grp in range(2):
                    c = act.activation(f[:, grp, :], bank[0][:, grp * SEQ:(grp + 1) * SEQ], ACT.Sigmoid, bias=b_gate[:, grp:grp + 1])
                c.then_inc(S(), 1)
                act.wait_ge(*S.last())
                act.activation(flat(f), flat(f), ACT.Ln).then_inc(S(), 1)
                act.wait_ge(*S.last())
                act.activation(flat(f), flat(f), ACT.Exp, scale=1.0 / GLA_TAU).then_inc(S("gla", "f"), 1)
                gr_cols = proj2[:, :, 1024:1536]
                act.activation(gr_cols, gr_cols, ACT.Silu).then_inc(S("gla", "silu"), 1)
                decayed_out(gla)
                head_norm("gla")
            if have("moba"):
                S.stage("moba")
                pairs(moba)
            if have("out_2"):
                S.stage("out_2")
                turn_split("mix_2", G["out_2"])
                product("out_2", None)
            if have("ff_2"):
                S.stage("ff_2")
                norm("norm_ff", x, mix, at("out_2", "added", 1))
                turn_split("norm_ff", G["ff_2"])

                def hidden_hi(p, step):
                    act.wait_ge(ff_loop.turned, step + 1)
                    act.activation(flat(hid2_hi[:, p]).rearrange("p (k t s) -> p t k s", k=2, t=TILES),
                                   bank[p][:, :].rearrange("p (t k s) -> p t k s", k=2, t=TILES), ACT.Copy)\
                       .then_inc(ff_loop.hid_hi, 1)

                def ff_round(i):
                    g = G["ff_2"]
                    split_hi(ring, g, i)
                    split_hi(ring, g + 1, i)
                    split_hi(ring, g + 2, i)
                    hidden_hi(0, 3 * i)
                    split_hi(ring, g + 3, i)
                    split_hi(ring, g + 4, i)
                    hidden_hi(1, 3 * i + 1)
                    split_hi(ring, g + 5, i)
                    hidden_hi(2, 3 * i + 2)
                repeat(act, FF2_STEPS // 3, ff_round)
                split_hi(ring, G["ff_2"] + 30, 0)
                split_hi(ring, G["ff_2"] + 31, 0)
                hidden_hi(0, 15)
            if have("final"):
                S.stage("final")
                norm("norm_out", x, mix, at("ff_2", "added"))

        @block.vector
        def _(dve):
            S = Signals("vector", semaphore, numbers)
            S.stage("prep")

            def f32(ap):
                return ap.bitcast(F32)

            def split_lo(R, g, rounds, n=UNIT):
                u = g - R.first
                dve.wait_ge(R.hi, u + 1 + R.credit + RING * rounds)
                before = u - SPLIT + 1 + R.credit
                if before > 0:
                    dve.wait_ge(R.used, before + RING * rounds)
                dve.tensor_tensor(w_lo[:, g % SPLIT, 0:n], raw[:, g % RING, 0:n], f32(w_hi[:, g % SPLIT, 0:n]),
                                  ALU.subtract).then_inc(R.lo, 1)

            def gain_row(n, width=D):
                dve.wait_ge(gain_in[n % 2], 16 * (n // 2 + 1))
                return gain[:, n % 2, 0:width]

            def norm(tag, src, dst, n, ada_at=None):
                dve.wait_ge(*at(tag, "squares"))
                dve.tensor_scalar(sumsq[:, :], sumsq[:, :], 1.0 / D, EPS, ALU.mult, ALU.add).then_inc(S(tag, "variance"), 1)
                g = gain_row(n)
                if ada_at is not None:
                    scale = ada[:, ada_at + 1, :]
                    dve.scalar_tensor_tensor(out=scale, in0=scale, scalar=1.0, in1=g, op0=ALU.add, op1=ALU.mult)\
                       .then_inc(S("gain used", n), 1)
                    g = scale
                dve.wait_ge(*at(tag, "deviation"))
                dve.reciprocal(rstd[:, :], rstd[:, :]).then_inc(S(), 1)
                dve.wait_ge(*S.last())
                for t in range(TILES):
                    h = dve.scalar_tensor_tensor(out=dst[:, t, 0:D], in0=src[:, t, :], scalar=rstd[:, t:t + 1], in1=g,
                                                 op0=ALU.mult, op1=ALU.mult)
                if ada_at is None:
                    h.then_inc(S(tag, "h"), 1)
                    S.also("gain used", n)
                    return
                h.then_inc(S(), 1)
                dve.wait_ge(*S.last())
                for t in range(TILES):
                    h = dve.tensor_tensor(dst[:, t, 0:D], dst[:, t, 0:D], ada[:, ada_at, :], ALU.add)
                h.then_inc(S(tag, "h"), 1)

            def turn_split(tag):
                for n in range(4):
                    dve.wait_ge(*at(tag, "hi", n))
                    dve.tensor_tensor(flat(hT_lo[:, 2 * n:2 * n + 2, :]), bank[6 + n % 2][:, :],
                                      f32(flat(hT_hi[:, 2 * n:2 * n + 2, :])), ALU.subtract).then_inc(S(tag, "taken", n), 1)

            def product(name, added, gate=None):
                def add(j):
                    c, n = COLS[name][j]
                    dve.wait_ge(ring.used, G[name] + 2 * j + 2)
                    for t in range(TILES):
                        y = bank[2 * ((B[name] + j) % 3) + t][:, 0:n]
                        if gate is not None:
                            dve.tensor_tensor(mix[:, t, c:c + n], y, gate[:, c:c + n], ALU.mult).then_inc(S(), 1)
                            dve.wait_ge(*S.last())
                            y = mix[:, t, c:c + n]
                        o = dve.tensor_tensor(x[:, t, c:c + n], x[:, t, c:c + n], y, ALU.add)
                    o.then_inc(block_out, 1)
                    numbers[(name, "added", j)] = ("block_out", B[name] + j + 1)

                for j, (c, n) in enumerate(COLS[name]):
                    for h in range(2):
                        split_lo(ring, G[name] + 2 * j + h, 0, 4 * n)
                    if added and j > 0:
                        add(j - 1)
                if added:
                    add(len(COLS[name]) - 1)

            def pairs(a, bias=None, scale=PAIR_SCALE):
                def scores(i):
                    k = i % 2
                    if bias == "distance":
                        slope = 2.0 ** (-8.0 * (i + 1) / DA_HEADS)
                        dve.scalar_tensor_tensor(out=flat(diff_bias), in0=con[:, C_DIST:C_DIST + 2 * SEQ], scalar=-slope,
                                                 in1=con[:, C_MASK:C_MASK + 2 * SEQ], op0=ALU.mult, op1=ALU.add).then_inc(S(), 1)
                        dve.wait_ge(*S.last())
                    if bias == "rows":
                        dve.wait_ge(loaded[f"bias{k}"], 32 * (i // 2 + 1))
                    if i >= 2:
                        dve.wait_ge(*at(a.tag, "turned", i - 2))
                    dve.wait_ge(*at(a.tag, "scores", i))
                    for m in range(2):
                        s_in, s_out = bank[2 * k + m][:, :], flat(a.probs[k][:, m])
                        if bias is None:
                            o = dve.tensor_scalar(s_out, s_in, scale, None, ALU.mult)
                        elif bias == "distance":
                            o = dve.scalar_tensor_tensor(out=s_out, in0=s_in, scalar=scale, in1=flat(diff_bias),
                                                         op0=ALU.mult, op1=ALU.add)
                        else:
                            o = dve.scalar_tensor_tensor(out=a.probs[k][:, m], in0=s_in.rearrange("p (t s) -> p t s", t=TILES),
                                                         scalar=scale, in1=bias_place(i)[:, m, :, ::-1],
                                                         op0=ALU.mult, op1=ALU.add)
                    o.then_inc(S(a.tag, "biased", i), 1)
                    dve.wait_ge(*S.last())
                    dve.tensor_reduce(top[:, k, :], a.probs[k].rearrange("p m t s -> p (m t) s"), AX.X, ALU.max).then_inc(S(), 1)
                    dve.wait_ge(*S.last())
                    dve.tensor_scalar(top[:, k, :], top[:, k, :], -1.0, None, ALU.mult).then_inc(S(a.tag, "max", i), 1)

                def outputs(i):
                    k = i % 2
                    dve.wait_ge(*at(a.tag, "exp", i))
                    dve.reciprocal(sums[:, k, :], sums[:, k, :]).then_inc(S(), 1)
                    dve.wait_ge(*S.last())
                    if a.tag == "diff":
                        dve.tensor_scalar(sums[:, k, 2:4], sums[:, k, 2:4], neg_lam[:, 2:3], None, ALU.mult).then_inc(S(), 1)
                        dve.wait_ge(*S.last())
                    dve.wait_ge(*at(a.tag, "values", i))
                    o = bank[6 + k][:, 0:4 * a.dv]
                    r = sums[:, k, :]
                    if a.tag == "diff":
                        dve.tensor_tensor(diff_sum, o.rearrange("p (j d) -> p j d", j=4),
                                          r.unsqueeze(2).broadcast_to([P, 4, a.dv]), ALU.mult).then_inc(S(), 1)
                        dve.wait_ge(*S.last())
                        dve.tensor_tensor(mix[:, :, i * P:(i + 1) * P], diff_sum[:, 0:2, :], diff_sum[:, 2:4, :],
                                          ALU.add).then_inc(S(a.tag, "out", i), 1)
                    else:
                        c = a.first + i * P
                        dve.tensor_tensor(mix[:, :, c:c + P].rearrange("p t (m d) -> p m t d", m=2),
                                          o.rearrange("p (m t d) -> p m t d", m=2, t=TILES),
                                          r.rearrange("p (m t) -> p m t", m=2).unsqueeze(3).broadcast_to([P, 2, TILES, a.dv]),
                                          ALU.mult).then_inc(S(a.tag, "out", i), 1)

                for i in range(a.n):
                    scores(i)
                    if i > 0:
                        outputs(i - 1)
                outputs(a.n - 1)

            def head_norm(tag, heads, scratch, n, ready, factor=1.0, gate=None):
                w = heads * P
                m = mix[:, :, 0:w]
                m4 = m.rearrange("p t (h d) -> p t h d", h=heads)
                sq = headsq[:, 0:TILES * heads]
                dve.wait_ge(*ready)
                dve.tensor_tensor(scratch, m, m, ALU.mult).then_inc(S(), 1)
                dve.wait_ge(*S.last())
                dve.tensor_reduce(sq, scratch.rearrange("p t (h d) -> p (t h) d", h=heads), AX.X, ALU.add).then_inc(S(), 1)
                dve.wait_ge(*S.last())
                if TILES * heads < TILES * HG_HEADS:
                    dve.memset(headsq[:, TILES * heads:], 1.0)
                dve.tensor_scalar(sq, sq, 1.0 / P, EPS, ALU.mult, ALU.add).then_inc(S(tag, "head variance"), 1)
                dve.wait_ge(*at(tag, "head deviation"))
                dve.reciprocal(sq, sq).then_inc(S(), 1)
                dve.wait_ge(*S.last())
                if factor != 1.0:
                    dve.tensor_scalar(sq, sq, factor, None, ALU.mult).then_inc(S(), 1)
                    dve.wait_ge(*S.last())
                dve.tensor_tensor(m4, m4, sq.rearrange("p (t h) -> p t h", t=TILES).unsqueeze(3).broadcast_to([P, TILES, heads, P]),
                                  ALU.mult).then_inc(S(), 1)
                dve.wait_ge(*S.last())
                if tag == "gla":
                    g = gain_row(n, w)
                    o = dve.tensor_tensor(m, m, g.unsqueeze(1).broadcast_to([P, TILES, w]), ALU.mult)
                else:
                    g = gain_row(n, P)
                    o = dve.tensor_tensor(m4, m4, g.unsqueeze(1).unsqueeze(1).broadcast_to([P, TILES, heads, P]), ALU.mult)
                o.then_inc(S(tag, "head normed"), 1)
                S.also("gain used", n)
                if gate is not None:
                    dve.wait_ge(*S.last())
                    dve.wait_ge(*at(tag, "silu"))
                    dve.tensor_tensor(m, m, gate, ALU.mult).then_inc(S(), 1)

            def decayed(d):
                tag = d.tag
                dve.memset(d.before, 1.0).then_inc(S(tag, "before", 0), 1)
                for a in d.att:
                    z = dve.memset(a, 0.0)
                z.then_inc(S(), 1)
                dve.wait_ge(*S.last())

                def keep(level):
                    dve.wait_ge(*at(tag, "level", level))
                    mask = con[:, C_TREE + level * P:C_TREE + (level + 1) * P].bitcast(U32)
                    for b, a in enumerate(d.att):
                        o = dve.copy_predicated(a, mask.unsqueeze(1).broadcast_to([P, 4, P]),
                                                bank[3 * (level % 2) + b][:, :].rearrange("p (a b) -> p a b", b=P))
                    o.then_inc(S(tag, "kept", level), 1)

                for level in range(LEVELS + 2):
                    if level > 0:
                        dve.wait_ge(*at(tag, "level", level - 1))
                    if level == 0:
                        dve.wait_ge(*at(tag + "_q", "taken", d.groups // 2 - 1))
                        dve.tensor_copy(d.dq, d.q).then_inc(S(tag, "queries", 0), 1)
                    elif level <= LEVELS:
                        dve.tensor_tensor(d.dq, d.q, d.after, ALU.mult).then_inc(S(tag, "queries", level), 1)
                    else:
                        dve.tensor_tensor(d.dq[:, :, P:SEQ], d.q[:, :, P:SEQ], d.after[:, :, P:SEQ], ALU.mult)\
                           .then_inc(S(tag, "queries", level), 1)
                    if 1 <= level <= LEVELS:
                        n = 1 << (level - 1)
                        before, after = (z.rearrange("p g (b two n) -> p (g b) two n", two=2, n=n)
                                         for z in (d.before, d.after))
                        nb = d.groups * SEQ // (2 * n)
                        dve.wait_ge(*at(tag, "keys", level))
                        dve.tensor_tensor(before[:, :, 0, :], before[:, :, 0, :],
                                          after[:, :, 1, n - 1:n].broadcast_to([P, nb, n]), ALU.mult)\
                           .then_inc(S(tag, "before", level + 1), 1)
                        dve.wait_ge(*S.last())
                        dve.tensor_tensor(after[:, :, 1, :], after[:, :, 1, :],
                                          after[:, :, 0, n - 1:n].broadcast_to([P, nb, n]), ALU.mult).then_inc(S(), 1)
                        dve.wait_ge(*S.last())
                    if level <= LEVELS:
                        keep(level)
                        dve.wait_ge(*S.last())

            def mlp_round(R, L, g, rounds, step, nt, n):
                def hidden(p):
                    for t in range(nt):
                        dve.wait_ge(L.gated, nt * (step + p) + t + 1)
                        dve.tensor_tensor(hid[:, p, t, :], gated[:, p, t, :], bank[2 * p + t][:, HID:2 * HID], ALU.mult)\
                           .then_inc(L.hidden, 1)

                def hidden_lo(p):
                    for t in range(nt):
                        dve.wait_ge(L.hid_hi, nt * (step + p) + t + 1)
                        dve.tensor_tensor(hid_lo[:, p, :, t * P:(t + 1) * P],
                                          bank[2 * p + t][:, 0:HID].rearrange("p (k s) -> p k s", k=2),
                                          f32(hid_hi[:, p, :, t * P:(t + 1) * P]), ALU.subtract).then_inc(L.hid_lo, 1)

                split_lo(R, g, rounds)
                split_lo(R, g + 1, rounds)
                split_lo(R, g + 2, rounds)
                hidden(0)
                if n == 2:
                    split_lo(R, g + 3, rounds)
                hidden_lo(0)
                if n == 2:
                    split_lo(R, g + 4, rounds)
                    hidden(1)
                    split_lo(R, g + 5, rounds)
                    hidden_lo(1)

            def add_mlp(label, units, gate=None):
                dve.wait_ge(ring.used, units)
                for t in range(TILES):
                    for n in range(2):
                        c = slice(n * 512, (n + 1) * 512)
                        y = bank[4 + 2 * t + n][:, :]
                        if gate is not None:
                            dve.tensor_tensor(mix[:, t, c], y, gate[:, c], ALU.mult).then_inc(S(), 1)
                            dve.wait_ge(*S.last())
                            y = mix[:, t, c]
                        o = dve.tensor_tensor(x[:, t, c], x[:, t, c], y, ALU.add)
                o.then_inc(S(label, "added"), 1)

            dve.wait_ge(loaded["lam"], 64)
            lam4 = lam_place()
            dve.tensor_tensor(lam4[:, 0:2, :], lam4[:, 0:2, :], lam4[:, 2:4, :], ALU.mult).then_inc(S(), 1)
            dve.wait_ge(*S.last())
            dve.tensor_reduce(neg_lam[:, 0:2], lam4[:, 0:2, :], AX.X, ALU.add).then_inc(S("lam sums"), 1)
            dve.wait_ge(loaded["lb"], 16)
            dve.tensor_tensor(lb[:, 1, :], lb[:, 0, :], lb[:, 0, :], ALU.subtract).then_inc(S("lb shifted"), 1)
            dve.wait_ge(*at("lam exp"))
            dve.tensor_tensor(neg_lam[:, 2:3], neg_lam[:, 1:2], neg_lam[:, 0:1], ALU.subtract).then_inc(S(), 1)
            dve.wait_ge(*S.last())
            dve.tensor_scalar(neg_lam[:, 2:3], neg_lam[:, 2:3], -LAM_INIT, None, ALU.add).then_inc(S(), 1)
            dve.wait_ge(*at("lb exp"))
            dve.reciprocal(lb[:, 2, :], lb[:, 1, :]).then_inc(S(), 1)
            dve.wait_ge(*S.last())
            dve.tensor_tensor(lb[:, 1, :], lb[:, 1, :], lb[:, 2, :], ALU.mult).then_inc(S(), 1)
            dve.wait_ge(*S.last())
            dve.tensor_tensor(lb[:, 2, :], lb[:, 1, :], lb[:, 1, :], ALU.subtract).then_inc(S(), 1)
            dve.wait_ge(*S.last())
            dve.tensor_scalar(lb[:, 3, :], lb[:, 2, :], -1.0, 1.0, ALU.mult, ALU.add).then_inc(S(), 1)

            if have("memory"):
                S.stage("memory")
                norm("norm_kv_a", mix, proj, 0)
                turn_split("norm_kv_a")
                product("kv_a", False)
                norm("norm_kv_b", mix, proj, 1)
                turn_split("norm_kv_b")
                product("kv_b", False)
            if have("a_in"):
                S.stage("a_in")
                norm("norm_a", x, mix, 2)
                turn_split("norm_a")
                product("a_in", False)
            if have("diff"):
                S.stage("diff")
                pairs(diff, "distance")
                head_norm("diff", DA_HEADS, head_scratch, 3, S.last(), 1.0 - LAM_INIT)
            if have("a_mem"):
                S.stage("a_mem")
                pairs(a_mem)
            if have("a_out"):
                S.also("mix_a")
                S.stage("a_out")
                turn_split("mix_a")
                product("a_out", True)
            if have("dense"):
                S.stage("dense")
                norm("norm_dense", x, mix, 4)
                turn_split("norm_dense")
                repeat(dve, DENSE_STEPS // 2,
                       lambda i: mlp_round(ring, dense_loop, G["dense"], i, 2 * i, TILES, 2))
                last = DENSE_STEPS - 1
                mlp_round(ring, dense_loop, G["dense"] + 3 * last, 0, last, TILES, 1)
                add_mlp("dense", G["b_in"])
            if have("b_in"):
                S.stage("b_in")
                norm("norm_b", x, mix, 5)
                turn_split("norm_b")
                product("b_in", False)
            if have("hgrn"):
                S.stage("hgrn")
                dve.wait_ge(*at("hgrn_f", "taken", 2))
                low, high = (lb[:, n, :].unsqueeze(2).broadcast_to([P, HG_HEADS, SEQ]) for n in (2, 3))
                dve.tensor_tensor(hgrn.k, hgrn.k, high, ALU.mult)
                dve.tensor_tensor(hgrn.after, hgrn.after, high, ALU.mult).then_inc(S(), 1)
                dve.wait_ge(*S.last())
                dve.tensor_tensor(hgrn.after, hgrn.after, low, ALU.add).then_inc(S(), 1)
                dve.wait_ge(*S.last())
                decayed(hgrn)
                head_norm("hgrn", HG_HEADS, part(work, 0, TILES, HG_W), 6, at("hgrn", "out"),
                          gate=proj[:, :, 3 * HG_W:4 * HG_W])
            if have("b_mem"):
                S.stage("b_mem")
                pairs(b_mem)
            if have("b_out"):
                S.also("mix_b")
                S.stage("b_out")
                turn_split("mix_b")
                product("b_out", True)
            if have("route"):
                S.stage("route")
                norm("norm_moe", x, mix, 7)
                turn_split("norm_moe")
                dve.memset(ones[:, :], 1.0).then_inc(S("ones"), 1)
                dve.wait_ge(*at("route", "h_hi"))
                dve.tensor_tensor(flat(moe_h_lo[:, :, :]), flat(mix[:, :, :]), f32(flat(moe_h_hi[:, :, :])), ALU.subtract)\
                   .then_inc(S("route", "h_lo"), 1)
                dve.wait_ge(*at("route", "logits"))
                dve.tensor_copy(flat(logits[:, :, :]), bank[0][:, 0:TILES * EXPERTS]).then_inc(S(), 1)
                dve.wait_ge(*S.last())
                for t in range(TILES):
                    l = logits[:, t, :]
                    other = l.unsqueeze(1).broadcast_to([P, EXPERTS, EXPERTS])
                    own = l.unsqueeze(2).broadcast_to([P, EXPERTS, EXPERTS])
                    sq = [z[:, t, :].rearrange("p (e f) -> p e f", e=EXPERTS) for z in (pairs_gt, pairs_eq)]
                    dve.max(best[:, t, :], l)
                    dve.tensor_tensor(sq[0], other, own, ALU.is_gt)
                    o = dve.tensor_tensor(sq[1], other, own, ALU.is_equal)
                o.then_inc(S(), 1)
                dve.wait_ge(*S.last())
                dve.tensor_tensor(ratio[:, 0, :], best[:, :, 1], best[:, :, 0], ALU.subtract).then_inc(S("route", "gap"), 1)
                before = con[:, C_BEFORE:C_BEFORE + 64].unsqueeze(1).broadcast_to([P, TILES, 64])
                dve.tensor_tensor(pairs_eq[:, :, :], pairs_eq[:, :, :], before, ALU.mult).then_inc(S(), 1)
                dve.wait_ge(*S.last())
                dve.tensor_tensor(pairs_eq[:, :, :], pairs_eq[:, :, :], pairs_gt[:, :, :], ALU.add).then_inc(S(), 1)
                dve.wait_ge(*S.last())
                dve.tensor_reduce(flat(rank[:, :, :]), pairs_eq[:, :, :].rearrange("p t (e f) -> p (t e) f", e=EXPERTS),
                                  AX.X, ALU.add).then_inc(S(), 1)
                dve.wait_ge(*S.last())
                dve.tensor_scalar(chosen[:, :, :], rank[:, :, :], 1.5, None, ALU.is_lt).then_inc(S("route", "chosen"), 1)
                dve.tensor_scalar(share[:, :, :], rank[:, :, :], 0.0, None, ALU.is_equal)
                dve.tensor_scalar(share2[:, :, :], rank[:, :, :], 1.0, None, ALU.is_equal).then_inc(S(), 1)
                dve.wait_ge(*at("route", "exp"))
                dve.tensor_scalar(ratio[:, 2, :], ratio[:, 1, :], 1.0, None, ALU.add).then_inc(S(), 1)
                dve.wait_ge(*S.last())
                dve.reciprocal(ratio[:, 2, :], ratio[:, 2, :]).then_inc(S(), 1)
                dve.wait_ge(*S.last())
                dve.tensor_tensor(ratio[:, 3, :], ratio[:, 1, :], ratio[:, 2, :], ALU.mult).then_inc(S(), 1)
                dve.wait_ge(*S.last())
                for a, r in ((share, 2), (share2, 3)):
                    o = dve.tensor_tensor(a[:, :, :], a[:, :, :], ratio[:, r, :].unsqueeze(2).broadcast_to([P, TILES, EXPERTS]), ALU.mult)
                o.then_inc(S(), 1)
                dve.wait_ge(*S.last())
                dve.tensor_tensor(share[:, :, :], share[:, :, :], share2[:, :, :], ALU.add).then_inc(S(), 1)
                dve.wait_ge(*S.last())
                dve.tensor_scalar(share2[:, :, :], chosen[:, :, :], -1000.0, 1000.0, ALU.mult, ALU.add).then_inc(S(), 1)
                dve.wait_ge(*S.last())
                dve.wait_ge(*at("route", "order"))
                order = bank[1][:, 0:2 * EXPERTS].rearrange("p (t e) -> p t e", t=TILES)
                dve.tensor_tensor(place[:, 0], order, share2[:, :, :], ALU.add)
                dve.tensor_copy(counts[:, 0:EXPERTS], bank[1][:, 2 * EXPERTS:3 * EXPERTS]).then_inc(S(), 1)
                dve.wait_ge(*S.last())
                dve.tensor_scalar(place[:, 1], place[:, 0], -float(capacity), None, ALU.add).then_inc(S(), 1)
                dve.tensor_reduce(counts[:, EXPERTS:EXPERTS + 1], counts[:, 0:EXPERTS], AX.X, ALU.max).then_inc(S(), 1)
                dve.wait_ge(*S.last())
                if capacity < P:
                    dve.tensor_scalar(share2[:, :, :], place[:, 0], capacity - 0.5, 1000.0, ALU.is_gt, ALU.mult).then_inc(S(), 1)
                    dve.wait_ge(*S.last())
                    dve.tensor_tensor(place[:, 0], place[:, 0], share2[:, :, :], ALU.add).then_inc(S(), 1)
                    dve.wait_ge(*S.last())
                dve.tensor_scalar(flag[:, 0:1], counts[:, EXPERTS:EXPERTS + 1], capacity + 0.5, None, ALU.is_gt)\
                   .then_inc(S("overflow"), 1)
                dve.wait_ge(*S.last())
            if have("experts"):
                S.stage("experts")

                def experts(R, L, again):
                    def hidden(p, step):
                        dve.wait_ge(L.gated, step + 1)
                        dve.tensor_tensor(hid[:, p, 0, :], gated[:, p, 0, :], bank[2 * p][:, HID:2 * HID], ALU.mult)\
                           .then_inc(L.hidden, 1)

                    def hidden_lo(p, step):
                        dve.wait_ge(L.hid_hi, step + 1)
                        dve.tensor_tensor(hid_lo[:, p, :, 0:P], bank[2 * p][:, 0:HID].rearrange("p (k s) -> p k s", k=2),
                                          f32(hid_hi[:, p, :, 0:P]), ALU.subtract).then_inc(L.hid_lo, 1)

                    def pick_tokens(e):
                        for t in range(TILES):
                            o = dve.tensor_scalar(pick[:, t, :], con[:, C_IOTA:C_IOTA + P],
                                                  place[:, again, t, bass.ds(e, 1)], None, ALU.is_equal)
                        o.then_inc(L.picked, 1)

                    def slots(n):
                        dve.wait_ge(L.gathered, 2 * n)
                        for k in range(2):
                            o = dve.tensor_copy(flat(slot_lo[:, 4 * k:4 * k + 4, :]), bank[1 + 2 * k][:, :])
                        o.then_inc(L.slots_lo, 1)

                    def add(e, j):
                        t, c = j // 2, slice(j % 2 * 512, (j % 2 + 1) * 512)
                        if j == 0:
                            dve.wait_ge(L.scattered, e + 1)
                            dve.wait_ge(L.added, e + 1)
                        o = dve.scalar_tensor_tensor(out=x[:, t, c], in0=bank[SCATTER[j]][:, :],
                                                     scalar=share[:, t, bass.ds(e, 1)], in1=x[:, t, c],
                                                     op0=ALU.mult, op1=ALU.add)
                        if j == 3:
                            o.then_inc(L.added, 1)

                    def place_pickT(n):
                        dve.wait_ge(L.staged, n)
                        dve.tensor_copy(flat(pickT[:, :, :]), staged[:, :]).then_inc(L.pickT, 1)

                    def one_round(g, rounds, step, e=None):
                        split_lo(R, g, rounds)
                        hidden(0, step)
                        if e is not None:
                            add(e, 0)
                        split_lo(R, g + 1, rounds)
                        hidden_lo(0, step)
                        split_lo(R, g + 2, rounds)
                        if e is not None:
                            add(e, 1)
                        split_lo(R, g + 3, rounds)
                        hidden(1, step + 1)
                        if e is not None:
                            add(e, 2)
                        split_lo(R, g + 4, rounds)
                        hidden_lo(1, step + 1)
                        split_lo(R, g + 5, rounds)
                        if e is not None:
                            add(e, 3)
                            place_pickT(e + 2)

                    def first():
                        dve.memset(sumsq[:, :], 0.0).then_inc(L.added, 1)
                        pick_tokens(0)
                        slots(1)
                        place_pickT(1)
                        split_lo(R, G["experts"], 0)
                        split_lo(R, G["experts"] + 1, 0)
                        one_round(FIRST_ROUND, 0, 0)

                    def tail(e, last):
                        r, step = PER_EXPERT * e, EXPERT_STEPS * e + EXPERT_STEPS - 2
                        if not last:
                            dve.wait_ge(L.pick_turned, e + 1)
                            pick_tokens(e + 1)
                        split_lo(R, TAIL, r)
                        hidden(0, step)
                        split_lo(R, TAIL + 1, r)
                        hidden_lo(0, step)
                        split_lo(R, TAIL + 2, r)
                        if not last:
                            slots(e + 2)
                        hidden(1, step + 1)
                        split_lo(R, TAIL + 3, r)
                        if last:
                            hidden_lo(1, step + 1)
                        else:
                            split_lo(R, TAIL + 4, r)
                            hidden_lo(1, step + 1)
                            split_lo(R, TAIL + 5, r)
                        dve.wait_ge(L.y_hi, e + 1)
                        for k in range(2):
                            c = slice(k * 512, (k + 1) * 512)
                            o = dve.tensor_tensor(y_lo[:, c], bank[4 + k][:, :], f32(y_hi[:, c]), ALU.subtract)
                        o.then_inc(L.y_lo, 1)
                        if last:
                            for j in range(4):
                                add(e, j)

                    expert_order(dve, first,
                                 lambda e, i: one_round(NEXT_ROUND, PER_EXPERT * e + i, EXPERT_STEPS * e + 2 * i + 2),
                                 tail,
                                 lambda e: one_round(NEXT_FIRST, PER_EXPERT * e, EXPERT_STEPS * e + EXPERT_STEPS, e))

                experts(ring, expert_loop, 0)
                more = dve.value_load(flag[0:1, 0:1], min_val=0, max_val=1)
                with dve.If(more > 0):
                    dve.sem_inc(more_ring.lo, RING)
                    dve.wait_ge(expert_loop.added, EXPERTS + 1)
                    experts(more_ring, more_loop, 1)
                    dve.wait_ge(more_loop.added, EXPERTS + 1)
                dve.wait_ge(expert_loop.added, EXPERTS + 1)
                dve.memset(headsq[:, :], 1.0).then_inc(S("experts done"), 1)
            if have("ada"):
                S.stage("ada")
                norm("norm_final", x, x, 8)
                dve.wait_ge(*at("ada", "c_hi"))
                dve.tensor_tensor(hT_lo[:, :, 0:P], c_col[:, :].unsqueeze(2).broadcast_to([P, KC, P]),
                                  f32(hT_hi[:, :, 0:P]), ALU.subtract).then_inc(S("ada", "c_lo"), 1)
                dve.wait_ge(loaded["b_ada"], 16)
                ada_flat = ada[:, :, :].rearrange("p a d -> p (a d)")

                def ada_blocks(i):
                    def leave(j):
                        dve.wait_ge(ring.used, G["ada"] + 2 * j + 2 + RING * i)
                        c = ada_flat[:, bass.ds(i * 1536 + j * 512, 512)]
                        dve.tensor_tensor(c, c, bank[2 * ((B["ada"] + j) % 3)][:, :], ALU.add).then_inc(block_out, 1)
                    for u in range(4):
                        split_lo(ring, G["ada"] + u, i)
                    leave(0)
                    for u in range(4, 6):
                        split_lo(ring, G["ada"] + u, i)
                    leave(1)
                    leave(2)
                repeat(dve, 4, ada_blocks)
                dve.wait_ge(block_out, B["ada"] + 12)
            if have("in_2"):
                S.stage("in_2")
                norm("norm_2", x, mix, 9, 0)
                turn_split("norm_2")
                product("in_2", False)
                split_lo(ring, G["in_2"] + 12, 0, KC * GLA_RANK)
            if have("gla"):
                S.stage("gla")
                dve.wait_ge(*at("gla", "f"))
                decayed(gla)
                head_norm("gla", GLA_HEADS, part(work2, 0, TILES, GLA_W), 10, at("gla", "out"),
                          gate=proj2[:, :, 1024:1536])
            if have("moba"):
                S.stage("moba")
                pairs(moba, "rows")
            if have("out_2"):
                S.also("mix_2")
                S.stage("out_2")
                turn_split("mix_2")
                product("out_2", True, ada[:, 2, :])
            if have("ff_2"):
                S.stage("ff_2")
                norm("norm_ff", x, mix, 11, 3)
                turn_split("norm_ff")

                def hidden(p, step, unit, rounds):
                    dve.wait_ge(ring.used, unit + 1 + RING * rounds)
                    h = flat(hid2[:, p])
                    dve.tensor_scalar(h, bank[p][:, :], 0.0, None, ALU.max).then_inc(ff_loop.gated, 1)
                    dve.wait_ge(ff_loop.gated, step + 1)
                    dve.tensor_tensor(h, h, bank[p][:, :], ALU.mult).then_inc(ff_loop.hidden, 1)

                def hidden_lo(p, step):
                    hi, lo = (flat(z[:, p]).rearrange("p (k t s) -> p t k s", k=2, t=TILES) for z in (hid2_hi, hid2_lo))
                    dve.wait_ge(ff_loop.hid_hi, step + 1)
                    dve.tensor_tensor(lo, bank[p][:, :].rearrange("p (t k s) -> p t k s", k=2, t=TILES), f32(hi),
                                      ALU.subtract).then_inc(ff_loop.hid_lo, 1)

                def ff_round(i):
                    g = G["ff_2"]
                    split_lo(ring, g, i)
                    split_lo(ring, g + 1, i)
                    hidden(0, 3 * i, g, i)
                    split_lo(ring, g + 2, i)
                    hidden_lo(0, 3 * i)
                    hidden(1, 3 * i + 1, g + 1, i)
                    split_lo(ring, g + 3, i)
                    split_lo(ring, g + 4, i)
                    hidden_lo(1, 3 * i + 1)
                    hidden(2, 3 * i + 2, g + 3, i)
                    split_lo(ring, g + 5, i)
                    hidden_lo(2, 3 * i + 2)
                repeat(dve, FF2_STEPS // 3, ff_round)
                g = G["ff_2"] + 30
                split_lo(ring, g, 0)
                split_lo(ring, g + 1, 0)
                hidden(0, 15, g, 0)
                hidden_lo(0, 15)
                add_mlp("ff_2", g + 2, ada[:, 5, :])
            if have("final"):
                S.stage("final")
                norm("norm_out", x, x, 12)
                S.also("result")
            else:
                dve.memset(headsq[:, :], 1.0).then_inc(S("result"), 1)

        @block.tensor
        def _(pe):
            S = Signals("tensor", semaphore, numbers)
            S.stage("prep")

            def consume(R, g, rounds, products):
                u = g - R.first
                s = g % SPLIT
                pe.wait_ge(R.hi, u + 1 + R.credit + RING * rounds)
                for out_, terms, start, stop in products:
                    for n, (hi, lo, c, w) in enumerate(terms):
                        pe.matmul(out_, hi, w_hi[:, s, c:c + w], start=(start and n == 0), stop=False, skip_group_check=True)
                        mm = pe.matmul(out_, lo, w_hi[:, s, c:c + w], start=False, stop=False, skip_group_check=True)
                mm.then_inc(R.hi_used, 1)
                pe.wait_ge(R.lo, u + 1 + R.credit + RING * rounds)
                for out_, terms, start, stop in products:
                    for n, (hi, lo, c, w) in enumerate(terms):
                        mm = pe.matmul(out_, hi, w_lo[:, s, c:c + w], start=False, stop=(stop and n == len(terms) - 1),
                                       skip_group_check=True)
                mm.then_inc(R.used, 1)

            def columns_terms(h, t, n):
                return [(hT_hi[:, 4 * h + k, t * P:(t + 1) * P], hT_lo[:, 4 * h + k, t * P:(t + 1) * P], k * n, n)
                        for k in range(4)]

            def turn(tag, blocks, ready, rows=P):
                pe.wait_ge(*ready)
                for n in range(0, len(blocks), 4):
                    j = n // 4
                    if j >= 2:
                        pe.wait_ge(*at(tag, "taken", j - 2))
                    for c, b in enumerate(blocks[n:n + 4]):
                        mm = pe.transpose(bank[6 + j % 2][:, c * P:(c + 1) * P], b, ident)
                    mm.then_inc(S(tag, "turned", j), 1)

            def turn_split(tag, src, ready):
                turn(tag, [src[:, t, k * P:(k + 1) * P] for k, t in NORM_BLOCKS], ready)
                for j in (2, 3):
                    pe.wait_ge(*at(tag, "taken", j))

            def product(name):
                for j, (c, n) in enumerate(COLS[name]):
                    b = B[name] + j
                    if b >= 3:
                        pe.wait_ge(block_out, b - 2)
                    for h in range(2):
                        consume(ring, G[name] + 2 * j + h, 0,
                                [(bank[2 * (b % 3) + t][:, 0:n], columns_terms(h, t, n), h == 0, h == 1) for t in range(TILES)])

            def pairs(a, ready):
                turn(a.tag + "_q", a.q_cols, ready)
                last = (len(a.q_cols) - 1) // 4
                for j in range(max(0, last - 1), last + 1):
                    pe.wait_ge(*at(a.tag + "_q", "taken", j))
                turn(a.tag + "_k", a.k_cols, ready)
                pe.wait_ge(*at(a.tag + "_k", "taken", last))

                def scores(i):
                    k = i % 2
                    if i >= 2:
                        pe.wait_ge(*at(a.tag, "biased", i - 2))
                    for t in range(TILES):
                        for m in range(2):
                            r = slice(64 * m, 64 * m + 64)
                            mm = pe.matmul(bank[2 * k + m][:, t * SEQ:(t + 1) * SEQ], a.qT[r, i, t * P:(t + 1) * P],
                                           a.kT[r, i, :], start=True, stop=True)
                    mm.then_inc(S(a.tag, "scores", i), 1)

                scores(0)
                for i in range(a.n):
                    k = i % 2
                    if i + 1 < a.n:
                        scores(i + 1)
                    pe.wait_ge(*at(a.tag, "exp", i))
                    if i > 0:
                        pe.wait_ge(*at(a.tag, "probsT", i - 1))
                    for m in range(2):
                        for s in range(TILES):
                            for t in range(TILES):
                                mm = pe.transpose(bank[4 + m][:, s * SEQ + t * P:s * SEQ + (t + 1) * P],
                                                  a.probs[k][:, m, t, s * P:(s + 1) * P], ident)
                    mm.then_inc(S(a.tag, "turned", i), 1)
                    pe.wait_ge(*at(a.tag, "probsT", i))
                    if i >= 2:
                        pe.wait_ge(*at(a.tag, "out", i - 2))
                    for m in range(2):
                        for t in range(TILES):
                            j = 2 * m + t
                            for s in range(TILES):
                                mm = pe.matmul(bank[6 + k][:, j * a.dv:(j + 1) * a.dv],
                                               a.probsT[k][:, m, s, t * P:(t + 1) * P], a.v(i, m, s),
                                               start=(s == 0), stop=(s == TILES - 1))
                    mm.then_inc(S(a.tag, "values", i), 1)

            def decayed(d):
                tag = d.tag
                for level in range(LEVELS + 2):
                    pe.wait_ge(*at(tag, "queries", level))
                    pe.wait_ge(*at(tag, "keys", level))
                    if level >= 2:
                        pe.wait_ge(*at(tag, "kept", level - 2))
                    if level <= LEVELS:
                        for n, (h, t) in enumerate(d.outs):
                            r, c = d.rows(h), slice(t * P, (t + 1) * P)
                            mm = pe.matmul(bank[3 * (level % 2) + n // 4][:, n % 4 * P:(n % 4 + 1) * P],
                                           d.dk[r, h // d.per, c], d.dq[r, h // d.per, c], start=True, stop=True)
                    else:
                        for b, heads in enumerate(cross_banks(d)):
                            for n, h in enumerate(heads):
                                r = d.rows(h)
                                mm = pe.matmul(bank[b][:, n * P:(n + 1) * P], d.dk[r, h // d.per, 0:P],
                                               d.dq[r, h // d.per, P:SEQ], start=True, stop=True)
                    mm.then_inc(S(tag, "level", level), 1)
                pe.wait_ge(*at(tag, "cross"))
                pe.wait_ge(*at(tag, "kept", LEVELS))
                where = {h: n for n, h in enumerate(h for heads in cross_banks(d) for h in heads)}
                for b, (t, h0, n) in enumerate(out_pieces(d)):
                    for j in range(n):
                        h = h0 + j
                        o = bank[b][:, j * P:(j + 1) * P]
                        i = d.outs.index((h, t))
                        mm = pe.matmul(o, d.att[i // 4][:, i % 4, :], d.v(h, t), start=True, stop=(t == 0))
                        if t > 0:
                            mm = pe.matmul(o, d.cross[:, where[h], :], d.v(h, 0), start=False, stop=True)
                mm.then_inc(S(tag, "products"), 1)

            def seed(banks):
                for b in banks:
                    pe.matmul(bank[b][:, :], zero[:, :], con[:, 0:SEQ].bitcast(BF16), start=True, stop=False,
                              skip_group_check=True)

            def mlp_round(R, L, g, rounds, step, nt, n, xs):
                def up(p, h):
                    consume(R, g + 2 * p + h, rounds,
                            [(bank[2 * p + t][:, :], [(xs(0, 4 * h + k, t), xs(1, 4 * h + k, t), k * 512, 512) for k in range(4)],
                              h == 0, h == 1) for t in range(nt)])

                def turn_hidden(p):
                    for t in range(nt):
                        pe.wait_ge(L.hidden, nt * (step + p) + t + 1)
                        for k in range(2):
                            mm = pe.transpose(bank[2 * p + t][:, k * P:(k + 1) * P], hid[:, p, t, k * P:(k + 1) * P], ident)
                        mm.then_inc(L.turned, 1)

                def down(p):
                    pe.wait_ge(L.hid_lo, nt * (step + p) + nt)
                    consume(R, g + 2 * n + p, rounds,
                            [(bank[4 + 2 * t + c][:, :], [(hid_hi[:, p, k, t * P:(t + 1) * P], hid_lo[:, p, k, t * P:(t + 1) * P],
                                                           k * D + c * 512, 512) for k in range(2)], False, False)
                             for t in range(nt) for c in range(2)])

                up(0, 0)
                up(0, 1)
                if n == 2:
                    up(1, 0)
                turn_hidden(0)
                if n == 2:
                    up(1, 1)
                down(0)
                if n == 2:
                    turn_hidden(1)
                    down(1)

            def model_xs(half, k, t):
                return (hT_hi, hT_lo)[half][:, k, t * P:(t + 1) * P]

            relx, onehot, _ = rel_places()
            pe.wait_ge(loaded["con"], 16)
            pe.wait_ge(loaded["rel"], 32)
            pe.matmul(bank[0][0:8, :], relx, onehot, start=True, stop=True).then_inc(S("rel product"), 1)
            pe.wait_ge(*at("zero"))

            if have("memory"):
                S.stage("memory")
                pe.wait_ge(*at("rel rows"))
                turn_split("norm_kv_a", proj, at("norm_kv_a", "h"))
                product("kv_a")
                turn_split("norm_kv_b", proj, at("norm_kv_b", "h"))
                product("kv_b")
            if have("a_in"):
                S.stage("a_in")
                turn_split("norm_a", mix, at("norm_a", "h"))
                product("a_in")
            if have("diff"):
                S.stage("diff")
                pairs(diff, (block_out, B["a_in"] + 5))
            if have("a_mem"):
                S.stage("a_mem")
                pairs(a_mem, at("diff", "head normed"))
            if have("a_out"):
                S.stage("a_out")
                turn_split("mix_a", mix, at("mix_a"))
                product("a_out")
            if have("dense"):
                S.stage("dense")
                turn_split("norm_dense", mix, at("norm_dense", "h"))
                seed(range(4, 8))
                repeat(pe, DENSE_STEPS // 2,
                       lambda i: mlp_round(ring, dense_loop, G["dense"], i, 2 * i, TILES, 2, model_xs))
                last = DENSE_STEPS - 1
                mlp_round(ring, dense_loop, G["dense"] + 3 * last, 0, last, TILES, 1, model_xs)
            if have("b_in"):
                S.stage("b_in")
                turn_split("norm_b", mix, at("norm_b", "h"))
                product("b_in")
            if have("hgrn"):
                S.stage("hgrn")
                all_in = (block_out, B["b_in"] + 7)
                turn("hgrn_q", [proj[:, t, h * P:(h + 1) * P] for h in range(HG_HEADS) for t in range(TILES)], all_in)
                for j in (1, 2):
                    pe.wait_ge(*at("hgrn_q", "taken", j))
                turn("hgrn_f", [proj[:, t, HG_W + h * P:HG_W + (h + 1) * P] for h in range(HG_HEADS) for t in range(TILES)], all_in)
                decayed(hgrn)
            if have("b_mem"):
                S.stage("b_mem")
                pairs(b_mem, at("hgrn", "head normed"))
            if have("b_out"):
                S.stage("b_out")
                turn_split("mix_b", mix, at("mix_b"))
                product("b_out")
            if have("route"):
                S.stage("route")
                turn_split("norm_moe", mix, at("norm_moe", "h"))
                pe.wait_ge(loaded["router"], 16)
                for t in range(TILES):
                    for k in range(KC):
                        for half in range(2):
                            mm = pe.matmul(bank[0][:, t * EXPERTS:(t + 1) * EXPERTS], model_xs(half, k, t).bitcast(F32),
                                           w_router[:, k, :], start=(k == 0 and half == 0), stop=(k == KC - 1 and half == 1))
                mm.then_inc(S("route", "logits"), 1)
                pe.wait_ge(*at("route", "chosen"))
                pe.wait_ge(*at("ones"))
                later = con[:, C_LATER:C_LATER + P]
                for c, terms in enumerate((((later, 0),), ((ones[:, :], 0), (later, 1)), ((ones[:, :], 0), (ones[:, :], 1)))):
                    for n, (w, t) in enumerate(terms):
                        mm = pe.matmul(bank[1][:, c * EXPERTS:(c + 1) * EXPERTS], w, chosen[:, t, :],
                                       start=(n == 0), stop=(n == len(terms) - 1))
                mm.then_inc(S("route", "order"), 1)
            if have("experts"):
                S.stage("experts")
                pe.wait_ge(*at("route", "h_lo"))

                def experts(R, L):
                    def up(p, h, g, rounds):
                        consume(R, g, rounds, [(bank[2 * p][:, :], [(slot_hi[:, 4 * h + k, :], slot_lo[:, 4 * h + k, :], k * 512, 512)
                                                                    for k in range(4)], h == 0, h == 1)])

                    def turn_hidden(p, step):
                        pe.wait_ge(L.hidden, step + 1)
                        for k in range(2):
                            mm = pe.transpose(bank[2 * p][:, k * P:(k + 1) * P], hid[:, p, 0, k * P:(k + 1) * P], ident)
                        mm.then_inc(L.turned, 1)

                    def down(p, step, g, rounds):
                        pe.wait_ge(L.hid_lo, step + 1)
                        consume(R, g, rounds,
                                [(bank[4 + c][:, :], [(hid_hi[:, p, k, 0:P], hid_lo[:, p, k, 0:P], k * D + c * 512, 512)
                                                      for k in range(2)], False, False) for c in range(2)])

                    def gather(n):
                        pe.wait_ge(L.picked, n)
                        for half, banks in ((moe_h_hi, (6, 7)), (moe_h_lo, (1, 3))):
                            for k in range(KC):
                                for t in range(TILES):
                                    mm = pe.matmul(bank[banks[k // 4]][:, k % 4 * P:(k % 4 + 1) * P],
                                                   half[:, t, k * P:(k + 1) * P], pick[:, t, :], start=(t == 0), stop=(t == 1))
                            mm.then_inc(L.gathered, 1)

                    def turn_pick(n):
                        pe.wait_ge(L.slots_lo, n)
                        for t in range(TILES):
                            mm = pe.transpose(bank[1][:, t * P:(t + 1) * P], pick[:, t, :].bitcast(F32), ident)
                        mm.then_inc(L.pick_turned, 1)

                    def scatter(e):
                        pe.wait_ge(L.y_lo, e + 1)
                        pe.wait_ge(L.pickT, e + 1)
                        for t in range(TILES):
                            for k in range(2):
                                o = bank[SCATTER[2 * t + k]][:, :]
                                pe.matmul(o, pickT[:, t, :], y_hi[:, k * 512:(k + 1) * 512], start=True, stop=False)
                                mm = pe.matmul(o, pickT[:, t, :], y_lo[:, k * 512:(k + 1) * 512], start=False, stop=True)
                        mm.then_inc(L.scattered, 1)

                    def one_round(g, rounds, step):
                        up(1, 0, g, rounds)
                        turn_hidden(0, step)
                        up(1, 1, g + 1, rounds)
                        down(0, step, g + 2, rounds)
                        up(0, 0, g + 3, rounds)
                        turn_hidden(1, step + 1)
                        up(0, 1, g + 4, rounds)
                        down(1, step + 1, g + 5, rounds)

                    def first():
                        gather(1)
                        turn_pick(1)
                        pe.wait_ge(L.slots_hi, 1)
                        seed((4, 5))
                        up(0, 0, G["experts"], 0)
                        up(0, 1, G["experts"] + 1, 0)
                        one_round(FIRST_ROUND, 0, 0)

                    def tail(e, last):
                        r, step = PER_EXPERT * e, EXPERT_STEPS * e + EXPERT_STEPS - 2
                        up(1, 0, TAIL, r)
                        turn_hidden(0, step)
                        up(1, 1, TAIL + 1, r)
                        if not last:
                            pe.wait_ge(L.added, e + 1)
                            gather(e + 2)
                        down(0, step, TAIL + 2, r)
                        turn_hidden(1, step + 1)
                        if last:
                            down(1, step + 1, TAIL + 3, r)
                            scatter(e)
                            return
                        pe.wait_ge(L.slots_hi, e + 2)
                        pe.wait_ge(L.slots_lo, e + 2)
                        up(0, 0, TAIL + 3, r)
                        turn_pick(e + 2)
                        down(1, step + 1, TAIL + 4, r)
                        up(0, 1, TAIL + 5, r)
                        pe.wait_ge(L.staged, e + 2)
                        scatter(e)
                        seed((4, 5))

                    expert_order(pe, first,
                                 lambda e, i: one_round(NEXT_ROUND, PER_EXPERT * e + i, EXPERT_STEPS * e + 2 * i + 2),
                                 tail,
                                 lambda e: one_round(NEXT_FIRST, PER_EXPERT * e, EXPERT_STEPS * e + EXPERT_STEPS))

                experts(ring, expert_loop)
                pe.wait_ge(*at("overflow"))
                more = pe.value_load(flag[0:1, 0:1], min_val=0, max_val=1)
                with pe.If(more > 0):
                    pe.sem_inc(more_ring.hi_used, RING)
                    pe.sem_inc(more_ring.used, RING)
                    experts(more_ring, more_loop)
            if have("ada"):
                S.stage("ada")
                pe.wait_ge(*at("ada", "c_lo"))

                def ada_blocks(i):
                    for j in range(3):
                        b = B["ada"] + j
                        pe.wait_ge(block_out, b - 2 + 3 * i)
                        for h in range(2):
                            consume(ring, G["ada"] + 2 * j + h, i, [(bank[2 * (b % 3)][:, :], columns_terms(h, 0, 512), h == 0, h == 1)])
                repeat(pe, 4, ada_blocks)
            if have("in_2"):
                S.stage("in_2")
                turn_split("norm_2", mix, at("norm_2", "h"))
                product("in_2")
                b = B["in_2"] + 6
                pe.wait_ge(block_out, b - 2)
                consume(ring, G["in_2"] + 12, 0,
                        [(bank[2 * (b % 3) + t][:, 0:GLA_RANK],
                          [(model_xs(0, k, t), model_xs(1, k, t), k * GLA_RANK, GLA_RANK) for k in range(KC)], True, True)
                         for t in range(TILES)])
            if have("gla"):
                S.stage("gla")
                all_in = (block_out, B["in_2"] + 7)
                turn("gla_q", [proj2[:, t, g * P:(g + 1) * P] for g in range(2) for t in range(TILES)], all_in)
                turn("gla_k", [proj2[:, t, 256 + g * P:256 + (g + 1) * P] for g in range(2) for t in range(TILES)],
                     at("gla_q", "taken", 0))
                pe.wait_ge(*at("gla_k", "taken", 0))
                for t in range(TILES):
                    mm = pe.transpose(bank[6][0:GLA_RANK, t * P:(t + 1) * P], proj2[:, t, 1536:1552], ident)
                mm.then_inc(S("gla", "rank turned"), 1)
                pe.wait_ge(*at("gla", "rankT"))
                pe.wait_ge(loaded["c"], 32)
                for grp in range(2):
                    mm = pe.matmul(bank[0][:, grp * SEQ:(grp + 1) * SEQ], w_gate[:, grp * P:(grp + 1) * P], gla_rankT(),
                                   start=True, stop=True)
                mm.then_inc(S("gla", "gate"), 1)
                decayed(gla)
            if have("moba"):
                S.stage("moba")
                pairs(moba, at("gla", "head normed"))
            if have("out_2"):
                S.stage("out_2")
                turn_split("mix_2", mix, at("mix_2"))
                product("out_2")
            if have("ff_2"):
                S.stage("ff_2")
                turn_split("norm_ff", mix, at("norm_ff", "h"))
                seed(range(4, 8))

                def up(p, g, rounds):
                    consume(ring, g, rounds,
                            [(bank[p][:, t * HID:(t + 1) * HID],
                              [(model_xs(0, k, t), model_xs(1, k, t), k * HID, HID) for k in range(KC)], t == 0, t == 1)
                             for t in range(TILES)])

                def turn_hidden(p, step):
                    pe.wait_ge(ff_loop.hidden, step + 1)
                    for t in range(TILES):
                        for k in range(2):
                            mm = pe.transpose(bank[p][:, t * HID + k * P:t * HID + (k + 1) * P], hid2[:, p, t, k * P:(k + 1) * P], ident)
                    mm.then_inc(ff_loop.turned, 1)

                def down(p, step, g, rounds):
                    pe.wait_ge(ff_loop.hid_lo, step + 1)
                    consume(ring, g, rounds,
                            [(bank[4 + 2 * t + c][:, :], [(hid2_hi[:, p, k, t * P:(t + 1) * P], hid2_lo[:, p, k, t * P:(t + 1) * P],
                                                           k * D + c * 512, 512) for k in range(2)], False, False)
                             for t in range(TILES) for c in range(2)])

                def ff_round(i):
                    g = G["ff_2"]
                    up(0, g, i)
                    up(1, g + 1, i)
                    turn_hidden(0, 3 * i)
                    down(0, 3 * i, g + 2, i)
                    up(2, g + 3, i)
                    turn_hidden(1, 3 * i + 1)
                    down(1, 3 * i + 1, g + 4, i)
                    turn_hidden(2, 3 * i + 2)
                    down(2, 3 * i + 2, g + 5, i)
                repeat(pe, FF2_STEPS // 3, ff_round)
                up(0, G["ff_2"] + 30, 0)
                turn_hidden(0, 15)
                down(0, 15, G["ff_2"] + 31, 0)


_INS = ["x", "mem", "a_norm_mix", "a_w_in", "a_lam_q1", "a_lam_k1", "a_lam_q2", "a_lam_k2", "a_subln", "a_mem_norm",
        "a_w_mem_kv", "a_w_out", "b_norm_mix", "b_w_in", "b_lb_logits", "b_out_norm", "b_mem_norm", "b_w_mem_kv",
        "b_w_out", "dense_norm", "dense_w_gate_up", "dense_w_down", "moe_norm", "moe_router", "moe_w_gate_up",
        "moe_w_down", "final_norm", "c_2", "w_ada_2", "b_ada_2", "g_mix_2", "w_in_2", "w_gla_gate_2", "b_gla_gate_2",
        "g_gla_out_2", "rel_bias_2", "w_out_2", "g_mlp_2", "w_ff1_2", "w_ff2_2", "g_final_2"]


def build(nc, shapes, known=None, stages=STAGES, capacity=CAPACITY):
    A = {n: nc.dram_tensor(f"in_{n}", s, F32, kind="ExternalInput").ap() for n, s in shapes.items()}
    consts = nc.dram_tensor("in_consts", (P, C_ALL), F32, kind="ExternalInput").ap()
    buckets = nc.dram_tensor("in_buckets", (BUCKETS + 1, 2 * SEQ), F32, kind="ExternalInput").ap()
    out = nc.dram_tensor("out", (1, SEQ, D), F32, kind="ExternalOutput").ap()
    numbers = {}
    program(nc, A, consts, buckets, out, {}, numbers, known, stages, capacity)
    return numbers


def kernel(**inputs):
    import concourse.bacc as bacc
    from concourse.bass_utils import run_bass_kernel_spmd

    arrays = {f"in_{n}": np.ascontiguousarray(inputs[n]) for n in _INS}
    shapes = {n: arrays[f"in_{n}"].shape for n in _INS}
    arrays["in_consts"], arrays["in_buckets"] = constants()
    known = build(bacc.Bacc("TRN2", target_bir_lowering=False, num_devices=1), shapes)
    nc = bacc.Bacc("TRN2", target_bir_lowering=False, num_devices=1)
    build(nc, shapes, known)
    r = run_bass_kernel_spmd(nc, [arrays], core_ids=[0])
    return r.results[0]["out"]
```

```python
from contextlib import ExitStack

import numpy as np

import concourse.bass as bass
from concourse import mybir

F32 = mybir.dt.float32
F32R = mybir.dt.float32r
BF16 = mybir.dt.bfloat16
I32 = mybir.dt.int32
U32 = mybir.dt.uint32
ALU = mybir.AluOpType
ACT = mybir.ActivationFunctionType
AX = mybir.AxisListType

P = 128
SEQ = 256
TILES = SEQ // P
D = 1024
KC = D // P
EPS = 1e-6
MASKED = -1e30

DA_HEADS = 6
DA_W = DA_HEADS * P
CHUNK = 64
LAM_INIT = 0.8 - 0.6 * float(np.exp(0.0))
MEM_PAIRS = 2
HG_HEADS = 6
HG_W = HG_HEADS * P
FF_DENSE = 2816
EXPERTS = 8
FF_EXPERT = 3584
CAPACITY = 128
GLA_HEADS = 4
GLA_DK = 64
GLA_W = GLA_HEADS * P
GLA_RANK = 16
GLA_TAU = 16.0
MOBA_PAIRS = 4
BUCKETS = 32
MAX_DIST = 128
FF2 = 4096
N_ADA = 6
ADA_BUFFERS = 3
PAIR_SCALE = 64 ** -0.5

UNIT = 2048
RING = 6
SPLIT = 2
HID = 256
DENSE_STEPS = FF_DENSE // HID
EXPERT_STEPS = FF_EXPERT // HID
FF2_STEPS = FF2 // HID
EXPERT_ROUNDS = EXPERT_STEPS // 2 - 1

C_IDENT, C_LATER, C_IOTA, C_TREE = 0, P, 2 * P, 3 * P
C_DIST = C_TREE + 8 * P
C_MASK = C_DIST + TILES * SEQ
C_BEFORE = C_MASK + TILES * SEQ
C_ALL = C_BEFORE + EXPERTS * EXPERTS

GAINS = ["a_mem_norm", "b_mem_norm", "a_norm_mix", "a_subln", "dense_norm", "b_norm_mix", "b_out_norm",
         "moe_norm", "final_norm", "g_mix_2", "g_gla_out_2", "g_mlp_2", "g_final_2"]

STAGES = ["prep", "memory", "a_in", "diff", "a_mem", "a_out", "dense", "b_in", "hgrn", "b_mem", "b_out",
          "route", "experts", "ada", "in_2", "gla", "moba", "out_2", "ff_2", "final"]


def constants():
    c = np.zeros((P, C_ALL), np.float32)
    a = np.arange(P)
    c[:, C_IDENT:C_IDENT + P] = np.eye(P)
    c[:, C_LATER:C_LATER + P] = a[:, None] < a[None, :]
    c[:, C_IOTA:C_IOTA + P] = a[None, :]
    c[:, C_TREE:C_TREE + P] = np.eye(P)
    for level in range(7):
        s, t = a[:, None] >> level, a[None, :] >> level
        c[:, C_TREE + (level + 1) * P:C_TREE + (level + 2) * P] = (t == s + 1) & (s % 2 == 0)
    for tile in range(TILES):
        q, k = tile * P + a[:, None], np.arange(SEQ)[None, :]
        c[:, C_DIST + tile * SEQ:C_DIST + (tile + 1) * SEQ] = abs(q - k)
        c[:, C_MASK + tile * SEQ:C_MASK + (tile + 1) * SEQ] = np.where(k // CHUNK <= q // CHUNK, 0.0, MASKED)
    e = np.arange(EXPERTS)
    c[:, C_BEFORE:] = (e[None, :] < e[:, None]).astype(np.float32).reshape(1, -1)
    n = np.arange(2 * SEQ) - (SEQ - 1)
    exact = BUCKETS // 2
    ratio = np.maximum(n, 1).astype(np.float32) / exact
    large = exact + (np.log(ratio) / np.float32(np.log(MAX_DIST / exact)) * (BUCKETS - exact)).astype(np.int32)
    bucket = np.where(n < exact, n, np.minimum(large, BUCKETS - 1))
    b = np.zeros((BUCKETS + 1, 2 * SEQ), np.float32)
    b[:BUCKETS] = (np.arange(BUCKETS)[:, None] == bucket[None, :]) & (n >= 0)[None, :] & (n < SEQ)[None, :]
    b[BUCKETS] = np.where((n < 0) | (n >= SEQ), MASKED, 0.0)
    return c, b


class Signals:

    def __init__(self, who, semaphore, numbers):
        self.who, self.semaphore, self.numbers = who, semaphore, numbers
        self.name, self.sem, self.n = None, None, 0

    def stage(self, name):
        self.name = f"{self.who}_{name}"
        self.sem, self.n = self.semaphore(self.name), 0

    def __call__(self, *label):
        self.n += 1
        if label:
            assert label not in self.numbers, label
            self.numbers[label] = (self.name, self.n)
        return self.sem

    def also(self, *label):
        self.numbers[label] = (self.name, self.n)

    def last(self):
        return self.sem, self.n


def program(nc, A, consts, buckets, out, semaphores, numbers, known, stages, capacity):
    ctx = ExitStack()

    def sb(name, shape, dt=F32, stack=ctx):
        return stack.enter_context(nc.sbuf_tensor(name, shape, dt))

    def semaphore(name):
        if name not in semaphores:
            semaphores[name] = ctx.enter_context(nc.semaphore(name))
        return semaphores[name]

    def at(*label):
        if known is None:
            return semaphore("prep_dry"), 1
        name, n = known[label]
        return semaphore(name), n

    with ctx:
        raw = sb("raw", [P, RING, UNIT])
        w_hi = sb("w_hi", [P, SPLIT, UNIT], F32R)
        w_lo = sb("w_lo", [P, SPLIT, UNIT], F32R)
        x = sb("x", [P, TILES, D])
        gain = sb("gain", [P, 2, D])
        over = ExitStack()
        plain = sb("plain", [P, 2, KC * SEQ], F32, over)
        over.close()
        hT_hi = sb("hT_hi", [P, KC, SEQ], F32R)
        hT_lo = sb("hT_lo", [P, KC, SEQ], F32R)
        con = sb("con", [P, C_ALL])
        mix = sb("mix", [P, TILES, D])
        kv = sb("kv", [P, 2, TILES, 512])
        zero = sb("zero", [P, P], BF16)
        ones = sb("ones", [P, P])
        c_col = sb("c_col", [P, KC])
        sumsq = sb("sumsq", [P, TILES])
        rstd = sb("rstd", [P, TILES])
        top = sb("top", [P, 2, 4])
        sums = sb("sums", [P, 4, 4])
        headsq = sb("headsq", [P, TILES * HG_HEADS])
        neg_lam = sb("neg_lam", [P, 4])
        lb = sb("lb", [P, 4, HG_HEADS])
        b_gate = sb("b_gate", [P, 2])
        flag = sb("flag", [P, 2], I32)
        ident = con[:, C_IDENT:C_IDENT + P]
        over = ExitStack()
        proj = sb("proj", [P, TILES, 3584], F32, over)
        work = sb("work", [P, 9728], F32, over)
        over.close()
        hid_hi = sb("hid_hi", [P, 3, 2, SEQ], F32R, over)
        hid_lo = sb("hid_lo", [P, 3, 2, SEQ], F32R, over)
        hid = sb("hid", [P, 3, TILES, HID], F32, over)
        gated = sb("gated", [P, 2, TILES, HID], F32, over)
        moe_h_hi = sb("moe_h_hi", [P, TILES, D], F32R, over)
        moe_h_lo = sb("moe_h_lo", [P, TILES, D], F32R, over)
        slot_hi = sb("slot_hi", [P, KC, P], F32R, over)
        slot_lo = sb("slot_lo", [P, KC, P], F32R, over)
        y_hi = sb("y_hi", [P, D], F32R, over)
        y_lo = sb("y_lo", [P, D], F32R, over)
        pick = sb("pick", [P, TILES, P], F32R, over)
        pickT = sb("pickT", [P, TILES, P], F32R, over)
        staged = sb("staged", [P, TILES * P], F32, over)
        w_router = sb("w_router", [P, KC, EXPERTS], F32, over)
        logits = sb("logits", [P, TILES, EXPERTS], F32, over)
        best = sb("best", [P, TILES, 8], F32, over)
        pairs_gt = sb("pairs_gt", [P, TILES, 64], F32, over)
        pairs_eq = sb("pairs_eq", [P, TILES, 64], F32, over)
        rank = sb("rank", [P, TILES, EXPERTS], F32, over)
        chosen = sb("chosen", [P, TILES, EXPERTS], F32, over)
        share = sb("share", [P, TILES, EXPERTS], F32, over)
        share2 = sb("share2", [P, TILES, EXPERTS], F32, over)
        place = sb("place", [P, 2, TILES, EXPERTS], F32, over)
        ratio = sb("ratio", [P, 4, TILES], F32, over)
        counts = sb("counts", [P, EXPERTS + 1], F32, over)
        over.close()
        ada = sb("ada", [P, N_ADA, D], F32, over)
        proj2 = sb("proj2", [P, TILES, 3088], F32, over)
        work2 = sb("work2", [P, 4096], F32, over)
        w_gate = sb("w_gate", [GLA_RANK, 256], F32, over)
        over.close()
        ada_keep = sb("ada_keep", [P, N_ADA, D], F32, over)
        hid2_hi = sb("hid2_hi", [P, 3, 2, SEQ], F32R, over)
        hid2_lo = sb("hid2_lo", [P, 3, 2, SEQ], F32R, over)
        hid2 = sb("hid2", [P, 3, TILES, HID], F32, over)
        over.close()

        bank = [ctx.enter_context(nc.psum_tensor(f"bank{i}", [P, 512], F32)) for i in range(8)]
        ada_parts = nc.dram_tensor("ada_parts", (P, N_ADA * D), F32, kind="Internal").ap()
        rel_rows = nc.dram_tensor("rel_rows", (2 * MOBA_PAIRS, 2 * SEQ), F32, kind="Internal").ap()

        G = {}
        g = 0
        for name, units in (("kv_a", 2), ("kv_b", 2), ("a_in", 10), ("a_out", 4), ("dense", 3 * DENSE_STEPS),
                            ("b_in", 14), ("b_out", 4), ("experts", 3 * EXPERT_STEPS * EXPERTS),
                            ("in_2", 13), ("out_2", 4), ("ff_2", 2 * FF2_STEPS)):
            G[name] = g
            g += units
        B = {}
        b = 0
        for name, blocks in (("kv_a", 1), ("kv_b", 1), ("a_in", 5), ("a_out", 2), ("b_in", 7), ("b_out", 2),
                             ("in_2", 7), ("out_2", 2)):
            B[name] = b
            b += blocks

        class Ring:

            def __init__(self, name, first=0, credit=0):
                self.first, self.credit = first, credit
                self.landed = [semaphore(f"{name}landed{i}") for i in range(RING)]
                self.hi = semaphore(f"{name}hi_ready")
                self.lo = semaphore(f"{name}lo_ready")
                self.hi_used = semaphore(f"{name}unit_hi_used")
                self.used = semaphore(f"{name}unit_used")

        ring = Ring("")
        more_ring = Ring("more_", G["experts"], RING)
        block_out = semaphore("block_out")
        gain_in = [semaphore("gain_in0"), semaphore("gain_in1")]
        loaded = {n: semaphore(f"in_{n}") for n in
                  ("con", "ident", "x", "mem", "lam", "rel", "lb", "router", "c", "wgate", "bgate", "bias0", "bias1")}
        rel_stored = semaphore("rel_stored")
        ada_ready = semaphore("ada_ready")
        ada_scaled = semaphore("ada_scaled")
        ada_in = [semaphore(f"ada_in{i}") for i in range(ADA_BUFFERS)]
        ada_bias_in = semaphore("ada_bias_in")
        ada_stored = semaphore("ada_stored")
        ada_back = [semaphore(f"ada_back{i}") for i in range(N_ADA // 2)]
        out_stored = semaphore("out_stored")

        def have(name):
            return name in stages

        block = ctx.enter_context(nc.Block())

        def wide(ap):
            return ap.rearrange("l (k p) n -> p (l k) n", p=P)

        W = {"kv_a": wide(A["a_w_mem_kv"]), "kv_b": wide(A["b_w_mem_kv"]), "a_in": wide(A["a_w_in"]),
             "a_out": wide(A["a_w_out"]), "b_in": wide(A["b_w_in"]), "b_out": wide(A["b_w_out"]),
             "in_2": wide(A["w_in_2"]), "out_2": wide(A["w_out_2"])}
        W_dense_up = A["dense_w_gate_up"].rearrange("l (k p) (two n) -> p (l k) two n", p=P, two=2)
        W_dense_down = wide(A["dense_w_down"])
        W_up = A["moe_w_gate_up"].rearrange("l e (k p) (two n) -> p (l e) k two n", p=P, two=2)
        W_down = A["moe_w_down"].rearrange("l e (k p) n -> p (l e) k n", p=P)
        W_ff1 = wide(A["w_ff1_2"])
        W_ff2 = wide(A["w_ff2_2"])

        def columns(n):
            return [(c, min(512, n - c)) for c in range(0, n, 512)]

        COLS = {"kv_a": columns(512), "kv_b": columns(512), "a_in": columns(3 * DA_W + 256),
                "a_out": columns(D), "b_in": columns(4 * HG_W + 256), "b_out": columns(D),
                "in_2": [(0, 512), (512, 512), (1024, 512), (1552, 512), (2064, 512), (2576, 512)],
                "out_2": columns(D)}

        def repeat(eng, n, body):
            with eng.Fori(0, n) as i:
                body(i)

        def rel_places():
            return work[0:BUCKETS + 1, 0:8], work[0:BUCKETS + 1, 8:520], work[0:8, 520:1032]

        def lam_place():
            return work[:, 1032:1288].rearrange("p (a n) -> p a n", a=4)

        def bias_place(i):
            return kv[:, i % 2].rearrange("p m (t s) -> p m t s", t=TILES)

        def part(buf, start, *dims):
            n = int(np.prod(dims))
            names = "abc"[:len(dims)]
            pattern = "p (" + " ".join(names) + ") -> p " + " ".join(names)
            return buf[:, start:start + n].rearrange(pattern, **dict(zip(names, dims)))

        class Pairs:

            def __init__(self, tag, n, qT, kT, q_cols, k_cols, probs, probsT, v, dv, first):
                self.tag, self.n, self.qT, self.kT = tag, n, qT, kT
                self.q_cols, self.k_cols = q_cols, k_cols
                self.probs, self.probsT, self.v, self.dv, self.first = probs, probsT, v, dv, first

        diff_bias = part(work, 7168, TILES, SEQ)
        diff_sum = part(work, 7680, 4, P)
        head_scratch = part(work, 8192, TILES, HG_W)
        diff = Pairs("diff", DA_HEADS, part(work, 0, DA_HEADS, SEQ), part(work, 1536, DA_HEADS, SEQ),
                     [proj[:, t, i * P:(i + 1) * P] for i in range(DA_HEADS) for t in range(TILES)],
                     [proj[:, t, DA_W + i * P:DA_W + (i + 1) * P] for i in range(DA_HEADS) for t in range(TILES)],
                     [part(work, 3072 + 1024 * k, 2, TILES, SEQ) for k in range(2)],
                     [part(work, 5120 + 1024 * k, 2, TILES, SEQ) for k in range(2)],
                     lambda i, m, t: proj[:, t, 2 * DA_W + i * P:2 * DA_W + (i + 1) * P], P, 0)

        def memory_pairs(tag, layer, q0):
            kvl = kv[:, layer]
            return Pairs(tag, MEM_PAIRS, part(work, 0, MEM_PAIRS, SEQ), part(work, 512, MEM_PAIRS, SEQ),
                         [proj[:, t, q0 + i * P:q0 + (i + 1) * P] for i in range(MEM_PAIRS) for t in range(TILES)],
                         [kvl[:, t, i * P:(i + 1) * P] for i in range(MEM_PAIRS) for t in range(TILES)],
                         [part(work, 3072 + 1024 * k, 2, TILES, SEQ) for k in range(2)],
                         [part(work, 5120 + 1024 * k, 2, TILES, SEQ) for k in range(2)],
                         lambda i, m, t: kvl[:, t, 256 + (2 * i + m) * 64:256 + (2 * i + m + 1) * 64], 64, 768)

        a_mem = memory_pairs("a_mem", 0, 3 * DA_W)
        b_mem = memory_pairs("b_mem", 1, 4 * HG_W)
        M0 = 3 * 512 + GLA_RANK
        moba = Pairs("moba", MOBA_PAIRS, part(work2, 0, MOBA_PAIRS, SEQ), part(work2, 1024, MOBA_PAIRS, SEQ),
                     [proj2[:, t, M0 + i * P:M0 + (i + 1) * P] for i in range(MOBA_PAIRS) for t in range(TILES)],
                     [proj2[:, t, M0 + 512 + i * P:M0 + 512 + (i + 1) * P] for i in range(MOBA_PAIRS) for t in range(TILES)],
                     [proj2[:, k, 0:1024].rearrange("p (m t s) -> p m t s", m=2, t=TILES) for k in range(2)],
                     [proj2[:, k, M0:M0 + 1024].rearrange("p (m t s) -> p m t s", m=2, t=TILES) for k in range(2)],
                     lambda i, m, t: proj2[:, t, M0 + 1024 + (2 * i + m) * 64:M0 + 1024 + (2 * i + m + 1) * 64], 64, 512)

        class Decayed:

            def __init__(self, tag, groups, per, place, keys, v, widths):
                self.tag, self.groups, self.per = tag, groups, per
                self.heads = groups * per
                n = groups * SEQ
                self.q, self.k, self.after, self.before = (part(place, i * n, groups, SEQ) for i in range(4))
                self.att = [part(place, 4 * n + i * 512, 4, P) for i in range(self.heads * TILES // 4)]
                self.cross = part(place, 4 * n + self.heads * TILES * P, self.heads, P)
                self.dq = [z[:, 0:n].rearrange("p (g s) -> p g s", g=groups)
                           for z in (mix[:, :, :].rearrange("p t d -> p (t d)"), plain[:, 1])]
                self.dk = [z[:, 0:n].rearrange("p (g s) -> p g s", g=groups) for z in (keys, plain[:, 0])]
                self.v = v
                self.widths = widths
                if per == 1:
                    self.outs = [(h, t) for h in range(self.heads) for t in range(TILES)]
                else:
                    self.outs = [(per * g + hh, t) for hh in range(per) for g in range(groups) for t in range(TILES)]

            def rows(self, h):
                n = P // self.per
                return slice((h % self.per) * n, (h % self.per + 1) * n)

        hgrn = Decayed("hgrn", HG_HEADS, 1, work, proj[:, 0, 0:1536],
                       lambda h, t: proj[:, t, 2 * HG_W + h * P:2 * HG_W + (h + 1) * P], None)
        gla = Decayed("gla", GLA_HEADS // 2, 2, work2, proj2[:, 0, 0:512],
                      lambda h, t: proj2[:, t, 512 + h * P:512 + (h + 1) * P], None)
        LEVELS = 7

        def cross_banks(d):
            if d.per == 1:
                return [list(range(h, min(h + 4, d.heads))) for h in range(0, d.heads, 4)]
            return [list(range(hh, d.heads, d.per)) for hh in range(d.per)]

        def out_pieces(d):
            return [(t, h, min(4, d.heads - h)) for t in range(TILES) for h in range(0, d.heads, 4)]

        SCATTER = (1, 3, 6, 7)

        def gla_rankT():
            return work2[0:GLA_RANK, 3584:3840]

        class Loop:

            def __init__(self, name):
                self.gated = semaphore(f"{name}_gated")
                self.hidden = semaphore(f"{name}_hidden")
                self.turned = semaphore(f"{name}_hidden_turned")
                self.hid_hi = semaphore(f"{name}_hidden_hi")
                self.hid_lo = semaphore(f"{name}_hidden_lo")

        class ExpertLoop(Loop):
            def __init__(self, name):
                super().__init__(name)
                self.picked = semaphore(f"{name}_picked")
                self.pick_turned = semaphore(f"{name}_pick_turned")
                self.staged = semaphore(f"{name}_pick_staged")
                self.pickT = semaphore(f"{name}_pickT")
                self.gathered = semaphore(f"{name}_gathered")
                self.slots_hi = semaphore(f"{name}_slots_hi")
                self.slots_lo = semaphore(f"{name}_slots_lo")
                self.y_hi = semaphore(f"{name}_y_hi")
                self.y_lo = semaphore(f"{name}_y_lo")
                self.scattered = semaphore(f"{name}_scattered")
                self.added = semaphore(f"{name}_added")

        dense_loop = Loop("dense")
        expert_loop = ExpertLoop("expert")
        more_loop = ExpertLoop("more")
        ff_loop = Loop("ff")

        def ada_sums(pool):
            acc = part(work, 0, N_ADA, D)
            rows = part(work, N_ADA * D, ADA_BUFFERS, D)
            weights = wide(A["w_ada_2"])
            pool.wait_ge(*at("mix_a"))
            for a in range(N_ADA):
                pool.memset(acc[:, a, :], 0.0).then_inc(ada_ready, 1)
            pool.wait_ge(ada_ready, N_ADA)
            pool.dma_start(work[0:1, 0:N_ADA * D], A["b_ada_2"]).then_inc(ada_bias_in, 16)

            def load_row(k, n):
                pool.dma_start(rows[:, n % ADA_BUFFERS, :], weights[:, k + n // N_ADA, n % N_ADA * D:(n % N_ADA + 1) * D])\
                    .then_inc(ada_in[n % ADA_BUFFERS], 16)

            def row_block(k, last):
                for a in range(N_ADA):
                    ahead = a + ADA_BUFFERS - 1
                    if not last or ahead < N_ADA:
                        pool.wait_ge(ada_ready, N_ADA * k + N_ADA + a)
                        load_row(k, ahead)
                    pool.wait_ge(ada_in[a % ADA_BUFFERS], 32 * k + 16 * (a // ADA_BUFFERS + 1))
                    row = rows[:, a % ADA_BUFFERS, :]
                    pool.tensor_tensor(row, row, c_col[:, k:k + 1].broadcast_to([P, D]), ALU.mult).then_inc(ada_scaled, 1)
                    pool.wait_ge(ada_scaled, N_ADA * k + a + 1)
                    pool.wait_ge(ada_ready, N_ADA * k + a + 1)
                    pool.tensor_tensor(acc[:, a, :], acc[:, a, :], row, ALU.add).then_inc(ada_ready, 1)

            for n in range(ADA_BUFFERS - 1):
                load_row(0, n)
            pool.wait_ge(ada_bias_in, 16)
            pool.wait_ge(*at("ada", "c"))
            for k in range(KC):
                row_block(k, k == KC - 1)
            pool.wait_ge(ada_ready, N_ADA * (KC + 1))
            pool.dma_start(ada_parts, work[:, 0:N_ADA * D]).then_inc(ada_stored, 16)

        def tree_keys(pool, S, tag):
            d = hgrn if tag == "hgrn" else gla
            for level in range(2, LEVELS + 2):
                pool.wait_ge(*at(tag, "before", level))
                if level > 3:
                    pool.wait_ge(*at(tag, "level", level - 2))
                o, a, b = d.dk[level % 2], d.k, d.before
                if level > LEVELS:
                    o, a, b = (z[:, :, 0:P] for z in (o, a, b))
                pool.tensor_tensor(o, a, b, ALU.mult).then_inc(S(tag, "keys", level), 1)

        assert EXPERT_STEPS % 2 == 0 and EXPERT_STEPS * 3 % RING == 0
        FIRST_ROUND = G["experts"] + 2
        NEXT_ROUND = FIRST_ROUND + RING
        TAIL = FIRST_ROUND + RING * EXPERT_ROUNDS
        NEXT_FIRST = TAIL + RING
        PER_EXPERT = 3 * EXPERT_STEPS // RING

        def expert_order(eng, first, rounds, tail, next_first):
            first()
            with eng.Fori(0, EXPERTS - 1) as e:
                with eng.Fori(0, EXPERT_ROUNDS - 1) as i:
                    rounds(e, i)
                tail(e, False)
                next_first(e)
            with eng.Fori(0, EXPERT_ROUNDS - 1) as i:
                rounds(EXPERTS - 1, i)
            tail(EXPERTS - 1, True)

        @block.sync
        def _(sp):
            def load(R, g, rounds, src, split):
                before = g - R.first - RING + 1 + R.credit
                if before > 0:
                    sp.wait_ge(R.hi, before + RING * rounds)
                    sp.wait_ge(R.lo, before + RING * rounds)
                dst = split(raw[:, g % RING, :])
                for n in range(2):
                    if split is two:
                        d, c = dst[:, :, n, :], src[:, :, n, :]
                    else:
                        k = dst.shape[1] // 2
                        d, c = dst[:, n * k:(n + 1) * k, :], src[:, n * k:(n + 1) * k, :]
                    sp.dma_start(d, c).then_inc(R.landed[g % RING], 16)

            def half(n):
                return lambda u: u[:, 0:4 * n].rearrange("p (k n) -> p k n", k=4)

            def load_block(name, j):
                c, n = COLS[name][j]
                for h in range(2):
                    load(ring, G[name] + 2 * j + h, 0, W[name][:, 4 * h:4 * h + 4, c:c + n], half(n))

            def two(u):
                return u.rearrange("p (k two n) -> p k two n", k=4, two=2)

            def down(u):
                return u.rearrange("p (k n) -> p k n", k=2)

            sp.dma_start(mix[:, :, :], A["mem"][0].rearrange("(t p) d -> p t d", p=P)).then_inc(loaded["mem"], 16)
            sp.dma_start(con[:, 0:P], consts[:, 0:P]).then_inc(loaded["ident"], 16)
            if have("memory"):
                load_block("kv_a", 0)
            sp.dma_start(x[:, :, :], A["x"][0].rearrange("(t p) d -> p t d", p=P)).then_inc(loaded["x"], 16)
            if have("memory"):
                load_block("kv_b", 0)
            for name in ("a_in", "a_out"):
                if have(name):
                    for j in range(len(COLS[name])):
                        load_block(name, j)
            if have("dense"):
                def dense_step(g, rounds, step, n):
                    for s in range(n):
                        for h in range(2):
                            load(ring, g + 2 * s + h, rounds,
                                 W_dense_up[:, 4 * h:4 * h + 4, :, bass.ds((step + s) * HID, HID)], two)
                    for s in range(n):
                        load(ring, g + 2 * n + s, rounds, W_dense_down[:, bass.ds((step + s) * 2, 2), :], down)

                dense_step(G["dense"], 0, 0, 1)
                repeat(sp, DENSE_STEPS // 2, lambda i: dense_step(G["dense"] + 3, i, 2 * i + 1, 2))
            for name in ("b_in", "b_out"):
                if have(name):
                    for j in range(len(COLS[name])):
                        load_block(name, j)
            if have("experts"):
                def experts(R):
                    def up(g, rounds, e, step, h):
                        load(R, g, rounds, W_up[:, bass.ds(e, 1), 4 * h:4 * h + 4, :, bass.ds(step * HID, HID)]
                             .rearrange("p e k two n -> p (e k) two n"), two)

                    def down_rows(g, rounds, e, step):
                        load(R, g, rounds, W_down[:, bass.ds(e, 1), bass.ds(step * 2, 2), :]
                             .rearrange("p e k n -> p (e k) n"), down)

                    def one_round(g, rounds, e, i):
                        up(g, rounds, e, 2 * i + 1, 0)
                        up(g + 1, rounds, e, 2 * i + 1, 1)
                        down_rows(g + 2, rounds, e, 2 * i)
                        up(g + 3, rounds, e, 2 * i + 2, 0)
                        up(g + 4, rounds, e, 2 * i + 2, 1)
                        down_rows(g + 5, rounds, e, 2 * i + 1)

                    def first():
                        up(G["experts"], 0, 0, 0, 0)
                        up(G["experts"] + 1, 0, 0, 0, 1)
                        one_round(FIRST_ROUND, 0, 0, 0)

                    def tail(e, last):
                        n, r = EXPERT_STEPS, PER_EXPERT * e
                        up(TAIL, r, e, n - 1, 0)
                        up(TAIL + 1, r, e, n - 1, 1)
                        down_rows(TAIL + 2, r, e, n - 2)
                        if last:
                            down_rows(TAIL + 3, r, e, n - 1)
                        else:
                            up(TAIL + 3, r, e + 1, 0, 0)
                            down_rows(TAIL + 4, r, e, n - 1)
                            up(TAIL + 5, r, e + 1, 0, 1)

                    expert_order(sp, first,
                                 lambda e, i: one_round(NEXT_ROUND, PER_EXPERT * e + i, e, i + 1), tail,
                                 lambda e: one_round(NEXT_FIRST, PER_EXPERT * e, e + 1, 0))

                experts(ring)
                sp.wait_ge(*at("overflow"))
                more = sp.value_load(flag[0:1, 0:1], min_val=0, max_val=1)
                with sp.If(more > 0):
                    sp.wait_ge(ring.hi, G["in_2"])
                    sp.wait_ge(ring.lo, G["in_2"])
                    experts(more_ring)
                    sp.wait_ge(more_ring.hi, RING + G["in_2"] - G["experts"])
                    sp.wait_ge(more_ring.lo, RING + G["in_2"] - G["experts"])
            if have("in_2"):
                for j in range(6):
                    load_block("in_2", j)
                load(ring, G["in_2"] + 12, 0, W["in_2"][:, :, 1536:1552],
                     lambda u: u[:, 0:KC * GLA_RANK].rearrange("p (k n) -> p k n", k=KC))
            if have("out_2"):
                for j in range(2):
                    load_block("out_2", j)
            if have("ff_2"):
                def ff_up(g, rounds, step):
                    load(ring, g, rounds, W_ff1[:, :, bass.ds(step * HID, HID)],
                         lambda u: u.rearrange("p (k n) -> p k n", k=KC))

                def ff_down(g, rounds, step):
                    load(ring, g, rounds, W_ff2[:, bass.ds(step * 2, 2), :], down)

                def ff_steps(i):
                    g0 = G["ff_2"]
                    ff_up(g0, i, 3 * i)
                    ff_up(g0 + 1, i, 3 * i + 1)
                    ff_up(g0 + 2, i, 3 * i + 2)
                    ff_down(g0 + 3, i, 3 * i)
                    ff_down(g0 + 4, i, 3 * i + 1)
                    ff_down(g0 + 5, i, 3 * i + 2)
                repeat(sp, FF2_STEPS // 3, ff_steps)
                ff_up(G["ff_2"] + 30, 0, 15)
                ff_down(G["ff_2"] + 31, 0, 15)

        @block.gpsimd
        def _(pool):
            S = Signals("pool", semaphore, numbers)
            S.stage("main")
            uses = [0]

            def load_gain():
                n = uses[0]
                name = GAINS[n]
                src = A[name]
                if len(src.shape) == 2:
                    src = src[0]
                if n >= 2:
                    pool.wait_ge(*at("gain used", n - 2))
                pool.dma_start(gain[:, n % 2, 0:src.shape[0]], src.partition_broadcast(P)).then_inc(gain_in[n % 2], 16)
                uses[0] += 1

            load_gain()
            load_gain()
            pool.memset(ones[:, :], 1.0)
            pool.memset(zero[:, :], 0.0).then_inc(S("zero"), 1)
            if have("a_in"):
                load_gain()
            relx, onehot, relout = rel_places()
            pool.memset(relx, 1.0).then_inc(S("relx"), 1)
            pool.wait_ge(*S.last())
            pool.dma_start(relx[0:BUCKETS, :], A["rel_bias_2"]).then_inc(loaded["rel"], 16)
            pool.dma_start(onehot, buckets).then_inc(loaded["rel"], 16)
            lam4 = lam_place()
            for n, name in enumerate(("a_lam_q1", "a_lam_q2", "a_lam_k1", "a_lam_k2")):
                pool.dma_start(lam4[:, n, :], A[name][0].partition_broadcast(P)).then_inc(loaded["lam"], 16)
            pool.dma_start(lb[:, 0, :], A["b_lb_logits"].rearrange("l (h p) -> p (l h)", p=P),
                           allow_slow_non_contiguous=True).then_inc(loaded["lb"], 16)
            pool.dma_start(b_gate[:, :], A["b_gla_gate_2"].rearrange("l (g p) -> p (l g)", p=P),
                           allow_slow_non_contiguous=True).then_inc(loaded["bgate"], 16)
            pool.dma_start(c_col[:, :], A["c_2"].rearrange("b (k p) -> p (b k)", p=P),
                           allow_slow_non_contiguous=True).then_inc(loaded["c"], 16)
            pool.dma_start(con[:, P:C_ALL], consts[:, P:C_ALL]).then_inc(loaded["con"], 16)
            pool.wait_ge(*at("rel rows"))
            pool.dma_start(rel_rows, relout).then_inc(rel_stored, 16)
            if have("diff"):
                load_gain()
            if have("dense"):
                load_gain()
            if have("b_in"):
                load_gain()
            if have("hgrn"):
                if have("ada"):
                    ada_sums(pool)
                load_gain()
                tree_keys(pool, S, "hgrn")
            if have("route"):
                pool.wait_ge(*at("b_out", "added", 1))
                pool.dma_start(w_router[:, :, :], A["moe_router"].rearrange("l (k p) e -> p (l k) e", p=P)).then_inc(loaded["router"], 16)
                load_gain()
            if have("ada"):
                load_gain()
                pool.wait_ge(*at("experts done"))
                pool.wait_ge(ada_stored, 16)
                for n in range(N_ADA // 2):
                    pool.dma_start(ada[:, 2 * n:2 * n + 2, :].rearrange("p a d -> p (a d)"),
                                   ada_parts[:, 2 * n * D:(2 * n + 2) * D]).then_inc(ada_back[n], 16)
                pool.dma_start(w_gate[:, :], A["w_gla_gate_2"][0]).then_inc(loaded["wgate"], 16)
            if have("in_2"):
                load_gain()
            if have("gla"):
                load_gain()
                tree_keys(pool, S, "gla")
            if have("moba"):
                pool.wait_ge(rel_stored, 16)
                for i in range(MOBA_PAIRS):
                    if i >= 2:
                        pool.wait_ge(*at("moba", "biased", i - 2))
                    else:
                        pool.wait_ge(*at("gla", "products"))
                    for m in range(2):
                        src = bass.AP(rel_rows.tensor, (2 * i + m) * 2 * SEQ, [[1, P], [P, TILES], [1, SEQ]])
                        pool.dma_start(bias_place(i)[:, m], src).then_inc(loaded[f"bias{i % 2}"], 16)
            if have("ff_2"):
                load_gain()
            if have("final"):
                load_gain()
            for t in range(TILES):
                pool.wait_ge(*at("result", t))
                pool.dma_start(out[0, t * P:(t + 1) * P, :], x[:, t, :]).then_inc(out_stored, 16)
            pool.wait_ge(rel_stored, 16)
            pool.wait_ge(out_stored, 16 * TILES)

        def flat(ap):
            return ap.rearrange("p a b -> p (a b)")

        NORM_BLOCKS = [(kc, t) for kc in range(KC) for t in range(TILES)]

        @block.scalar
        def _(act):
            S = Signals("scalar", semaphore, numbers)
            S.stage("prep")

            def split_hi(R, g, rounds, n=UNIT):
                u = g - R.first
                act.wait_ge(R.landed[g % RING], 32 * (u // RING + 1) + 32 * rounds)
                before = u - SPLIT + 1 + R.credit
                if before > 0:
                    act.wait_ge(R.hi_used, before + RING * rounds)
                    act.wait_ge(R.lo, before + RING * rounds)
                act.activation(w_hi[:, g % SPLIT, 0:n], raw[:, g % RING, 0:n], ACT.Copy).then_inc(R.hi, 1)

            def norm(tag, src, junk, *waits):
                *waits, tiles = waits
                for w in waits:
                    act.wait_ge(*w)
                for t in range(TILES):
                    if t == 0 or isinstance(tiles, list):
                        act.wait_ge(*(tiles[t] if isinstance(tiles, list) else tiles))
                    sq = act.activation(junk[:, t, 0:D], src[:, t, :], ACT.Square, accum_out=sumsq[:, t:t + 1])
                sq.then_inc(S(tag, "squares"), 1)
                act.wait_ge(*at(tag, "variance"))
                act.activation(rstd[:, :], sumsq[:, :], ACT.Sqrt).then_inc(S(tag, "deviation"), 1)

            def turn_split(tag, unit):
                act.wait_ge(ring.used, unit) if unit else None
                for n in range(4):
                    act.wait_ge(*at(tag, "turned", n))
                    act.activation(flat(hT_hi[:, 2 * n:2 * n + 2, :]), bank[6 + n % 2][:, :], ACT.Copy)\
                       .then_inc(S(tag, "hi", n), 1)

            def turn_copy(tag, dst, cols, scale=1.0):
                for n in range(0, cols, 512):
                    act.wait_ge(*at(tag, "turned", n // 512))
                    act.activation(dst[:, n:n + 512], bank[6 + n // 512 % 2][:, 0:min(512, cols - n)], ACT.Copy, scale=scale)\
                       .then_inc(S(tag, "taken", n // 512), 1)

            def begin(name):
                for h in range(2):
                    split_hi(ring, G[name] + h, 0, 4 * COLS[name][0][1])

            def product(name, dst, meanwhile=None):
                def leave(j):
                    c, n = COLS[name][j]
                    act.wait_ge(ring.used, G[name] + 2 * j + 2)
                    for t in range(TILES):
                        out_ = act.activation(dst[:, t, c:c + n], bank[2 * ((B[name] + j) % 3) + t][:, 0:n], ACT.Copy)
                    out_.then_inc(block_out, 1)

                for j, (c, n) in enumerate(COLS[name]):
                    for h in range(2 if j or name == "kv_a" else 0):
                        split_hi(ring, G[name] + 2 * j + h, 0, 4 * n)
                    if j > 0 and dst is not None:
                        leave(j - 1)
                if meanwhile is not None:
                    meanwhile()
                if dst is not None:
                    leave(len(COLS[name]) - 1)

            def pairs(a, before=None):
                turn_copy(a.tag + "_q", flat(a.qT), a.n * SEQ)
                turn_copy(a.tag + "_k", flat(a.kT), a.n * SEQ)
                if before is not None:
                    head_norm(before)

                def exponentials(i):
                    k = i % 2
                    act.wait_ge(*at(a.tag, "max", i))
                    for m in range(2):
                        for t in range(TILES):
                            j = 2 * m + t
                            e = act.activation(a.probs[k][:, m, t, :], a.probs[k][:, m, t, :], ACT.Exp,
                                               bias=top[:, k, j:j + 1], accum_out=sums[:, i % 4, j:j + 1])
                    e.then_inc(S(a.tag, "exp", i), 1)

                exponentials(0)
                for i in range(a.n):
                    k = i % 2
                    if i + 1 < a.n:
                        exponentials(i + 1)
                    act.wait_ge(*at(a.tag, "turned", i))
                    if i >= 2:
                        act.wait_ge(*at(a.tag, "values", i - 2))
                    for m in range(2):
                        c = act.activation(flat(a.probsT[k][:, m]), bank[4 + m][:, :], ACT.Copy)
                    c.then_inc(S(a.tag, "probsT", i), 1)

            def head_norm(tag):
                act.wait_ge(*at(tag, "head variance"))
                act.activation(headsq[:, :], headsq[:, :], ACT.Sqrt).then_inc(S(tag, "head deviation"), 1)

            def decayed_out(d):
                act.wait_ge(*at(d.tag, "level", LEVELS + 1))
                done = 0
                for b, heads in enumerate(cross_banks(d)):
                    n = len(heads)
                    c = act.activation(flat(d.cross[:, done:done + n, :]), bank[b][:, 0:n * P], ACT.Copy)
                    done += n
                c.then_inc(S(d.tag, "cross"), 1)
                act.wait_ge(*at(d.tag, "products"))
                for n, (t, h0, m) in enumerate(out_pieces(d)):
                    c = act.activation(mix[:, t, h0 * P:(h0 + m) * P], bank[n][:, 0:m * P], ACT.Copy)
                c.then_inc(S(d.tag, "out"), 1)

            def mlp_round(R, L, g, rounds, step, nt, n):
                def silu(p):
                    act.wait_ge(R.used, g - R.first + R.credit + 2 * p + 2 + RING * rounds)
                    for t in range(nt):
                        act.activation(gated[:, p, t, :], bank[2 * p + t][:, 0:HID], ACT.Silu).then_inc(L.gated, 1)

                def hidden_hi(p):
                    for t in range(nt):
                        act.wait_ge(L.turned, nt * (step + p) + t + 1)
                        act.activation(hid_hi[:, p, :, t * P:(t + 1) * P],
                                       bank[2 * p + t][:, 0:HID].rearrange("p (k s) -> p k s", k=2), ACT.Copy)\
                           .then_inc(L.hid_hi, 1)

                if n == 2:
                    split_hi(R, g, rounds)
                    split_hi(R, g + 1, rounds)
                split_hi(R, g + 2, rounds)
                if n == 2:
                    split_hi(R, g + 3, rounds)
                silu(0)
                if n == 2:
                    split_hi(R, g + 4, rounds)
                hidden_hi(0)
                if n == 2:
                    split_hi(R, g + 5, rounds)
                    silu(1)
                    hidden_hi(1)

            def ada_out(first, end):
                for j in range(first, end):
                    act.wait_ge(*at("ada", "summed", j))
                    act.activation(ada[:, j // 2, j % 2 * 512:(j % 2 + 1) * 512], bank[j % 6][:, :], ACT.Copy)\
                       .then_inc(S("ada", "out", j), 1)

            def prepare():
                act.wait_ge(*at("lam sums"))
                act.activation(neg_lam[:, 0:2], neg_lam[:, 0:2], ACT.Exp).then_inc(S("lam exp"), 1)
                act.wait_ge(*at("lb shifted"))
                act.activation(lb[:, 1, :], lb[:, 1, :], ACT.Exp).then_inc(S("lb exp"), 1)
                act.wait_ge(*at("rel product"))
                act.activation(rel_places()[2], bank[0][0:8, :], ACT.Copy).then_inc(S("rel rows"), 1)

            if have("memory"):
                S.stage("memory")
                norm("norm_kv_a", mix, proj, (loaded["mem"], 16))
                turn_split("norm_kv_a", 0)
                product("kv_a", kv[:, 0], lambda: (norm("norm_a", x, mix, (loaded["x"], 16), at("norm_kv_b", "h")), begin("kv_b")))
                turn_split("norm_kv_b", G["kv_b"])
                product("kv_b", kv[:, 1], lambda: begin("a_in"))
            if have("a_in"):
                S.stage("a_in")
                prepare()
                turn_split("norm_a", G["a_in"])
                product("a_in", proj)
            if have("diff"):
                S.stage("diff")
                act.wait_ge(rel_stored, 16)
                pairs(diff)
            if have("a_mem"):
                S.stage("a_mem")
                pairs(a_mem, "diff")
            if have("a_out"):
                S.stage("a_out")
                act.wait_ge(loaded["c"], 16)
                act.activation(c_col[:, :], c_col[:, :], ACT.Silu).then_inc(S("ada", "c"), 1)
                begin("a_out")
                turn_split("mix_a", G["a_out"])
                product("a_out", None)
            if have("dense"):
                S.stage("dense")
                for h in range(2):
                    split_hi(ring, G["dense"] + h, 0)
                norm("norm_dense", x, mix, at("a_out", "added", 1))
                turn_split("norm_dense", G["dense"])
                mlp_round(ring, dense_loop, G["dense"], 0, 0, TILES, 1)
                repeat(act, DENSE_STEPS // 2,
                       lambda i: mlp_round(ring, dense_loop, G["dense"] + 3, i, 2 * i + 1, TILES, 2))
            if have("b_in"):
                S.stage("b_in")
                begin("b_in")
                norm("norm_b", x, mix, [at("dense", "added", t) for t in range(TILES)])
                turn_split("norm_b", G["b_in"])
                product("b_in", proj)
            if have("hgrn"):
                S.stage("hgrn")
                if have("ada"):
                    act.wait_ge(ada_stored, 16)
                turn_copy("hgrn_q", flat(hgrn.q), HG_W * TILES)
                for n in range(HG_W * TILES // 512):
                    act.wait_ge(*at("hgrn_f", "turned", n))
                    act.activation(flat(hgrn.after)[:, n * 512:(n + 1) * 512], bank[6 + n % 2][:, :], ACT.Sigmoid)
                    act.activation(flat(hgrn.k)[:, n * 512:(n + 1) * 512], bank[6 + n % 2][:, :], ACT.Sigmoid, scale=-1.0)\
                       .then_inc(S("hgrn_f", "taken", n), 1)
                g_cols = proj[:, :, 3 * HG_W:4 * HG_W]
                act.activation(g_cols, g_cols, ACT.Silu).then_inc(S("hgrn", "silu"), 1)
                decayed_out(hgrn)
            if have("b_mem"):
                S.stage("b_mem")
                pairs(b_mem, "hgrn")
            if have("b_out"):
                S.stage("b_out")
                begin("b_out")
                turn_split("mix_b", G["b_out"])
                product("b_out", None)
            if have("route"):
                S.stage("route")
                norm("norm_moe", x, mix, at("b_out", "added", 1))
                turn_split("norm_moe", G["experts"])
                act.activation(flat(moe_h_hi[:, :, :]), flat(mix[:, :, :]), ACT.Copy).then_inc(S("route", "h_hi"), 1)
                act.wait_ge(*at("route", "gap"))
                act.activation(ratio[:, 1, :], ratio[:, 0, :], ACT.Exp).then_inc(S("route", "exp"), 1)
            if have("experts"):
                S.stage("experts")

                def experts(R, L):
                    def silu(p, step, units, rounds):
                        act.wait_ge(R.used, units - R.first + R.credit + RING * rounds)
                        act.activation(gated[:, p, 0, :], bank[2 * p][:, 0:HID], ACT.Silu).then_inc(L.gated, 1)

                    def hidden_hi(p, step):
                        act.wait_ge(L.turned, step + 1)
                        act.activation(hid_hi[:, p, :, 0:P], bank[2 * p][:, 0:HID].rearrange("p (k s) -> p k s", k=2),
                                       ACT.Copy).then_inc(L.hid_hi, 1)

                    def one_round(g, rounds, step, after_two):
                        split_hi(R, g, rounds)
                        if after_two:
                            silu(0, step, g - 1, rounds)
                        split_hi(R, g + 1, rounds)
                        if not after_two:
                            silu(0, step, g, rounds)
                        split_hi(R, g + 2, rounds)
                        hidden_hi(0, step)
                        split_hi(R, g + 3, rounds)
                        silu(1, step + 1, g + 2, rounds)
                        split_hi(R, g + 4, rounds)
                        split_hi(R, g + 5, rounds)
                        hidden_hi(1, step + 1)

                    def slots(n, used=None):
                        act.wait_ge(L.gathered, 2 * n - 1)
                        if used is not None:
                            act.wait_ge(R.used, used)
                        for k in range(2):
                            c = act.activation(flat(slot_hi[:, 4 * k:4 * k + 4, :]), bank[6 + k][:, :], ACT.Copy)
                        c.then_inc(L.slots_hi, 1)

                    def stage_pick(n):
                        act.wait_ge(L.pick_turned, n)
                        act.activation(staged[:, :], bank[1][:, 0:TILES * P], ACT.Copy).then_inc(L.staged, 1)

                    def first():
                        split_hi(R, G["experts"], 0)
                        split_hi(R, G["experts"] + 1, 0)
                        slots(1)
                        stage_pick(1)
                        one_round(FIRST_ROUND, 0, 0, False)

                    def tail(e, last):
                        r, step = PER_EXPERT * e, EXPERT_STEPS * e + EXPERT_STEPS - 2
                        split_hi(R, TAIL, r)
                        silu(0, step, TAIL - 1, r)
                        split_hi(R, TAIL + 1, r)
                        split_hi(R, TAIL + 2, r)
                        hidden_hi(0, step)
                        if not last:
                            slots(e + 2, TAIL + 2 - R.first + R.credit + RING * r)
                        silu(1, step + 1, TAIL + 2, r)
                        split_hi(R, TAIL + 3, r)
                        if last:
                            hidden_hi(1, step + 1)
                        else:
                            split_hi(R, TAIL + 4, r)
                            hidden_hi(1, step + 1)
                            act.wait_ge(L.pickT, e + 1)
                            stage_pick(e + 2)
                            split_hi(R, TAIL + 5, r)
                        act.wait_ge(R.used, TAIL + (4 if last else 5) - R.first + R.credit + RING * r)
                        for k in range(2):
                            c = act.activation(y_hi[:, k * 512:(k + 1) * 512], bank[4 + k][:, :], ACT.Copy)
                        c.then_inc(L.y_hi, 1)

                    expert_order(act, first,
                                 lambda e, i: one_round(NEXT_ROUND, PER_EXPERT * e + i, EXPERT_STEPS * e + 2 * i + 2, True),
                                 tail,
                                 lambda e: one_round(NEXT_FIRST, PER_EXPERT * e, EXPERT_STEPS * e + EXPERT_STEPS, False))

                experts(ring, expert_loop)
                act.wait_ge(*at("overflow"))
                more = act.value_load(flag[0:1, 0:1], min_val=0, max_val=1)
                with act.If(more > 0):
                    act.wait_ge(ring.used, G["in_2"])
                    act.sem_inc(more_ring.hi, RING)
                    experts(more_ring, more_loop)
                    act.wait_ge(more_ring.used, RING + G["in_2"] - G["experts"])
            if have("ada"):
                S.stage("ada")
                norm("norm_final", x, mix, at("experts done"))
                ada_out(0, 6)
            if have("in_2"):
                norm("norm_2", x, mix, at("norm_final", "h"))
                ada_out(6, 12)
                S.stage("in_2")
                begin("in_2")
                turn_split("norm_2", G["in_2"])
                product("in_2", proj2)
                split_hi(ring, G["in_2"] + 12, 0, KC * GLA_RANK)
                act.wait_ge(ring.used, G["in_2"] + 13)
                for t in range(TILES):
                    c = act.activation(proj2[:, t, 1536:1552], bank[2 * ((B["in_2"] + 6) % 3) + t][:, 0:GLA_RANK], ACT.Copy)
                c.then_inc(block_out, 1)
            if have("gla"):
                S.stage("gla")
                turn_copy("gla_q", flat(gla.q), 512, PAIR_SCALE)
                turn_copy("gla_k", flat(gla.k), 512)
                act.wait_ge(*at("gla", "rank turned"))
                act.activation(gla_rankT(), bank[6][0:GLA_RANK, 0:SEQ], ACT.Copy).then_inc(S("gla", "rankT"), 1)
                act.wait_ge(*at("gla", "gate"))
                act.wait_ge(loaded["bgate"], 16)
                f = gla.after
                for grp in range(2):
                    c = act.activation(f[:, grp, :], bank[7][:, grp * SEQ:(grp + 1) * SEQ], ACT.Sigmoid, bias=b_gate[:, grp:grp + 1])
                c.then_inc(S(), 1)
                act.wait_ge(*S.last())
                act.activation(flat(f), flat(f), ACT.Ln).then_inc(S(), 1)
                act.wait_ge(*S.last())
                act.activation(flat(f), flat(f), ACT.Exp, scale=1.0 / GLA_TAU).then_inc(S("gla", "f"), 1)
                gr_cols = proj2[:, :, 1024:1536]
                act.activation(gr_cols, gr_cols, ACT.Silu).then_inc(S("gla", "silu"), 1)
                decayed_out(gla)
            if have("moba"):
                S.stage("moba")
                pairs(moba, "gla")
            if have("out_2"):
                S.stage("out_2")
                begin("out_2")
                turn_split("mix_2", G["out_2"])
                product("out_2", None)
            if have("ff_2"):
                S.stage("ff_2")
                norm("norm_ff", x, mix, at("out_2", "added", 1))
                turn_split("norm_ff", G["ff_2"])

                def hidden_hi(p, step):
                    act.wait_ge(ff_loop.turned, step + 1)
                    act.activation(flat(hid2_hi[:, p]).rearrange("p (k t s) -> p t k s", k=2, t=TILES),
                                   bank[p][:, :].rearrange("p (t k s) -> p t k s", k=2, t=TILES), ACT.Copy)\
                       .then_inc(ff_loop.hid_hi, 1)

                def ff_round(i):
                    g = G["ff_2"]
                    split_hi(ring, g, i)
                    split_hi(ring, g + 1, i)
                    split_hi(ring, g + 2, i)
                    split_hi(ring, g + 3, i)
                    hidden_hi(0, 3 * i)
                    split_hi(ring, g + 4, i)
                    hidden_hi(1, 3 * i + 1)
                    split_hi(ring, g + 5, i)
                    hidden_hi(2, 3 * i + 2)
                repeat(act, FF2_STEPS // 3, ff_round)
                split_hi(ring, G["ff_2"] + 30, 0)
                split_hi(ring, G["ff_2"] + 31, 0)
                hidden_hi(0, 15)
            if have("final"):
                S.stage("final")
                norm("norm_out", x, mix, [at("ff_2", "added", t) for t in range(TILES)])

        @block.vector
        def _(dve):
            S = Signals("vector", semaphore, numbers)
            S.stage("prep")

            def f32(ap):
                return ap.bitcast(F32)

            def split_lo(R, g, rounds, n=UNIT):
                u = g - R.first
                dve.wait_ge(R.hi, u + 1 + R.credit + RING * rounds)
                before = u - SPLIT + 1 + R.credit
                if before > 0:
                    dve.wait_ge(R.used, before + RING * rounds)
                dve.tensor_tensor(w_lo[:, g % SPLIT, 0:n], raw[:, g % RING, 0:n], f32(w_hi[:, g % SPLIT, 0:n]),
                                  ALU.subtract).then_inc(R.lo, 1)

            def gain_row(n, width=D):
                dve.wait_ge(gain_in[n % 2], 16 * (n // 2 + 1))
                return gain[:, n % 2, 0:width]

            def norm(tag, src, dst, n, ada_at=None):
                dve.wait_ge(*at(tag, "squares"))
                dve.tensor_scalar(sumsq[:, :], sumsq[:, :], 1.0 / D, EPS, ALU.mult, ALU.add).then_inc(S(tag, "variance"), 1)
                g = gain_row(n)
                if ada_at is not None:
                    scale = ada[:, ada_at + 1, :]
                    dve.scalar_tensor_tensor(out=scale, in0=scale, scalar=1.0, in1=g, op0=ALU.add, op1=ALU.mult)\
                       .then_inc(S("gain used", n), 1)
                    g = scale
                dve.wait_ge(*at(tag, "deviation"))
                dve.reciprocal(rstd[:, :], rstd[:, :]).then_inc(S(), 1)
                dve.wait_ge(*S.last())
                for t in range(TILES):
                    h = dve.scalar_tensor_tensor(out=dst[:, t, 0:D], in0=src[:, t, :], scalar=rstd[:, t:t + 1], in1=g,
                                                 op0=ALU.mult, op1=ALU.mult)
                    if t < TILES - 1 and tag == "norm_out":
                        h.then_inc(S("result", t), 1)
                if ada_at is None:
                    h.then_inc(S(tag, "h"), 1)
                    S.also("gain used", n)
                    return
                h.then_inc(S(), 1)
                dve.wait_ge(*S.last())
                for t in range(TILES):
                    h = dve.tensor_tensor(dst[:, t, 0:D], dst[:, t, 0:D], ada[:, ada_at, :], ALU.add)
                h.then_inc(S(tag, "h"), 1)

            def turn_split(tag):
                for n in range(4):
                    dve.wait_ge(*at(tag, "hi", n))
                    dve.tensor_tensor(flat(hT_lo[:, 2 * n:2 * n + 2, :]), bank[6 + n % 2][:, :],
                                      f32(flat(hT_hi[:, 2 * n:2 * n + 2, :])), ALU.subtract).then_inc(S(tag, "taken", n), 1)

            def product(name, added, gate=None):
                def add(j):
                    c, n = COLS[name][j]
                    dve.wait_ge(ring.used, G[name] + 2 * j + 2)
                    for t in range(TILES):
                        y = bank[2 * ((B[name] + j) % 3) + t][:, 0:n]
                        if gate is not None:
                            dve.tensor_tensor(mix[:, t, c:c + n], y, gate[:, c:c + n], ALU.mult).then_inc(S(), 1)
                            dve.wait_ge(*S.last())
                            y = mix[:, t, c:c + n]
                        o = dve.tensor_tensor(x[:, t, c:c + n], x[:, t, c:c + n], y, ALU.add)
                    o.then_inc(block_out, 1)
                    numbers[(name, "added", j)] = ("block_out", B[name] + j + 1)

                for j, (c, n) in enumerate(COLS[name]):
                    for h in range(2):
                        split_lo(ring, G[name] + 2 * j + h, 0, 4 * n)
                    if added and j > 0:
                        add(j - 1)
                if added:
                    add(len(COLS[name]) - 1)

            def pairs(a, bias=None, scale=PAIR_SCALE):
                def scores(i):
                    k = i % 2
                    if bias == "distance":
                        slope = 2.0 ** (-8.0 * (i + 1) / DA_HEADS)
                        dve.scalar_tensor_tensor(out=flat(diff_bias), in0=con[:, C_DIST:C_DIST + 2 * SEQ], scalar=-slope,
                                                 in1=con[:, C_MASK:C_MASK + 2 * SEQ], op0=ALU.mult, op1=ALU.add).then_inc(S(), 1)
                        dve.wait_ge(*S.last())
                    if bias == "rows":
                        dve.wait_ge(loaded[f"bias{k}"], 32 * (i // 2 + 1))
                    if i >= 2:
                        dve.wait_ge(*at(a.tag, "turned", i - 2))
                    dve.wait_ge(*at(a.tag, "scores", i))
                    for m in range(2):
                        s_in, s_out = bank[2 * k + m][:, :], flat(a.probs[k][:, m])
                        if bias is None:
                            o = dve.tensor_scalar(s_out, s_in, scale, None, ALU.mult)
                        elif bias == "distance":
                            o = dve.scalar_tensor_tensor(out=s_out, in0=s_in, scalar=scale, in1=flat(diff_bias),
                                                         op0=ALU.mult, op1=ALU.add)
                        else:
                            o = dve.scalar_tensor_tensor(out=a.probs[k][:, m], in0=s_in.rearrange("p (t s) -> p t s", t=TILES),
                                                         scalar=scale, in1=bias_place(i)[:, m, :, ::-1],
                                                         op0=ALU.mult, op1=ALU.add)
                    o.then_inc(S(a.tag, "biased", i), 1)
                    dve.wait_ge(*S.last())
                    dve.tensor_reduce(top[:, k, :], a.probs[k].rearrange("p m t s -> p (m t) s"), AX.X, ALU.max).then_inc(S(), 1)
                    dve.wait_ge(*S.last())
                    dve.tensor_scalar(top[:, k, :], top[:, k, :], -1.0, None, ALU.mult).then_inc(S(a.tag, "max", i), 1)

                def outputs(i):
                    k = i % 2
                    r = sums[:, i % 4, :]
                    dve.wait_ge(*at(a.tag, "exp", i))
                    dve.reciprocal(r, r).then_inc(S(), 1)
                    dve.wait_ge(*S.last())
                    if a.tag == "diff":
                        dve.tensor_scalar(r[:, 2:4], r[:, 2:4], neg_lam[:, 2:3], None, ALU.mult).then_inc(S(), 1)
                        dve.wait_ge(*S.last())
                    dve.wait_ge(*at(a.tag, "values", i))
                    o = bank[6 + k][:, 0:4 * a.dv]
                    if a.tag == "diff":
                        dve.tensor_tensor(diff_sum, o.rearrange("p (j d) -> p j d", j=4),
                                          r.unsqueeze(2).broadcast_to([P, 4, a.dv]), ALU.mult).then_inc(S(), 1)
                        dve.wait_ge(*S.last())
                        dve.tensor_tensor(mix[:, :, i * P:(i + 1) * P], diff_sum[:, 0:2, :], diff_sum[:, 2:4, :],
                                          ALU.add).then_inc(S(a.tag, "out", i), 1)
                    else:
                        c = a.first + i * P
                        dve.tensor_tensor(mix[:, :, c:c + P].rearrange("p t (m d) -> p m t d", m=2),
                                          o.rearrange("p (m t d) -> p m t d", m=2, t=TILES),
                                          r.rearrange("p (m t) -> p m t", m=2).unsqueeze(3).broadcast_to([P, 2, TILES, a.dv]),
                                          ALU.mult).then_inc(S(a.tag, "out", i), 1)

                for i in range(a.n):
                    scores(i)
                    if i > 1:
                        outputs(i - 2)
                outputs(a.n - 2)
                outputs(a.n - 1)

            def head_norm(tag, heads, scratch, n, ready, factor=1.0, gate=None):
                w = heads * P
                m = mix[:, :, 0:w]
                m4 = m.rearrange("p t (h d) -> p t h d", h=heads)
                sq = headsq[:, 0:TILES * heads]
                dve.wait_ge(*ready)
                dve.tensor_tensor(scratch, m, m, ALU.mult).then_inc(S(), 1)
                dve.wait_ge(*S.last())
                dve.tensor_reduce(sq, scratch.rearrange("p t (h d) -> p (t h) d", h=heads), AX.X, ALU.add).then_inc(S(), 1)
                dve.wait_ge(*S.last())
                if TILES * heads < TILES * HG_HEADS:
                    dve.memset(headsq[:, TILES * heads:], 1.0)
                dve.tensor_scalar(sq, sq, 1.0 / P, EPS, ALU.mult, ALU.add).then_inc(S(tag, "head variance"), 1)
                dve.wait_ge(*at(tag, "head deviation"))
                dve.reciprocal(sq, sq).then_inc(S(), 1)
                dve.wait_ge(*S.last())
                if factor != 1.0:
                    dve.tensor_scalar(sq, sq, factor, None, ALU.mult).then_inc(S(), 1)
                    dve.wait_ge(*S.last())
                dve.tensor_tensor(m4, m4, sq.rearrange("p (t h) -> p t h", t=TILES).unsqueeze(3).broadcast_to([P, TILES, heads, P]),
                                  ALU.mult).then_inc(S(), 1)
                dve.wait_ge(*S.last())
                if tag == "gla":
                    g = gain_row(n, w)
                    o = dve.tensor_tensor(m, m, g.unsqueeze(1).broadcast_to([P, TILES, w]), ALU.mult)
                else:
                    g = gain_row(n, P)
                    o = dve.tensor_tensor(m4, m4, g.unsqueeze(1).unsqueeze(1).broadcast_to([P, TILES, heads, P]), ALU.mult)
                o.then_inc(S(tag, "head normed"), 1)
                S.also("gain used", n)
                if gate is not None:
                    dve.wait_ge(*S.last())
                    dve.wait_ge(*at(tag, "silu"))
                    dve.tensor_tensor(m, m, gate, ALU.mult).then_inc(S(), 1)

            def decayed_start(d):
                dve.memset(d.before, 1.0)
                for a in d.att:
                    z = dve.memset(a, 0.0)
                z.then_inc(S(), 1)
                dve.wait_ge(*S.last())

            def decayed(d):
                tag = d.tag

                def keep(level):
                    dve.wait_ge(*at(tag, "level", level))
                    mask = con[:, C_TREE + level * P:C_TREE + (level + 1) * P].bitcast(U32)
                    for b, a in enumerate(d.att):
                        o = dve.copy_predicated(a, mask.unsqueeze(1).broadcast_to([P, 4, P]),
                                                bank[3 * (level % 2) + b][:, :].rearrange("p (a b) -> p a b", b=P))
                    o.then_inc(S(tag, "kept", level), 1)

                dve.wait_ge(*at(tag + "_q", "taken", d.groups // 2 - 1))
                for level in range(1, LEVELS + 2):
                    if level > 2:
                        dve.wait_ge(*at(tag, "level", level - 2))
                    dq = d.dq[level % 2]
                    if level <= LEVELS:
                        dve.tensor_tensor(dq, d.q, d.after, ALU.mult).then_inc(S(tag, "queries", level), 1)
                    else:
                        dve.tensor_tensor(dq[:, :, P:SEQ], d.q[:, :, P:SEQ], d.after[:, :, P:SEQ], ALU.mult)\
                           .then_inc(S(tag, "queries", level), 1)
                    if level <= LEVELS:
                        n = 1 << (level - 1)
                        before, after = (z.rearrange("p g (b two n) -> p (g b) two n", two=2, n=n)
                                         for z in (d.before, d.after))
                        nb = d.groups * SEQ // (2 * n)
                        if level > 1:
                            dve.wait_ge(*at(tag, "keys", level))
                        dve.tensor_tensor(before[:, :, 0, :], before[:, :, 0, :],
                                          after[:, :, 1, n - 1:n].broadcast_to([P, nb, n]), ALU.mult)\
                           .then_inc(S(tag, "before", level + 1), 1)
                        dve.wait_ge(*S.last())
                        dve.tensor_tensor(after[:, :, 1, :], after[:, :, 1, :],
                                          after[:, :, 0, n - 1:n].broadcast_to([P, nb, n]), ALU.mult).then_inc(S(), 1)
                        dve.wait_ge(*S.last())
                    keep(level - 1)
                    dve.wait_ge(*S.last())

            def mlp_round(R, L, g, rounds, step, nt, n):
                def hidden(p):
                    for t in range(nt):
                        dve.wait_ge(L.gated, nt * (step + p) + t + 1)
                        dve.tensor_tensor(hid[:, p, t, :], gated[:, p, t, :], bank[2 * p + t][:, HID:2 * HID], ALU.mult)\
                           .then_inc(L.hidden, 1)

                def hidden_lo(p):
                    for t in range(nt):
                        dve.wait_ge(L.hid_hi, nt * (step + p) + t + 1)
                        dve.tensor_tensor(hid_lo[:, p, :, t * P:(t + 1) * P],
                                          bank[2 * p + t][:, 0:HID].rearrange("p (k s) -> p k s", k=2),
                                          f32(hid_hi[:, p, :, t * P:(t + 1) * P]), ALU.subtract).then_inc(L.hid_lo, 1)

                split_lo(R, g, rounds)
                split_lo(R, g + 1, rounds)
                split_lo(R, g + 2, rounds)
                hidden(0)
                if n == 2:
                    split_lo(R, g + 3, rounds)
                hidden_lo(0)
                if n == 2:
                    split_lo(R, g + 4, rounds)
                    hidden(1)
                    split_lo(R, g + 5, rounds)
                    hidden_lo(1)

            def add_mlp(label, units, gate=None):
                dve.wait_ge(ring.used, units)
                for t in range(TILES):
                    for n in range(2):
                        c = slice(n * 512, (n + 1) * 512)
                        y = bank[4 + 2 * t + n][:, :]
                        if gate is not None:
                            dve.tensor_tensor(mix[:, t, c], y, gate[:, c], ALU.mult).then_inc(S(), 1)
                            dve.wait_ge(*S.last())
                            y = mix[:, t, c]
                        o = dve.tensor_tensor(x[:, t, c], x[:, t, c], y, ALU.add)
                    o.then_inc(S(label, "added", t), 1)

            if have("memory"):
                S.stage("memory")
                norm("norm_kv_a", mix, proj, 0)
                g = gain_row(1)
                for t in range(TILES):
                    h = dve.scalar_tensor_tensor(out=proj[:, t, D:2 * D], in0=mix[:, t, :], scalar=rstd[:, t:t + 1], in1=g,
                                                 op0=ALU.mult, op1=ALU.mult)
                h.then_inc(S("norm_kv_b", "h"), 1)
                S.also("gain used", 1)
                turn_split("norm_kv_a")
                product("kv_a", False)
                norm("norm_a", x, mix, 2)
                turn_split("norm_kv_b")
                product("kv_b", False)
            if have("a_in"):
                S.stage("a_in")
                dve.wait_ge(loaded["lam"], 64)
                lam4 = lam_place()
                dve.tensor_tensor(lam4[:, 0:2, :], lam4[:, 0:2, :], lam4[:, 2:4, :], ALU.mult).then_inc(S(), 1)
                dve.wait_ge(*S.last())
                dve.tensor_reduce(neg_lam[:, 0:2], lam4[:, 0:2, :], AX.X, ALU.add).then_inc(S("lam sums"), 1)
                dve.wait_ge(loaded["lb"], 16)
                dve.tensor_tensor(lb[:, 1, :], lb[:, 0, :], lb[:, 0, :], ALU.subtract).then_inc(S("lb shifted"), 1)
                dve.wait_ge(*at("lam exp"))
                dve.tensor_tensor(neg_lam[:, 2:3], neg_lam[:, 1:2], neg_lam[:, 0:1], ALU.subtract).then_inc(S(), 1)
                dve.wait_ge(*S.last())
                dve.tensor_scalar(neg_lam[:, 2:3], neg_lam[:, 2:3], -LAM_INIT, None, ALU.add).then_inc(S(), 1)
                dve.wait_ge(*at("lb exp"))
                dve.reciprocal(lb[:, 2, :], lb[:, 1, :]).then_inc(S(), 1)
                dve.wait_ge(*S.last())
                dve.tensor_tensor(lb[:, 1, :], lb[:, 1, :], lb[:, 2, :], ALU.mult).then_inc(S(), 1)
                dve.wait_ge(*S.last())
                dve.tensor_tensor(lb[:, 2, :], lb[:, 1, :], lb[:, 1, :], ALU.subtract).then_inc(S(), 1)
                dve.wait_ge(*S.last())
                dve.tensor_scalar(lb[:, 3, :], lb[:, 2, :], -1.0, 1.0, ALU.mult, ALU.add).then_inc(S(), 1)
                turn_split("norm_a")
                product("a_in", False)
            if have("diff"):
                S.stage("diff")
                dve.wait_ge(loaded["con"], 16)
                pairs(diff, "distance")
                head_norm("diff", DA_HEADS, head_scratch, 3, S.last(), 1.0 - LAM_INIT)
            if have("a_mem"):
                S.stage("a_mem")
                pairs(a_mem)
            if have("a_out"):
                S.also("mix_a")
                S.stage("a_out")
                turn_split("mix_a")
                product("a_out", True)
            if have("dense"):
                S.stage("dense")
                norm("norm_dense", x, mix, 4)
                turn_split("norm_dense")
                mlp_round(ring, dense_loop, G["dense"], 0, 0, TILES, 1)
                repeat(dve, DENSE_STEPS // 2,
                       lambda i: mlp_round(ring, dense_loop, G["dense"] + 3, i, 2 * i + 1, TILES, 2))
                add_mlp("dense", G["b_in"])
            if have("b_in"):
                S.stage("b_in")
                norm("norm_b", x, mix, 5)
                turn_split("norm_b")
                product("b_in", False)
            if have("hgrn"):
                S.stage("hgrn")
                if have("ada"):
                    dve.wait_ge(ada_stored, 16)
                decayed_start(hgrn)
                dve.wait_ge(*at("hgrn_f", "taken", 2))
                low, high = (lb[:, n, :].unsqueeze(2).broadcast_to([P, HG_HEADS, SEQ]) for n in (2, 3))
                dve.tensor_tensor(hgrn.k, hgrn.k, high, ALU.mult).then_inc(S("hgrn", "k"), 1)
                dve.tensor_tensor(hgrn.after, hgrn.after, high, ALU.mult).then_inc(S(), 1)
                dve.wait_ge(*S.last())
                dve.tensor_tensor(hgrn.after, hgrn.after, low, ALU.add).then_inc(S(), 1)
                dve.wait_ge(*S.last())
                decayed(hgrn)
                head_norm("hgrn", HG_HEADS, part(work, 1024, TILES, HG_W), 6, at("hgrn", "out"),
                          gate=proj[:, :, 3 * HG_W:4 * HG_W])
            if have("b_mem"):
                S.stage("b_mem")
                pairs(b_mem)
            if have("b_out"):
                S.also("mix_b")
                S.stage("b_out")
                turn_split("mix_b")
                product("b_out", True)
            if have("route"):
                S.stage("route")
                norm("norm_moe", x, mix, 7)
                turn_split("norm_moe")
                dve.wait_ge(*at("route", "h_hi"))
                dve.tensor_tensor(flat(moe_h_lo[:, :, :]), flat(mix[:, :, :]), f32(flat(moe_h_hi[:, :, :])), ALU.subtract)\
                   .then_inc(S("route", "h_lo"), 1)
                dve.wait_ge(*at("route", "logits"))
                dve.tensor_copy(flat(logits[:, :, :]), bank[0][:, 0:TILES * EXPERTS]).then_inc(S(), 1)
                dve.wait_ge(*S.last())
                for t in range(TILES):
                    l = logits[:, t, :]
                    other = l.unsqueeze(1).broadcast_to([P, EXPERTS, EXPERTS])
                    own = l.unsqueeze(2).broadcast_to([P, EXPERTS, EXPERTS])
                    sq = [z[:, t, :].rearrange("p (e f) -> p e f", e=EXPERTS) for z in (pairs_gt, pairs_eq)]
                    dve.max(best[:, t, :], l)
                    dve.tensor_tensor(sq[0], other, own, ALU.is_gt)
                    o = dve.tensor_tensor(sq[1], other, own, ALU.is_equal)
                o.then_inc(S(), 1)
                dve.wait_ge(*S.last())
                dve.tensor_tensor(ratio[:, 0, :], best[:, :, 1], best[:, :, 0], ALU.subtract).then_inc(S("route", "gap"), 1)
                before = con[:, C_BEFORE:C_BEFORE + 64].unsqueeze(1).broadcast_to([P, TILES, 64])
                dve.tensor_tensor(pairs_eq[:, :, :], pairs_eq[:, :, :], before, ALU.mult).then_inc(S(), 1)
                dve.wait_ge(*S.last())
                dve.tensor_tensor(pairs_eq[:, :, :], pairs_eq[:, :, :], pairs_gt[:, :, :], ALU.add).then_inc(S(), 1)
                dve.wait_ge(*S.last())
                dve.tensor_reduce(flat(rank[:, :, :]), pairs_eq[:, :, :].rearrange("p t (e f) -> p (t e) f", e=EXPERTS),
                                  AX.X, ALU.add).then_inc(S(), 1)
                dve.wait_ge(*S.last())
                dve.tensor_scalar(chosen[:, :, :], rank[:, :, :], 1.5, None, ALU.is_lt).then_inc(S("route", "chosen"), 1)
                dve.tensor_scalar(share[:, :, :], rank[:, :, :], 0.0, None, ALU.is_equal)
                dve.tensor_scalar(share2[:, :, :], rank[:, :, :], 1.0, None, ALU.is_equal).then_inc(S(), 1)
                dve.wait_ge(*at("route", "exp"))
                dve.tensor_scalar(ratio[:, 2, :], ratio[:, 1, :], 1.0, None, ALU.add).then_inc(S(), 1)
                dve.wait_ge(*S.last())
                dve.reciprocal(ratio[:, 2, :], ratio[:, 2, :]).then_inc(S(), 1)
                dve.wait_ge(*S.last())
                dve.tensor_tensor(ratio[:, 3, :], ratio[:, 1, :], ratio[:, 2, :], ALU.mult).then_inc(S(), 1)
                dve.wait_ge(*S.last())
                for a, r in ((share, 2), (share2, 3)):
                    o = dve.tensor_tensor(a[:, :, :], a[:, :, :], ratio[:, r, :].unsqueeze(2).broadcast_to([P, TILES, EXPERTS]), ALU.mult)
                o.then_inc(S(), 1)
                dve.wait_ge(*S.last())
                dve.tensor_tensor(share[:, :, :], share[:, :, :], share2[:, :, :], ALU.add).then_inc(S(), 1)
                dve.wait_ge(*S.last())
                dve.tensor_scalar(share2[:, :, :], chosen[:, :, :], -1000.0, 1000.0, ALU.mult, ALU.add).then_inc(S(), 1)
                dve.wait_ge(*S.last())
                dve.wait_ge(*at("route", "order"))
                order = bank[1][:, 0:2 * EXPERTS].rearrange("p (t e) -> p t e", t=TILES)
                dve.tensor_tensor(place[:, 0], order, share2[:, :, :], ALU.add)
                dve.tensor_copy(counts[:, 0:EXPERTS], bank[1][:, 2 * EXPERTS:3 * EXPERTS]).then_inc(S(), 1)
                dve.wait_ge(*S.last())
                dve.tensor_scalar(place[:, 1], place[:, 0], -float(capacity), None, ALU.add).then_inc(S(), 1)
                dve.tensor_reduce(counts[:, EXPERTS:EXPERTS + 1], counts[:, 0:EXPERTS], AX.X, ALU.max).then_inc(S(), 1)
                dve.wait_ge(*S.last())
                if capacity < P:
                    dve.tensor_scalar(share2[:, :, :], place[:, 0], capacity - 0.5, 1000.0, ALU.is_gt, ALU.mult).then_inc(S(), 1)
                    dve.wait_ge(*S.last())
                    dve.tensor_tensor(place[:, 0], place[:, 0], share2[:, :, :], ALU.add).then_inc(S(), 1)
                    dve.wait_ge(*S.last())
                dve.tensor_scalar(flag[:, 0:1], counts[:, EXPERTS:EXPERTS + 1], capacity + 0.5, None, ALU.is_gt)\
                   .then_inc(S("overflow"), 1)
                dve.wait_ge(*S.last())
            if have("experts"):
                S.stage("experts")

                def experts(R, L, again):
                    def hidden(p, step):
                        dve.wait_ge(L.gated, step + 1)
                        dve.tensor_tensor(hid[:, p, 0, :], gated[:, p, 0, :], bank[2 * p][:, HID:2 * HID], ALU.mult)\
                           .then_inc(L.hidden, 1)

                    def hidden_lo(p, step):
                        dve.wait_ge(L.hid_hi, step + 1)
                        dve.tensor_tensor(hid_lo[:, p, :, 0:P], bank[2 * p][:, 0:HID].rearrange("p (k s) -> p k s", k=2),
                                          f32(hid_hi[:, p, :, 0:P]), ALU.subtract).then_inc(L.hid_lo, 1)

                    def pick_tokens(e):
                        for t in range(TILES):
                            o = dve.tensor_scalar(pick[:, t, :], con[:, C_IOTA:C_IOTA + P],
                                                  place[:, again, t, bass.ds(e, 1)], None, ALU.is_equal)
                        o.then_inc(L.picked, 1)

                    def slots(n, used=None):
                        dve.wait_ge(L.gathered, 2 * n)
                        if used is not None:
                            dve.wait_ge(R.used, used)
                        for k in range(2):
                            o = dve.tensor_copy(flat(slot_lo[:, 4 * k:4 * k + 4, :]), bank[1 + 2 * k][:, :])
                        o.then_inc(L.slots_lo, 1)

                    def add(e, j):
                        t, c = j // 2, slice(j % 2 * 512, (j % 2 + 1) * 512)
                        if j == 0:
                            dve.wait_ge(L.scattered, e + 1)
                            dve.wait_ge(L.added, e + 1)
                        o = dve.scalar_tensor_tensor(out=x[:, t, c], in0=bank[SCATTER[j]][:, :],
                                                     scalar=share[:, t, bass.ds(e, 1)], in1=x[:, t, c],
                                                     op0=ALU.mult, op1=ALU.add)
                        if j == 3:
                            o.then_inc(L.added, 1)

                    def place_pickT(n):
                        dve.wait_ge(L.staged, n)
                        dve.tensor_copy(flat(pickT[:, :, :]), staged[:, :]).then_inc(L.pickT, 1)

                    def one_round(g, rounds, step, e=None):
                        split_lo(R, g, rounds)
                        hidden(0, step)
                        if e is not None:
                            add(e, 0)
                        split_lo(R, g + 1, rounds)
                        hidden_lo(0, step)
                        split_lo(R, g + 2, rounds)
                        if e is not None:
                            add(e, 1)
                        split_lo(R, g + 3, rounds)
                        hidden(1, step + 1)
                        if e is not None:
                            add(e, 2)
                        split_lo(R, g + 4, rounds)
                        hidden_lo(1, step + 1)
                        split_lo(R, g + 5, rounds)
                        if e is not None:
                            add(e, 3)
                            place_pickT(e + 2)

                    def first():
                        dve.memset(sumsq[:, :], 0.0).then_inc(L.added, 1)
                        pick_tokens(0)
                        split_lo(R, G["experts"], 0)
                        slots(1)
                        place_pickT(1)
                        split_lo(R, G["experts"] + 1, 0)
                        one_round(FIRST_ROUND, 0, 0)

                    def tail(e, last):
                        r, step = PER_EXPERT * e, EXPERT_STEPS * e + EXPERT_STEPS - 2
                        if not last:
                            dve.wait_ge(L.pick_turned, e + 1)
                            pick_tokens(e + 1)
                        split_lo(R, TAIL, r)
                        hidden(0, step)
                        split_lo(R, TAIL + 1, r)
                        hidden_lo(0, step)
                        if not last:
                            slots(e + 2, TAIL + 2 - R.first + R.credit + RING * r)
                        split_lo(R, TAIL + 2, r)
                        hidden(1, step + 1)
                        split_lo(R, TAIL + 3, r)
                        if last:
                            hidden_lo(1, step + 1)
                        else:
                            split_lo(R, TAIL + 4, r)
                            hidden_lo(1, step + 1)
                            split_lo(R, TAIL + 5, r)
                        dve.wait_ge(L.y_hi, e + 1)
                        for k in range(2):
                            c = slice(k * 512, (k + 1) * 512)
                            o = dve.tensor_tensor(y_lo[:, c], bank[4 + k][:, :], f32(y_hi[:, c]), ALU.subtract)
                        o.then_inc(L.y_lo, 1)
                        if last:
                            for j in range(4):
                                add(e, j)

                    expert_order(dve, first,
                                 lambda e, i: one_round(NEXT_ROUND, PER_EXPERT * e + i, EXPERT_STEPS * e + 2 * i + 2),
                                 tail,
                                 lambda e: one_round(NEXT_FIRST, PER_EXPERT * e, EXPERT_STEPS * e + EXPERT_STEPS, e))

                experts(ring, expert_loop, 0)
                more = dve.value_load(flag[0:1, 0:1], min_val=0, max_val=1)
                with dve.If(more > 0):
                    dve.sem_inc(more_ring.lo, RING)
                    dve.wait_ge(expert_loop.added, EXPERTS + 1)
                    experts(more_ring, more_loop, 1)
                    dve.wait_ge(more_loop.added, EXPERTS + 1)
                dve.wait_ge(expert_loop.added, EXPERTS + 1)
                dve.memset(headsq[:, :], 1.0).then_inc(S("experts done"), 1)
            if have("ada"):
                S.stage("ada")
                norm("norm_final", x, x, 8)
                dve.wait_ge(*at("ada", "out", 3))
            if have("in_2"):
                S.stage("in_2")
                norm("norm_2", x, mix, 9, 0)
                dve.wait_ge(*at("ada", "out", 11))
                turn_split("norm_2")
                product("in_2", False)
                split_lo(ring, G["in_2"] + 12, 0, KC * GLA_RANK)
            if have("gla"):
                S.stage("gla")
                decayed_start(gla)
                dve.wait_ge(*at("gla", "f"))
                decayed(gla)
                head_norm("gla", GLA_HEADS, part(work2, 2048, TILES, GLA_W), 10, at("gla", "out"),
                          gate=proj2[:, :, 1024:1536])
            if have("moba"):
                S.stage("moba")
                pairs(moba, "rows")
            if have("out_2"):
                S.also("mix_2")
                S.stage("out_2")
                turn_split("mix_2")
                product("out_2", True, ada[:, 2, :])
            if have("ff_2"):
                S.stage("ff_2")
                norm("norm_ff", x, mix, 11, 3)
                turn_split("norm_ff")

                def hidden(p, step, unit, rounds):
                    dve.wait_ge(ring.used, unit + 1 + RING * rounds)
                    h = flat(hid2[:, p])
                    dve.tensor_scalar(h, bank[p][:, :], 0.0, None, ALU.max).then_inc(ff_loop.gated, 1)
                    dve.wait_ge(ff_loop.gated, step + 1)
                    dve.tensor_tensor(h, h, bank[p][:, :], ALU.mult).then_inc(ff_loop.hidden, 1)

                def hidden_lo(p, step):
                    hi, lo = (flat(z[:, p]).rearrange("p (k t s) -> p t k s", k=2, t=TILES) for z in (hid2_hi, hid2_lo))
                    dve.wait_ge(ff_loop.hid_hi, step + 1)
                    dve.tensor_tensor(lo, bank[p][:, :].rearrange("p (t k s) -> p t k s", k=2, t=TILES), f32(hi),
                                      ALU.subtract).then_inc(ff_loop.hid_lo, 1)

                def ff_round(i):
                    g = G["ff_2"]
                    split_lo(ring, g, i)
                    split_lo(ring, g + 1, i)
                    hidden(0, 3 * i, g, i)
                    split_lo(ring, g + 2, i)
                    hidden(1, 3 * i + 1, g + 1, i)
                    hidden_lo(0, 3 * i)
                    split_lo(ring, g + 3, i)
                    hidden(2, 3 * i + 2, g + 2, i)
                    hidden_lo(1, 3 * i + 1)
                    split_lo(ring, g + 4, i)
                    hidden_lo(2, 3 * i + 2)
                    split_lo(ring, g + 5, i)
                repeat(dve, FF2_STEPS // 3, ff_round)
                g = G["ff_2"] + 30
                split_lo(ring, g, 0)
                split_lo(ring, g + 1, 0)
                hidden(0, 15, g, 0)
                hidden_lo(0, 15)
                add_mlp("ff_2", g + 2, ada[:, 5, :])
            if have("final"):
                S.stage("final")
                norm("norm_out", x, x, 12)
                S.also("result", TILES - 1)
            else:
                dve.memset(headsq[:, :], 1.0).then_inc(S("result", 0), 1)
                S.also("result", 1)

        @block.tensor
        def _(pe):
            S = Signals("tensor", semaphore, numbers)
            S.stage("prep")

            def consume(R, g, rounds, products, between=None):
                u = g - R.first
                s = g % SPLIT
                pe.wait_ge(R.hi, u + 1 + R.credit + RING * rounds)
                for out_, terms, start, stop in products:
                    for n, (hi, lo, c, w) in enumerate(terms):
                        pe.matmul(out_, hi, w_hi[:, s, c:c + w], start=(start and n == 0), stop=False, skip_group_check=True)
                        mm = pe.matmul(out_, lo, w_hi[:, s, c:c + w], start=False, stop=False, skip_group_check=True)
                mm.then_inc(R.hi_used, 1)
                if between is not None:
                    between()
                pe.wait_ge(R.lo, u + 1 + R.credit + RING * rounds)
                for out_, terms, start, stop in products:
                    for n, (hi, lo, c, w) in enumerate(terms):
                        mm = pe.matmul(out_, hi, w_lo[:, s, c:c + w], start=False, stop=(stop and n == len(terms) - 1),
                                       skip_group_check=True)
                mm.then_inc(R.used, 1)

            def columns_terms(h, t, n):
                return [(hT_hi[:, 4 * h + k, t * P:(t + 1) * P], hT_lo[:, 4 * h + k, t * P:(t + 1) * P], k * n, n)
                        for k in range(4)]

            def turn(tag, blocks, ready, rows=P):
                pe.wait_ge(*ready)
                for n in range(0, len(blocks), 4):
                    j = n // 4
                    if j >= 2:
                        pe.wait_ge(*at(tag, "taken", j - 2))
                    for c, b in enumerate(blocks[n:n + 4]):
                        mm = pe.transpose(bank[6 + j % 2][:, c * P:(c + 1) * P], b, ident)
                    mm.then_inc(S(tag, "turned", j), 1)

            def turn_split(tag, src, ready):
                turn(tag, [src[:, t, k * P:(k + 1) * P] for k, t in NORM_BLOCKS], ready)

            def turned(tag):
                for j in (2, 3):
                    pe.wait_ge(*at(tag, "taken", j))

            def product(name, tag):
                for j, (c, n) in enumerate(COLS[name]):
                    b = B[name] + j
                    if b >= 3:
                        pe.wait_ge(block_out, b - 2)
                    for h in range(2):
                        if j == 0:
                            pe.wait_ge(*at(tag, "taken", 2 * h + 1))
                        consume(ring, G[name] + 2 * j + h, 0,
                                [(bank[2 * (b % 3) + t][:, 0:n], columns_terms(h, t, n), h == 0, h == 1) for t in range(TILES)])

            def pairs(a, ready):
                turn(a.tag + "_q", a.q_cols, ready)
                last = (len(a.q_cols) - 1) // 4
                for j in range(max(0, last - 1), last + 1):
                    pe.wait_ge(*at(a.tag + "_q", "taken", j))
                turn(a.tag + "_k", a.k_cols, ready)
                pe.wait_ge(*at(a.tag + "_k", "taken", last))

                def scores(i):
                    k = i % 2
                    if i >= 2:
                        pe.wait_ge(*at(a.tag, "biased", i - 2))
                    for t in range(TILES):
                        for m in range(2):
                            r = slice(64 * m, 64 * m + 64)
                            mm = pe.matmul(bank[2 * k + m][:, t * SEQ:(t + 1) * SEQ], a.qT[r, i, t * P:(t + 1) * P],
                                           a.kT[r, i, :], start=True, stop=True)
                    mm.then_inc(S(a.tag, "scores", i), 1)

                def values(i):
                    k = i % 2
                    pe.wait_ge(*at(a.tag, "probsT", i))
                    if i >= 2:
                        pe.wait_ge(*at(a.tag, "out", i - 2))
                    for m in range(2):
                        for t in range(TILES):
                            j = 2 * m + t
                            for s in range(TILES):
                                mm = pe.matmul(bank[6 + k][:, j * a.dv:(j + 1) * a.dv],
                                               a.probsT[k][:, m, s, t * P:(t + 1) * P], a.v(i, m, s),
                                               start=(s == 0), stop=(s == TILES - 1))
                    mm.then_inc(S(a.tag, "values", i), 1)

                scores(0)
                for i in range(a.n):
                    if i + 1 < a.n:
                        scores(i + 1)
                    pe.wait_ge(*at(a.tag, "exp", i))
                    if i > 0:
                        pe.wait_ge(*at(a.tag, "probsT", i - 1))
                    for m in range(2):
                        for s in range(TILES):
                            for t in range(TILES):
                                mm = pe.transpose(bank[4 + m][:, s * SEQ + t * P:s * SEQ + (t + 1) * P],
                                                  a.probs[i % 2][:, m, t, s * P:(s + 1) * P], ident)
                    mm.then_inc(S(a.tag, "turned", i), 1)
                    if i > 0:
                        values(i - 1)
                values(a.n - 1)

            def decayed(d, ready):
                tag = d.tag
                for level in range(LEVELS + 2):
                    dk = d.dk[level % 2] if level > 1 else d.k
                    dq = d.dq[level % 2] if level > 0 else d.q
                    pe.wait_ge(*(at(tag, "queries", level) if level > 0 else ready))
                    if level > 1:
                        pe.wait_ge(*at(tag, "keys", level))
                    if level >= 2:
                        pe.wait_ge(*at(tag, "kept", level - 2))
                    if level <= LEVELS:
                        for n, (h, t) in enumerate(d.outs):
                            r, c = d.rows(h), slice(t * P, (t + 1) * P)
                            mm = pe.matmul(bank[3 * (level % 2) + n // 4][:, n % 4 * P:(n % 4 + 1) * P],
                                           dk[r, h // d.per, c], dq[r, h // d.per, c], start=True, stop=True)
                    else:
                        for b, heads in enumerate(cross_banks(d)):
                            for n, h in enumerate(heads):
                                r = d.rows(h)
                                mm = pe.matmul(bank[b][:, n * P:(n + 1) * P], dk[r, h // d.per, 0:P],
                                               dq[r, h // d.per, P:SEQ], start=True, stop=True)
                    mm.then_inc(S(tag, "level", level), 1)
                pe.wait_ge(*at(tag, "cross"))
                pe.wait_ge(*at(tag, "kept", LEVELS))
                where = {h: n for n, h in enumerate(h for heads in cross_banks(d) for h in heads)}
                for b, (t, h0, n) in enumerate(out_pieces(d)):
                    for j in range(n):
                        h = h0 + j
                        o = bank[b][:, j * P:(j + 1) * P]
                        i = d.outs.index((h, t))
                        mm = pe.matmul(o, d.att[i // 4][:, i % 4, :], d.v(h, t), start=True, stop=(t == 0))
                        if t > 0:
                            mm = pe.matmul(o, d.cross[:, where[h], :], d.v(h, 0), start=False, stop=True)
                mm.then_inc(S(tag, "products"), 1)

            def seed(banks):
                for b in banks:
                    pe.matmul(bank[b][:, :], zero[:, :], con[:, 0:SEQ].bitcast(BF16), start=True, stop=False,
                              skip_group_check=True)

            def mlp_round(R, L, g, rounds, step, nt, n, xs, tag=None):
                def up(p, h):
                    consume(R, g + 2 * p + h, rounds,
                            [(bank[2 * p + t][:, :], [(xs(0, 4 * h + k, t), xs(1, 4 * h + k, t), k * 512, 512) for k in range(4)],
                              h == 0, h == 1) for t in range(nt)])

                def turn_hidden(p):
                    for t in range(nt):
                        pe.wait_ge(L.hidden, nt * (step + p) + t + 1)
                        for k in range(2):
                            mm = pe.transpose(bank[2 * p + t][:, k * P:(k + 1) * P], hid[:, p, t, k * P:(k + 1) * P], ident)
                        mm.then_inc(L.turned, 1)

                def down(p, between=None):
                    pe.wait_ge(L.hid_lo, nt * (step + p) + nt)
                    consume(R, g + 2 * n + p, rounds,
                            [(bank[4 + 2 * t + c][:, :], [(hid_hi[:, p, k, t * P:(t + 1) * P], hid_lo[:, p, k, t * P:(t + 1) * P],
                                                           k * D + c * 512, 512) for k in range(2)], False, False)
                             for t in range(nt) for c in range(2)], between)

                if tag is not None:
                    pe.wait_ge(*at(tag, "taken", 1))
                up(0, 0)
                if tag is not None:
                    pe.wait_ge(*at(tag, "taken", 2))
                    pe.wait_ge(*at(tag, "taken", 3))
                    seed(range(4, 8))
                up(0, 1)
                if n == 2:
                    up(1, 0)
                turn_hidden(0)
                if n == 2:
                    up(1, 1)
                    down(0, lambda: turn_hidden(1))
                    down(1)
                else:
                    down(0)

            def model_xs(half, k, t):
                return (hT_hi, hT_lo)[half][:, k, t * P:(t + 1) * P]

            if have("memory"):
                S.stage("memory")
                pe.wait_ge(loaded["ident"], 16)
                turn_split("norm_kv_a", proj, at("norm_kv_a", "h"))
                product("kv_a", "norm_kv_a")
                turn_split("norm_kv_b", proj[:, :, D:2 * D], at("norm_kv_b", "h"))
                product("kv_b", "norm_kv_b")
            if have("a_in"):
                S.stage("a_in")
                relx, onehot, _ = rel_places()
                pe.wait_ge(loaded["rel"], 32)
                pe.wait_ge(*at("relx"))
                pe.wait_ge(block_out, 1)
                pe.matmul(bank[0][0:8, :], relx, onehot, start=True, stop=True).then_inc(S("rel product"), 1)
                turn_split("norm_a", mix, at("norm_a", "h"))
                pe.wait_ge(*at("rel rows"))
                product("a_in", "norm_a")
            if have("diff"):
                S.stage("diff")
                pairs(diff, (block_out, B["a_in"] + 5))
            if have("a_mem"):
                S.stage("a_mem")
                pairs(a_mem, at("diff", "out", DA_HEADS - 1))
            if have("a_out"):
                S.stage("a_out")
                turn_split("mix_a", mix, at("mix_a"))
                product("a_out", "mix_a")
            if have("dense"):
                S.stage("dense")
                turn_split("norm_dense", mix, at("norm_dense", "h"))
                pe.wait_ge(*at("zero"))
                mlp_round(ring, dense_loop, G["dense"], 0, 0, TILES, 1, model_xs, "norm_dense")
                repeat(pe, DENSE_STEPS // 2,
                       lambda i: mlp_round(ring, dense_loop, G["dense"] + 3, i, 2 * i + 1, TILES, 2, model_xs))
            if have("b_in"):
                S.stage("b_in")
                turn_split("norm_b", mix, at("norm_b", "h"))
                product("b_in", "norm_b")
            if have("hgrn"):
                S.stage("hgrn")
                all_in = (block_out, B["b_in"] + 7)
                turn("hgrn_q", [proj[:, t, h * P:(h + 1) * P] for h in range(HG_HEADS) for t in range(TILES)], all_in)
                for j in (1, 2):
                    pe.wait_ge(*at("hgrn_q", "taken", j))
                turn("hgrn_f", [proj[:, t, HG_W + h * P:HG_W + (h + 1) * P] for h in range(HG_HEADS) for t in range(TILES)], all_in)
                for j in (1, 2):
                    pe.wait_ge(*at("hgrn_f", "taken", j))
                decayed(hgrn, at("hgrn", "k"))
            if have("b_mem"):
                S.stage("b_mem")
                pairs(b_mem, at("hgrn", "out"))
            if have("b_out"):
                S.stage("b_out")
                turn_split("mix_b", mix, at("mix_b"))
                product("b_out", "mix_b")
            if have("route"):
                S.stage("route")
                turn_split("norm_moe", mix, at("norm_moe", "h"))
                turned("norm_moe")
                pe.wait_ge(loaded["router"], 16)
                for t in range(TILES):
                    for k in range(KC):
                        for half in range(2):
                            mm = pe.matmul(bank[0][:, t * EXPERTS:(t + 1) * EXPERTS], model_xs(half, k, t).bitcast(F32),
                                           w_router[:, k, :], start=(k == 0 and half == 0), stop=(k == KC - 1 and half == 1))
                mm.then_inc(S("route", "logits"), 1)
                pe.wait_ge(*at("route", "chosen"))
                pe.wait_ge(loaded["con"], 16)
                pe.wait_ge(*at("zero"))
                later = con[:, C_LATER:C_LATER + P]
                for c, terms in enumerate((((later, 0),), ((ones[:, :], 0), (later, 1)), ((ones[:, :], 0), (ones[:, :], 1)))):
                    for n, (w, t) in enumerate(terms):
                        mm = pe.matmul(bank[1][:, c * EXPERTS:(c + 1) * EXPERTS], w, chosen[:, t, :],
                                       start=(n == 0), stop=(n == len(terms) - 1))
                mm.then_inc(S("route", "order"), 1)
            if have("experts"):
                S.stage("experts")
                pe.wait_ge(*at("route", "h_lo"))

                def experts(R, L):
                    def up(p, h, g, rounds):
                        consume(R, g, rounds, [(bank[2 * p][:, :], [(slot_hi[:, 4 * h + k, :], slot_lo[:, 4 * h + k, :], k * 512, 512)
                                                                    for k in range(4)], h == 0, h == 1)])

                    def turn_hidden(p, step):
                        pe.wait_ge(L.hidden, step + 1)
                        for k in range(2):
                            mm = pe.transpose(bank[2 * p][:, k * P:(k + 1) * P], hid[:, p, 0, k * P:(k + 1) * P], ident)
                        mm.then_inc(L.turned, 1)

                    def down(p, step, g, rounds):
                        pe.wait_ge(L.hid_lo, step + 1)
                        consume(R, g, rounds,
                                [(bank[4 + c][:, :], [(hid_hi[:, p, k, 0:P], hid_lo[:, p, k, 0:P], k * D + c * 512, 512)
                                                      for k in range(2)], False, False) for c in range(2)])

                    def gather(n):
                        pe.wait_ge(L.picked, n)
                        for half, banks in ((moe_h_hi, (6, 7)), (moe_h_lo, (1, 3))):
                            for k in range(KC):
                                for t in range(TILES):
                                    mm = pe.matmul(bank[banks[k // 4]][:, k % 4 * P:(k % 4 + 1) * P],
                                                   half[:, t, k * P:(k + 1) * P], pick[:, t, :], start=(t == 0), stop=(t == 1))
                            mm.then_inc(L.gathered, 1)

                    def turn_pick(n):
                        pe.wait_ge(L.slots_lo, n)
                        for t in range(TILES):
                            mm = pe.transpose(bank[1][:, t * P:(t + 1) * P], pick[:, t, :].bitcast(F32), ident)
                        mm.then_inc(L.pick_turned, 1)

                    def scatter(e):
                        pe.wait_ge(L.y_lo, e + 1)
                        pe.wait_ge(L.pickT, e + 1)
                        for t in range(TILES):
                            for k in range(2):
                                o = bank[SCATTER[2 * t + k]][:, :]
                                pe.matmul(o, pickT[:, t, :], y_hi[:, k * 512:(k + 1) * 512], start=True, stop=False)
                                mm = pe.matmul(o, pickT[:, t, :], y_lo[:, k * 512:(k + 1) * 512], start=False, stop=True)
                        mm.then_inc(L.scattered, 1)

                    def one_round(g, rounds, step):
                        up(1, 0, g, rounds)
                        turn_hidden(0, step)
                        up(1, 1, g + 1, rounds)
                        down(0, step, g + 2, rounds)
                        up(0, 0, g + 3, rounds)
                        turn_hidden(1, step + 1)
                        up(0, 1, g + 4, rounds)
                        down(1, step + 1, g + 5, rounds)

                    def first():
                        gather(1)
                        turn_pick(1)
                        pe.wait_ge(L.slots_hi, 1)
                        seed((4, 5))
                        up(0, 0, G["experts"], 0)
                        up(0, 1, G["experts"] + 1, 0)
                        one_round(FIRST_ROUND, 0, 0)

                    def tail(e, last):
                        r, step = PER_EXPERT * e, EXPERT_STEPS * e + EXPERT_STEPS - 2
                        if not last:
                            pe.wait_ge(L.added, e + 1)
                            gather(e + 2)
                        up(1, 0, TAIL, r)
                        turn_hidden(0, step)
                        up(1, 1, TAIL + 1, r)
                        down(0, step, TAIL + 2, r)
                        turn_hidden(1, step + 1)
                        if last:
                            down(1, step + 1, TAIL + 3, r)
                            scatter(e)
                            return
                        pe.wait_ge(L.slots_hi, e + 2)
                        pe.wait_ge(L.slots_lo, e + 2)
                        up(0, 0, TAIL + 3, r)
                        turn_pick(e + 2)
                        down(1, step + 1, TAIL + 4, r)
                        up(0, 1, TAIL + 5, r)
                        pe.wait_ge(L.staged, e + 2)
                        scatter(e)
                        seed((4, 5))

                    expert_order(pe, first,
                                 lambda e, i: one_round(NEXT_ROUND, PER_EXPERT * e + i, EXPERT_STEPS * e + 2 * i + 2),
                                 tail,
                                 lambda e: one_round(NEXT_FIRST, PER_EXPERT * e, EXPERT_STEPS * e + EXPERT_STEPS))

                experts(ring, expert_loop)
                pe.wait_ge(*at("overflow"))
                more = pe.value_load(flag[0:1, 0:1], min_val=0, max_val=1)
                with pe.If(more > 0):
                    pe.sem_inc(more_ring.hi_used, RING)
                    pe.sem_inc(more_ring.used, RING)
                    experts(more_ring, more_loop)
            if have("ada"):
                S.stage("ada")
                pe.wait_ge(*at("experts done"))
                for j in range(2 * N_ADA):
                    pe.wait_ge(ada_back[j // 4], 16)
                    if j >= 6:
                        pe.wait_ge(*at("ada", "out", j - 6))
                    pe.matmul(bank[j % 6][:, :], ones[:, :], ada[:, j // 2, j % 2 * 512:(j % 2 + 1) * 512], start=True, stop=True)\
                      .then_inc(S("ada", "summed", j), 1)
            if have("in_2"):
                S.stage("in_2")
                turn_split("norm_2", mix, at("norm_2", "h"))
                pe.wait_ge(*at("ada", "out", 11))
                product("in_2", "norm_2")
                b = B["in_2"] + 6
                pe.wait_ge(block_out, b - 2)
                consume(ring, G["in_2"] + 12, 0,
                        [(bank[2 * (b % 3) + t][:, 0:GLA_RANK],
                          [(model_xs(0, k, t), model_xs(1, k, t), k * GLA_RANK, GLA_RANK) for k in range(KC)], True, True)
                         for t in range(TILES)])
            if have("gla"):
                S.stage("gla")
                all_in = (block_out, B["in_2"] + 7)
                turn("gla_q", [proj2[:, t, g * P:(g + 1) * P] for g in range(2) for t in range(TILES)], all_in)
                turn("gla_k", [proj2[:, t, 256 + g * P:256 + (g + 1) * P] for g in range(2) for t in range(TILES)],
                     at("gla_q", "taken", 0))
                pe.wait_ge(*at("gla_k", "taken", 0))
                for t in range(TILES):
                    mm = pe.transpose(bank[6][0:GLA_RANK, t * P:(t + 1) * P], proj2[:, t, 1536:1552], ident)
                mm.then_inc(S("gla", "rank turned"), 1)
                pe.wait_ge(*at("gla", "rankT"))
                pe.wait_ge(loaded["wgate"], 16)
                for grp in range(2):
                    mm = pe.matmul(bank[7][:, grp * SEQ:(grp + 1) * SEQ], w_gate[:, grp * P:(grp + 1) * P], gla_rankT(),
                                   start=True, stop=True)
                mm.then_inc(S("gla", "gate"), 1)
                decayed(gla, at("gla_k", "taken", 0))
            if have("moba"):
                S.stage("moba")
                pairs(moba, at("gla", "out"))
            if have("out_2"):
                S.stage("out_2")
                turn_split("mix_2", mix, at("mix_2"))
                product("out_2", "mix_2")
            if have("ff_2"):
                S.stage("ff_2")
                turn_split("norm_ff", mix, at("norm_ff", "h"))
                turned("norm_ff")
                seed(range(4, 8))

                def up(p, g, rounds):
                    consume(ring, g, rounds,
                            [(bank[p][:, t * HID:(t + 1) * HID],
                              [(model_xs(0, k, t), model_xs(1, k, t), k * HID, HID) for k in range(KC)], t == 0, t == 1)
                             for t in range(TILES)])

                def turn_hidden(p, step):
                    pe.wait_ge(ff_loop.hidden, step + 1)
                    for t in range(TILES):
                        for k in range(2):
                            mm = pe.transpose(bank[p][:, t * HID + k * P:t * HID + (k + 1) * P], hid2[:, p, t, k * P:(k + 1) * P], ident)
                    mm.then_inc(ff_loop.turned, 1)

                def down(p, step, g, rounds):
                    pe.wait_ge(ff_loop.hid_lo, step + 1)
                    consume(ring, g, rounds,
                            [(bank[4 + 2 * t + c][:, :], [(hid2_hi[:, p, k, t * P:(t + 1) * P], hid2_lo[:, p, k, t * P:(t + 1) * P],
                                                           k * D + c * 512, 512) for k in range(2)], False, False)
                             for t in range(TILES) for c in range(2)])

                def ff_round(i):
                    g = G["ff_2"]
                    up(0, g, i)
                    up(1, g + 1, i)
                    turn_hidden(0, 3 * i)
                    up(2, g + 2, i)
                    turn_hidden(1, 3 * i + 1)
                    down(0, 3 * i, g + 3, i)
                    turn_hidden(2, 3 * i + 2)
                    down(1, 3 * i + 1, g + 4, i)
                    down(2, 3 * i + 2, g + 5, i)
                repeat(pe, FF2_STEPS // 3, ff_round)
                up(0, G["ff_2"] + 30, 0)
                turn_hidden(0, 15)
                down(0, 15, G["ff_2"] + 31, 0)


_INS = ["x", "mem", "a_norm_mix", "a_w_in", "a_lam_q1", "a_lam_k1", "a_lam_q2", "a_lam_k2", "a_subln", "a_mem_norm",
        "a_w_mem_kv", "a_w_out", "b_norm_mix", "b_w_in", "b_lb_logits", "b_out_norm", "b_mem_norm", "b_w_mem_kv",
        "b_w_out", "dense_norm", "dense_w_gate_up", "dense_w_down", "moe_norm", "moe_router", "moe_w_gate_up",
        "moe_w_down", "final_norm", "c_2", "w_ada_2", "b_ada_2", "g_mix_2", "w_in_2", "w_gla_gate_2", "b_gla_gate_2",
        "g_gla_out_2", "rel_bias_2", "w_out_2", "g_mlp_2", "w_ff1_2", "w_ff2_2", "g_final_2"]


def build(nc, shapes, known=None, stages=STAGES, capacity=CAPACITY):
    A = {n: nc.dram_tensor(f"in_{n}", s, F32, kind="ExternalInput").ap() for n, s in shapes.items()}
    consts = nc.dram_tensor("in_consts", (P, C_ALL), F32, kind="ExternalInput").ap()
    buckets = nc.dram_tensor("in_buckets", (BUCKETS + 1, 2 * SEQ), F32, kind="ExternalInput").ap()
    out = nc.dram_tensor("out", (1, SEQ, D), F32, kind="ExternalOutput").ap()
    numbers = {}
    program(nc, A, consts, buckets, out, {}, numbers, known, stages, capacity)
    return numbers


def kernel(**inputs):
    import concourse.bacc as bacc
    from concourse.bass_utils import run_bass_kernel_spmd

    arrays = {f"in_{n}": np.ascontiguousarray(inputs[n]) for n in _INS}
    shapes = {n: arrays[f"in_{n}"].shape for n in _INS}
    arrays["in_consts"], arrays["in_buckets"] = constants()
    known = build(bacc.Bacc("TRN2", target_bir_lowering=False, num_devices=1), shapes)
    nc = bacc.Bacc("TRN2", target_bir_lowering=False, num_devices=1)
    build(nc, shapes, known)
    r = run_bass_kernel_spmd(nc, [arrays], core_ids=[0])
    return r.results[0]["out"]
```
